# Optimizing a Trainium2 kernel written in Bass

```python
import jax, jax.numpy as jnp
from jax import lax
import numpy as np

D_MODEL = 1024
BATCH = 1
SEQ = 256
DEPTH = 2

CHUNK = 64
Q_BLOCK = 128
HEAD_DIM = 64
ROPE_THETA = 10000.0
EPS = 1e-6
SB_HEADS = 4
SB_W = SB_HEADS * HEAD_DIM
DSA_HEADS = 4
DSA_W = DSA_HEADS * HEAD_DIM
IDX_HEADS = 4
IDX_DIM = 64
TOPK_MAX = 256
GLA_HEADS = 4
GLA_DK = 32
GLA_DV = 64
GLA_KW = GLA_HEADS * GLA_DK
GLA_VW = GLA_HEADS * GLA_DV
GLA_RANK = 16
GLA_TAU = 16.0
N_BRANCH = 3
N_MEM = 256
X_HEADS = 4
X_DIM = D_MODEL // X_HEADS
D_FF = -(-8 * D_MODEL // (3 * 256)) * 256
SPLIT_SIZES = (SB_W, SB_W, SB_W,
               DSA_W, HEAD_DIM, HEAD_DIM, IDX_HEADS * IDX_DIM, IDX_DIM, IDX_HEADS,
               GLA_KW, GLA_KW, GLA_VW, GLA_RANK, GLA_VW,
               N_BRANCH * D_MODEL)
IN_WIDTH = (3 * SB_W + DSA_W + 2 * HEAD_DIM + IDX_HEADS * IDX_DIM + IDX_DIM + IDX_HEADS
            + 2 * GLA_KW + 2 * GLA_VW + GLA_RANK + N_BRANCH * D_MODEL)

kernel_name = 'hybrid_sb_dsa_gla_streaming_encoder'

F32 = jnp.float32

def rmsnorm(x, g):
    xf = x.astype(F32)
    y = xf * lax.rsqrt(jnp.mean(xf * xf, axis=-1, keepdims=True) + EPS)
    return (y * g.astype(F32)).astype(x.dtype)

def rope(t, pos):
    d = t.shape[-1]
    half = d // 2
    inv = 1.0 / (ROPE_THETA ** (jnp.arange(half, dtype=F32) * (2.0 / d)))
    ang = pos[:, None] * inv[None, :]
    cos = jnp.cos(ang)[None, :, None, :]
    sin = jnp.sin(ang)[None, :, None, :]
    tf = t.astype(F32)
    t1, t2 = tf[..., :half], tf[..., half:]
    return jnp.concatenate([t1 * cos - t2 * sin, t2 * cos + t1 * sin], axis=-1).astype(t.dtype)

def split_columns(z, sizes):
    out, start = [], 0
    for n in sizes:
        out.append(z[..., start:start + n])
        start += n
    return out

def to_blocks(t, nb):
    return jnp.moveaxis(t.reshape((t.shape[0], nb, Q_BLOCK) + t.shape[2:]), 1, 0)

def from_blocks(t):
    t = jnp.moveaxis(t, 0, 1)
    return t.reshape((t.shape[0], t.shape[1] * t.shape[2]) + t.shape[3:])

def stick_breaking_attention(q, k, v):
    B, S, H, dh = q.shape
    nb = S // Q_BLOCK
    scale = dh ** -0.5
    qi = np.repeat(np.arange(nb), np.arange(1, nb + 1))
    start = qi * (qi + 1) // 2
    ki = qi - (np.arange(qi.shape[0]) - start)
    last = np.arange(nb) * (np.arange(nb) + 1) // 2 + np.arange(nb)
    qbl = to_blocks(q.astype(F32) * scale, nb)
    kbl = to_blocks(k.astype(F32), nb)
    vbl = to_blocks(v.astype(F32), nb)
    strict_lower = jnp.tril(jnp.ones((Q_BLOCK, Q_BLOCK), F32), -1)

    def step(carry, idx):
        acc, run = carry
        qb, kb = idx
        first = kb == qb
        acc = jnp.where(first, 0.0, acc)
        run = jnp.where(first, 0.0, run)
        z = jnp.einsum('bqhd,bkhd->bhqk', qbl[qb], kbl[kb])
        valid = (kb < qb) | (strict_lower > 0)
        log_beta = jax.nn.log_sigmoid(z)
        log_keep = jnp.where(valid, log_beta - z, 0.0)
        between = jnp.einsum('bhqj,js->bhqs', log_keep, strict_lower) + run[..., None]
        weight = jnp.where(valid, jnp.exp(log_beta + between), 0.0)
        acc = acc + jnp.einsum('bhqk,bkhd->bhqd', weight, vbl[kb])
        run = run + jnp.sum(log_keep, axis=-1)
        return (acc, run), acc

    init = (jnp.zeros((B, H, Q_BLOCK, dh), F32), jnp.zeros((B, H, Q_BLOCK), F32))
    _, partial = lax.scan(step, init, (jnp.asarray(qi, jnp.int32), jnp.asarray(ki, jnp.int32)))
    out = partial[last]
    out = out.transpose(1, 0, 3, 2, 4).reshape(B, S, H, dh)
    return out.astype(q.dtype)

def dsa_attention(q, k, v, q_idx, k_idx, w_idx):
    B, S, H, dh = q.shape
    nb = S // Q_BLOCK
    n_keep = min(TOPK_MAX, S // 4)
    scale = dh ** -0.5
    kif = k_idx.astype(F32)
    key_chunk = jnp.arange(S) // CHUNK
    gather = jax.vmap(lambda kk, ii: kk[ii])

    def block(args):
        qb, qib, wb, blk = args
        qchunk = (blk * Q_BLOCK + jnp.arange(Q_BLOCK)) // CHUNK
        admissible = key_chunk[None, :] <= qchunk[:, None]
        logits = jnp.einsum('bqhd,bkd->bqhk', qib.astype(F32), kif) * (IDX_DIM ** -0.5)
        iscore = jnp.einsum('bqh,bqhk->bqk', wb.astype(F32), jax.nn.relu(logits))
        iscore = jnp.where(admissible[None], iscore, -jnp.inf)
        _, sel = lax.top_k(iscore, n_keep)
        valid = key_chunk[sel] <= qchunk[None, :, None]
        k_sel = gather(k, sel).astype(F32)
        v_sel = gather(v, sel).astype(F32)
        s = jnp.einsum('bqhd,bqnd->bhqn', qb.astype(F32), k_sel) * scale
        s = jnp.where(valid[:, None], s, -jnp.inf)
        p = jax.nn.softmax(s, axis=-1)
        return jnp.einsum('bhqn,bqnd->bqhd', p, v_sel)

    out = lax.map(block, (to_blocks(q, nb), to_blocks(q_idx, nb), to_blocks(w_idx, nb), jnp.arange(nb)))
    return from_blocks(out).astype(q.dtype)

def gated_linear_attention(q, k, v, log_alpha):
    B, S, H, dk = q.shape
    n = S // CHUNK

    def to_chunks(t):
        return t.astype(F32).reshape(B, n, CHUNK, H, -1).transpose(1, 0, 3, 2, 4)

    qc = to_chunks(q) * (dk ** -0.5)
    kc, vc = to_chunks(k), to_chunks(v)
    bc = jnp.cumsum(to_chunks(log_alpha), axis=3)
    causal = jnp.tril(jnp.ones((CHUNK, CHUNK), bool))[:, :, None]

    def step(state, inp):
        qt, kt, vt, bt = inp
        o_inter = jnp.einsum('bhtd,bhde->bhte', qt * jnp.exp(bt), state)
        diff = bt[:, :, :, None, :] - bt[:, :, None, :, :]
        decay = jnp.exp(jnp.where(causal, diff, -jnp.inf))
        a = jnp.einsum('bhtd,bhjd,bhtjd->bhtj', qt, kt, decay)
        o_intra = jnp.einsum('bhtj,bhje->bhte', a, vt)
        b_last = bt[:, :, -1:, :]
        state = (jnp.exp(b_last[:, :, 0, :])[..., None] * state
                 + jnp.einsum('bhjd,bhje->bhde', kt * jnp.exp(b_last - bt), vt))
        return state, o_inter + o_intra

    state0 = jnp.zeros((B, H, dk, v.shape[-1]), F32)
    _, out = lax.scan(step, state0, (qc, kc, vc, bc))
    return out.transpose(1, 0, 3, 2, 4).reshape(B, S, H, -1).astype(v.dtype)

def hybrid_mixer(h, w_in, gla_w_up, gla_b, gla_norm_g, w_br_a, w_br_b, w_br_c, w_mix_out, pos):
    B, S, _ = h.shape
    z = h @ w_in
    (sb_q, sb_k, sb_v, ds_q, ds_k, ds_v, ix_q, ix_k, ix_w,
     gl_q, gl_k, gl_v, gl_g, gl_o, gates) = split_columns(z, SPLIT_SIZES)
    heads = lambda t, nh: t.reshape(B, S, nh, -1)
    y_a = stick_breaking_attention(heads(sb_q, SB_HEADS), heads(sb_k, SB_HEADS), heads(sb_v, SB_HEADS))
    y_a = y_a.reshape(B, S, SB_W) @ w_br_a
    q_b = rope(heads(ds_q, DSA_HEADS), pos)
    k_b = rope(ds_k[:, :, None, :], pos)[:, :, 0, :]
    qi = rope(heads(ix_q, IDX_HEADS), pos)
    ki = rope(ix_k[:, :, None, :], pos)[:, :, 0, :]
    wi = ix_w * (IDX_HEADS ** -0.5)
    y_b = dsa_attention(q_b, k_b, ds_v, qi, ki, wi)
    y_b = y_b.reshape(B, S, DSA_W) @ w_br_b
    gate_logit = (gl_g @ gla_w_up + gla_b).astype(F32)
    log_alpha = jax.nn.log_sigmoid(gate_logit) / GLA_TAU
    o_c = gated_linear_attention(heads(gl_q, GLA_HEADS), heads(gl_k, GLA_HEADS),
                                 heads(gl_v, GLA_HEADS), heads(log_alpha, GLA_HEADS))
    o_c = rmsnorm(o_c, gla_norm_g) * jax.nn.silu(heads(gl_o, GLA_HEADS))
    y_c = o_c.reshape(B, S, GLA_VW) @ w_br_c
    g = jax.nn.sigmoid(gates.reshape(B, S, N_BRANCH, D_MODEL))
    merged = g[:, :, 0] * y_a + g[:, :, 1] * y_b + g[:, :, 2] * y_c
    return merged @ w_mix_out

def memory_cross_attention(h, mem_n, w_xq, w_xkv, w_xo):
    B, S, _ = h.shape
    M = mem_n.shape[1]
    q = (h @ w_xq).reshape(B, S, X_HEADS, X_DIM)
    kv = (mem_n @ w_xkv).reshape(B, M, 2, X_HEADS, X_DIM)
    k, v = kv[:, :, 0], kv[:, :, 1]
    s = jnp.einsum('bqhd,bmhd->bhqm', q.astype(F32), k.astype(F32)) * (X_DIM ** -0.5)
    p = jax.nn.softmax(s, axis=-1)
    o = jnp.einsum('bhqm,bmhd->bqhd', p, v.astype(F32)).astype(h.dtype)
    return o.reshape(B, S, D_MODEL) @ w_xo

def swiglu(h, w_ffn_in, w_ffn_out):
    gu = h @ w_ffn_in
    gate, up = gu[..., :D_FF], gu[..., D_FF:]
    return (jax.nn.silu(gate) * up) @ w_ffn_out

def setup_inputs(seed: int = 0) -> dict:
    key = jax.random.key(seed)
    ks = jax.random.split(key, 20)

    def nrm(k, shape, fan_in):
        return jax.random.normal(k, shape, F32) * (fan_in ** -0.5)

    def gain(k, shape):
        return 1.0 + 0.02 * jax.random.normal(k, shape, F32)

    return {
        'x': jax.random.normal(ks[0], (BATCH, SEQ, D_MODEL), F32),
        'mem': jax.random.normal(ks[1], (BATCH, N_MEM, D_MODEL), F32),
        'mix_norm_g': gain(ks[2], (DEPTH, D_MODEL)),
        'w_in': nrm(ks[3], (DEPTH, D_MODEL, IN_WIDTH), D_MODEL),
        'gla_w_up': nrm(ks[4], (DEPTH, GLA_RANK, GLA_KW), GLA_RANK),
        'gla_b': 0.02 * jax.random.normal(ks[5], (DEPTH, GLA_KW), F32),
        'gla_norm_g': gain(ks[6], (DEPTH, GLA_DV)),
        'w_br_a': nrm(ks[7], (DEPTH, SB_W, D_MODEL), SB_W),
        'w_br_b': nrm(ks[8], (DEPTH, DSA_W, D_MODEL), DSA_W),
        'w_br_c': nrm(ks[9], (DEPTH, GLA_VW, D_MODEL), GLA_VW),
        'w_mix_out': nrm(ks[10], (DEPTH, D_MODEL, D_MODEL), D_MODEL),
        'xattn_norm_g': gain(ks[11], (DEPTH, D_MODEL)),
        'mem_norm_g': gain(ks[12], (DEPTH, D_MODEL)),
        'w_xq': nrm(ks[13], (DEPTH, D_MODEL, D_MODEL), D_MODEL),
        'w_xkv': nrm(ks[14], (DEPTH, D_MODEL, 2 * D_MODEL), D_MODEL),
        'w_xo': nrm(ks[15], (DEPTH, D_MODEL, D_MODEL), D_MODEL),
        'ffn_norm_g': gain(ks[16], (DEPTH, D_MODEL)),
        'w_ffn_in': nrm(ks[17], (DEPTH, D_MODEL, 2 * D_FF), D_MODEL),
        'w_ffn_out': nrm(ks[18], (DEPTH, D_FF, D_MODEL), D_FF),
        'final_norm_g': gain(ks[19], (D_MODEL,)),
    }

def reference(x, mem, mix_norm_g, w_in, gla_w_up, gla_b, gla_norm_g, w_br_a, w_br_b, w_br_c,
              w_mix_out, xattn_norm_g, mem_norm_g, w_xq, w_xkv, w_xo, ffn_norm_g,
              w_ffn_in, w_ffn_out, final_norm_g):
    pos = jnp.arange(x.shape[1], dtype=F32)
    for l in range(DEPTH):
        h = rmsnorm(x, mix_norm_g[l])
        x = x + hybrid_mixer(h, w_in[l], gla_w_up[l], gla_b[l], gla_norm_g[l],
                             w_br_a[l], w_br_b[l], w_br_c[l], w_mix_out[l], pos)
        h = rmsnorm(x, xattn_norm_g[l])
        mem_n = rmsnorm(mem, mem_norm_g[l])
        x = x + memory_cross_attention(h, mem_n, w_xq[l], w_xkv[l], w_xo[l])
        h = rmsnorm(x, ffn_norm_g[l])
        x = x + swiglu(h, w_ffn_in[l], w_ffn_out[l])
    return rmsnorm(x, final_norm_g)


_drawn_inputs = setup_inputs


def setup_inputs(seed=0):
    import zlib

    import numpy as np

    out = dict(_drawn_inputs(seed))
    spreads = {}
    factors = {'gla_b': 8.0,
     'gla_norm_g': 4.416,
     'xattn_norm_g': 8.0,
     'mem_norm_g': 8.0,
     'final_norm_g': 8.059,
     'ffn_norm_g': 3.934}
    for name, (base, spread) in spreads.items():
        noise = np.random.default_rng([zlib.crc32(name.encode()), seed]).standard_normal(out[name].shape)
        drawn = base * np.exp(spread * noise) if base else spread * noise
        out[name] = __import__('jax').numpy.asarray(drawn.astype(out[name].dtype))
    for name, factor in factors.items():
        out[name] = (out[name] * factor).astype(out[name].dtype)
    return out
```

```python
from contextlib import ExitStack

import concourse.bass as bass
import numpy as np
from concourse import mybir

F32 = mybir.dt.float32
F32R = mybir.dt.float32r
I32 = mybir.dt.int32
ALU = mybir.AluOpType
ACT = mybir.ActivationFunctionType
AX_X = mybir.AxisListType.X

P = 128
D_MODEL = 1024
SEQ = 256
DEPTH = 2
N_MEM = 256
KT = D_MODEL // P
TT = SEQ // P
D_FF = 2816
HEADS = 4
HEAD_DIM = 64
GLA_DK = 32
GLA_RANK = 16
GLA_TAU = 16.0
IDX_HEADS = 4
TOPK = 64
CHUNK = 64
X_DIM = D_MODEL // HEADS
EPS = 1e-6
ROPE_THETA = 10000.0
CW = 256
NEG = -3.0e38
TAKEN = -3.4e38

C_SBQ, C_SBK, C_SBV, C_DSQ, C_DSK, C_DSV = 0, 256, 512, 768, 1024, 1088
C_IXQ, C_IXK, C_IXW, C_GLQ, C_GLV, C_GLG, C_GLO, C_GATE = 1152, 1408, 1472, 1476, 1732, 1988, 2004, 2260
IN_WIDTH = C_GATE + 3 * D_MODEL

SLABS = [("ixq", 0), ("keys", 0), ("sbk", 0), ("sbq", 0), ("dsq", 0), ("sbv", 0),
         ("glqk", 0), ("glv", 0), ("glo", 0)]
SLABS += [("xk", j) for j in range(4)] + [("xv", j) for j in range(4)]
SLABS += [("gate", (0, b)) for b in range(3)] + [("gate", (1, b)) for b in range(3)] + [("y", 0)]
SLABS += [("gate", (2, b)) for b in range(3)] + [("y", 1)] + [("gate", (3, b)) for b in range(3)] + [("y", 2), ("y", 3)]
SLABS += [("mix", j) for j in range(4)] + [("xq", j) for j in range(4)] + [("xo", j) for j in range(4)]
N_HEAD_SLABS = len(SLABS)
N_PAIRS = D_FF // CW
N_SLABS = N_HEAD_SLABS + 3 * N_PAIRS
AT = {s: i for i, s in enumerate(SLABS)}
RING = 3
K_IX, K_DS, K_V, K_W, K_G, K_END = 0, 64, 128, 192, 196, 212

PLAN = {
    1: ["rot0"],
    2: ["rot1", "rope0", "rope1", "swap", "swapped"],
    3: ["index"],
    4: ["topk1", "sb_z0", "sb_z1"],
    5: ["sb_ln0", "sb_ln1", "topk0"],
    6: ["sb_keep0", "sb_keep1", "sb_btw0", "rot2"],
    7: ["sb_arg0", "rope2", "sb_exp0", "sb_btw1", "memsplit"],
    8: ["sb_arg1", "sb_w0", "sb_exp1", "sb_pv0", "sb_z2", "sb_z3"],
    9: ["sb_w1", "sb_pv1", "sb_ln2", "sb_ln3", "gl_silu"],
    10: ["sb_keep2", "sb_keep3", "sb_btw2", "gl_gate", "gl_ln"],
    11: ["sb_arg2", "sb_exp2", "sb_btw3", "gl_cum"],
    12: ["sb_arg3", "sb_w2", "sb_exp3", "sb_pv2", "dif0", "dec0"],
    13: ["sb_w3", "sb_pv3", "dif1", "dec1", "lev0"],
    14: ["sb_out", "lev1", "dif2", "dec2", "dif3", "dec3", "app0"],
    15: ["lev2", "app1", "lev3", "dif4", "dec4", "dif5", "dec5"],
    16: ["app2", "lev4", "app3", "lev5", "dif6", "dec6", "dif7", "dec7"],
    17: ["app4", "lev6", "app5", "lev7"],
    18: ["app6", "lev8", "app7"],
    19: ["app8", "gl_pv"],
    20: ["gl_var", "gl_root", "ds_s"],
    21: ["gl_o", "ds_max", "ds_exp", "gl_otr"],
    22: ["gl_out", "ds_norm", "ds_tr", "ds_pv", "ds_out"],
}

EVAC = {}
for _kind, _idx in SLABS:
    for _part in {"y": (), "mix": (), "xo": (), "keys": ("kk", "misc")}.get(_kind, (_kind,)):
        EVAC[(_part, _idx)] = EVAC[_part] = len({k for k in EVAC if isinstance(k, tuple)}) + 1
LEVEL_COUNT = [0, 2, 4, 6, 8, 10, 12, 14, 15, 17]
Y_ORDER = {"a": 1, "c": 2, "b": 3}


def bank_plan():
    at, out = 0, []
    for kind, _ in SLABS:
        n = {"y": 3, "mix": 4, "xo": 4, "keys": 2}.get(kind, 1)
        if n == 4:
            at = 0
        out.append([(at + i) % 4 for i in range(n)])
        at = (at + n) % 4
    return out


BANKS = bank_plan()


def slab_pieces(kind, idx):
    if kind == "keys":
        return [(C_IXK, K_IX, 64), (C_DSK, K_DS, 128), (C_IXW, K_W, 4), (C_GLG, K_G, 16)]
    start = {"ixq": C_IXQ, "sbq": C_SBQ, "sbk": C_SBK, "dsq": C_DSQ, "sbv": C_SBV, "glqk": C_GLQ,
             "glv": C_GLV, "glo": C_GLO}
    if kind in start:
        return [(start[kind], 0, CW)]
    return None


def n_dmas(kind):
    return {"keys": 4, "y": 3}.get(kind, 1)


def landed_plan():
    counts, out = [0] * RING, []
    for n in range(N_SLABS):
        counts[n % RING] += n_dmas(SLABS[n][0]) if n < N_HEAD_SLABS else 1
        out.append(counts[n % RING])
    return out, counts


LANDED, LANDED_TOTAL = landed_plan()

CONST = {}


def constants():
    parts = []

    def put(name, a):
        CONST[name] = (sum(p.shape[1] for p in parts), a.shape[1])
        parts.append(a.astype(np.float32))

    r, c = np.arange(P)[:, None], np.arange(P)[None, :]
    put("ident", r == c)
    lower = (c % HEAD_DIM) < HEAD_DIM // 2
    put("rot", np.where(lower & (r == c + 32), -1.0, 0.0) + np.where(~lower & (r == c - 32), 1.0, 0.0))
    put("later", r > c)
    put("valid", r < c)
    q, k = np.arange(SEQ)[:, None], np.arange(SEQ)[None, :]
    adm = np.where(k // CHUNK <= q // CHUNK, 0.0, NEG)
    put("adm0", adm[:P, :P])
    put("adm1", adm[P:, :])
    inv = np.float32(1.0) / np.float32(ROPE_THETA) ** (np.arange(32, dtype=np.float32) * np.float32(2.0 / HEAD_DIM))
    ang = (np.arange(SEQ, dtype=np.float32)[None, :] * inv[:, None]).astype(np.float32)
    put("cos", np.tile(np.cos(ang), (4, 1)))
    put("sin", np.tile(np.sin(ang), (4, 1)))
    for lev in range(7):
        s = 1 << lev
        put(f"lev{lev}", (r // (2 * s) == c // (2 * s)) & (r % (2 * s) < s) & (c % (2 * s) >= s))
    return np.concatenate(parts, axis=1)


CONST_ARRAY = constants()

PER = dict(
    slab_hi=N_SLABS, slab_lo=N_SLABS, slab_used=N_SLABS,
    gain_rows=5 * 16, gain_t=1, gain=1, gate_w=2 * 16, mem_in=16,
    norm_sq=6, norm_v=3, norm_ln=3, norm_y=3, norm_xn=6, norm_tr=12, norm_hi=12, norm_lo=12,
    evac=34, merged_mul=12, merged=4, merged_hi=4, merged_lo=4, res=12,
    rot=3, rope=3, swap=1, swapped=1, idx=4, idx_relu=4, scored=1,
    sb_z=4, sb_ln=4, sb_keep=4, sb_btw=4, sb_arg=4, sb_exp=4, sb_w=4, sb_pv=4,
    gl_gate=1, gl_x=1, gl_ln=1, gl_cum=1, gl_silu=1, zeroed=1,
    gl_dif=8, gl_dec=8, gl_qk=9, gl_lev=17, gl_app=17, gl_pv=1, gl_sq=1, gl_v=1, gl_y=1, gl_o=1, gl_otr=1,
    ds_s=4, ds_p=4, ds_max=2, ds_exp=2, ds_norm=2, ds_tr=3, ds_pt=3, ds_pv=1,
    y_hi=3, y_lo=3, mem_hi=8, mem_lo=8,
    xs=4, x_max=4, x_exp=4, x_norm=4, x_tr=4, x_pt=4, x_pv=4, o_hi=4, o_lo=4,
    ffn_silu=N_PAIRS, ffn_mul=N_PAIRS, ffn_hi=N_PAIRS, ffn_lo=N_PAIRS,
    act_chain=19, dve_chain=92,
)

PRIMED = {"PE": ("slab_used", "gain_t", "xs", "gl_gate"),
          "DVE": ("slab_lo", "norm_lo", "norm_xn", "res", "rope", "gl_silu", "ffn_mul", "ffn_lo")}
PRIMED_ALL = PRIMED["PE"] + PRIMED["DVE"]


def program(nc, a, out):
    ctx = ExitStack()
    with ctx:
        def sb(name, shape, dt=F32):
            return ctx.enter_context(nc.sbuf_tensor(name, shape, dt))

        S = {n: ctx.enter_context(nc.semaphore(f"s_{n}")) for n in PER}
        landed = [ctx.enter_context(nc.semaphore(f"s_landed{i}")) for i in range(RING)]
        once = {n: ctx.enter_context(nc.semaphore(f"s_{n}")) for n in (
            "consts", "pool_junk", "x_in", "mem_raw", "p_sq", "p_v", "p_ln", "p_y", "p_memx", "p_memtr", "p_memt",
            "mem_out", "ones", "f_sq", "f_v", "f_ln", "f_y", "f_g", "f_out", "f_chain", "stored")}

        const = sb("const", [P, CONST_ARRAY.shape[1]])
        K = {n: const[:, o:o + w] for n, (o, w) in CONST.items()}
        ones = sb("ones", [P, SEQ])
        x = sb("x", [P, TT, D_MODEL])
        xn = sb("xn", [P, TT, D_MODEL])
        h_hi, h_lo = sb("h_hi", [P, KT, SEQ], F32R), sb("h_lo", [P, KT, SEQ], F32R)
        s_hi, s_lo = sb("s_hi", [P, KT, SEQ], F32R), sb("s_lo", [P, KT, SEQ], F32R)
        y_hi, y_lo = sb("y_hi", [P, 3, 2, SEQ], F32R), sb("y_lo", [P, 3, 2, SEQ], F32R)
        raw = sb("raw", [P, RING, 8 * CW])
        w_hi, w_lo = sb("w_hi", [P, RING, 8 * CW], F32R), sb("w_lo", [P, RING, 8 * CW], F32R)
        xk, xv = sb("xk", [P, KT, SEQ]), sb("xv", [P, 2, D_MODEL])
        proj = {n: sb(n, [P, 2 * SEQ]) for n in ("ixq", "kk", "dsq", "sbq", "sbk", "sbv", "glqk", "glv", "glo")}
        gg = sb("gg", [GLA_RANK, SEQ])
        dv = sb("dv", [P, TT, HEAD_DIM])
        wi = sb("wi", [P, TT, IDX_HEADS])
        gain_rows = sb("gain_rows", [P, P])
        gain = sb("gain", [P, 33])
        w_up = sb("w_up", [GLA_RANK, P])
        norm_g = sb("norm_g", [P, HEAD_DIM])
        tmp = sb("tmp", [P, 2 * SEQ])
        scr = sb("scr", [P, 6656])
        st = sb("st", [P, 64])
        junk = sb("junk", [P, 64])
        m8 = sb("m8", [P, TT, 8])
        bank = [ctx.enter_context(nc.psum_tensor(f"bank{i}", [P, 512], F32)) for i in range(8)]
        mem_t = nc.dram_tensor("mem_t_scratch", (P, KT * SEQ), F32, kind="Internal").ap()

        sig = [[scr[:, (3 * s + b) * 512:(3 * s + b + 1) * 512] for b in range(3)] for s in range(2)]
        score = [scr[:, 3072:3200], scr[:, 3200:3456]]
        bias = [scr[:, 3456:3584], scr[:, 3584:3840]]
        F0 = 3840
        relu = {1: [scr[:, F0:F0 + 512], scr[:, F0 + 512:F0 + 1024]],
                0: [scr[:, F0 + 1024:F0 + 1280], scr[:, F0 + 1280:F0 + 1536]]}
        dprob = {1: scr[:, F0:F0 + 1024], 0: scr[:, F0 + 1024:F0 + 1536]}
        dpt = [scr[:, F0 + 1536:F0 + 2048], scr[:, F0 + 2048:F0 + 2560], tmp[:, :]]
        sbuf3 = [[scr[:, F0 + 1152 * p + 384 * i:F0 + 1152 * p + 384 * (i + 1)] for i in range(3)] for p in range(2)]
        dec = [scr[:, F0:F0 + 256], scr[:, F0 + 256:F0 + 512]]
        ke = [scr[:, F0 + 512:F0 + 768], scr[:, F0 + 768:F0 + 1024]]
        att = [scr[:, F0 + 1024:F0 + 1536], scr[:, F0 + 1536:F0 + 2048]]
        attx = scr[:, F0 + 2048:F0 + 2560]
        cum = scr[:, F0 + 2560:F0 + 2816]
        lx, la = tmp[:, 0:SEQ], tmp[:, SEQ:2 * SEQ]
        qe = [xn[:, i, :].rearrange("p (h t) -> p h t", h=HEADS) for i in range(2)]
        xq = xn[:, :, :].rearrange("p a b -> p (a b)").rearrange("p (k t) -> p k t", k=KT)
        xprob = [scr[:, 512 * i:512 * (i + 1)] for i in range(4)]
        xpt = [scr[:, 2048 + 512 * i:2560 + 512 * i] for i in range(4)]
        acc = scr[:, 5632:6144]
        part = scr[:, 6144:6656]
        silu = [scr[:, 0:512], scr[:, 512:1024]]
        actf = [scr[:, 1024:1536], scr[:, 1536:2048]]
        memx = xk[:, :, :].rearrange("p a b -> p (a b)").rearrange("p (t d) -> p t d", t=TT)

        def pair(ap, n=2):
            return ap.rearrange("p (a b) -> p a b", a=n)

        def over(ap, n):
            return ap.unsqueeze(1).to_broadcast([P, n, ap.shape[1]])

        def spread(ap, n):
            return ap.unsqueeze(2).to_broadcast([P, ap.shape[1], n])

        def slot_of(n):
            return n % RING

        def ffn_index(kind, j):
            if kind == "out":
                return 3 * j + 4 if j < N_PAIRS - 1 else 3 * N_PAIRS - 1
            first = 3 * j - 1 if j else 0
            return first + (kind == "up")

        PAIRS_LOOPED = N_PAIRS - 3
        assert PAIRS_LOOPED % 2 == 0

        def ffn_walk(eng, step):
            step("gate", 0, 0)
            step("up", 0, 0)
            for kind, j in (("gate", 1), ("up", 1), ("out", 0)):
                step(kind, j, 0)
            with eng.Fori(0, PAIRS_LOOPED // 2) as i:
                for d in (1, 2):
                    for kind, j in (("gate", d + 1), ("up", d + 1), ("out", d)):
                        step(kind, j, i)
            for kind, j in (("gate", N_PAIRS - 1), ("up", N_PAIRS - 1), ("out", N_PAIRS - 2), ("out", N_PAIRS - 1)):
                step(kind, j, 0)

        block = ctx.enter_context(nc.Block())

        @block.sync
        def _(sp):
            sp.dma_start(const[:, :], a["shape_constants"]).then_inc(once["consts"], 16)
            sp.dma_start(memx, a["mem"].rearrange("b (t p) d -> p (b t) d", p=P)).then_inc(once["mem_raw"], 16)
            sp.dma_start(x[:, :, :], a["x"].rearrange("b (t p) d -> p (b t) d", p=P)).then_inc(once["x_in"], 16)
            sp.wait_ge(once["ones"], 2)
            with sp.Fori(0, DEPTH) as L:
                def after(name, n):
                    sp.wait_ge(S[name], L * PER[name] + n + (name in PRIMED_ALL))

                def load_slab(n, pieces, i=0):
                    if n != RING:
                        after("slab_lo", max(n - RING + 1, 0) + 6 * i)
                    for dst, src in pieces:
                        sp.dma_start(dst, src).then_inc(landed[slot_of(n)], 16)

                def gains():
                    after("gain_t", 0)
                    for r, name in enumerate(("mix_norm_g", "xattn_norm_g", "ffn_norm_g", "mem_norm_g")):
                        sp.dma_start(gain_rows[8 * r:8 * r + 8, :],
                                     a[name][L].rearrange("(k p) -> k p", p=P)).then_inc(S["gain_rows"], 16)
                    sp.dma_start(gain_rows[32:33, :], a["gla_b"][L].rearrange("(a n) -> a n", a=1)).then_inc(S["gain_rows"], 16)

                def col_slab(w, c0, cols=CW):
                    return w[L].rearrange("(k p) n -> p k n", p=P)[:, :, c0:c0 + cols]

                def head_slab(n):
                    kind, idx = SLABS[n]
                    dst = raw[:, slot_of(n), :].rearrange("p (k n) -> p k n", k=KT)
                    pieces = slab_pieces(kind, idx)
                    if pieces is not None:
                        load_slab(n, [(dst[:, :, d:d + c], col_slab(a["w_in"], s, c)) for s, d, c in pieces])
                    elif kind == "gate":
                        j, b = idx
                        load_slab(n, [(dst, col_slab(a["w_in"], C_GATE + b * D_MODEL + j * CW))])
                    elif kind == "y":
                        load_slab(n, [(dst[:, 2 * b:2 * b + 2, :], col_slab(a[w], idx * CW))
                                      for b, w in enumerate(("w_br_a", "w_br_b", "w_br_c"))])
                    elif kind in ("xk", "xv"):
                        load_slab(n, [(dst, col_slab(a["w_xkv"], (kind == "xv") * D_MODEL + idx * CW))])
                    elif kind == "xq":
                        load_slab(n, [(dst, col_slab(a["w_xq"], idx * CW))])
                    else:
                        w = a["w_mix_out" if kind == "mix" else "w_xo"]
                        load_slab(n, [(raw[:, slot_of(n), :].rearrange("p (k n) -> p k n", k=2),
                                       w[L, idx * 256:idx * 256 + 256, :].rearrange("(k p) n -> p k n", p=P))])

                gains()
                head_slab(0)
                head_slab(1)
                after("xs", 0)
                sp.wait_ge(once["mem_out"], 16)
                sp.dma_start(xk[:, :, :].rearrange("p a b -> p (a b)"), mem_t).then_inc(S["mem_in"], 16)
                head_slab(2)
                after("gl_gate", 0)
                sp.dma_start(w_up[:, :], a["gla_w_up"][L]).then_inc(S["gate_w"], 16)
                after("slab_lo", 1)
                after("gl_silu", 0)
                sp.dma_start(norm_g[:, :], a["gla_norm_g"][L].rearrange("(a n) -> a n", a=1)
                             .to_broadcast([P, HEAD_DIM])).then_inc(S["gate_w"], 16)
                for n in range(3, N_HEAD_SLABS):
                    head_slab(n)

                def ffn_slab(kind, j, i):
                    n = N_HEAD_SLABS + ffn_index(kind, j)
                    if kind == "out":
                        src = a["w_ffn_out"][L, bass.ds(i * 2 * CW + j * CW, CW), :].rearrange("(k p) n -> p k n", p=P)
                        dst = raw[:, slot_of(n), :].rearrange("p (k n) -> p k n", k=2)
                    else:
                        c0 = (kind == "up") * D_FF + j * CW
                        src = a["w_ffn_in"][L].rearrange("(k p) n -> p k n", p=P)[:, :, bass.ds(i * 2 * CW + c0, CW)]
                        dst = raw[:, slot_of(n), :].rearrange("p (k n) -> p k n", k=KT)
                    load_slab(n, [(dst, src)], i)

                ffn_walk(sp, ffn_slab)
            sp.wait_ge(S["xs"], DEPTH * PER["xs"] + 1)
            sp.dma_start(xk[:, 0:4, :].rearrange("p a b -> p (a b)"),
                         a["final_norm_g"].rearrange("(a n) -> a n", a=1).to_broadcast([P, D_MODEL])).then_inc(once["f_g"], 16)
            sp.wait_ge(once["f_out"], 2)
            sp.dma_start(out.rearrange("b (t p) d -> p (b t) d", p=P), xn[:, :, :]).then_inc(once["stored"], 16)
            sp.wait_ge(once["stored"], 16)

        @block.gpsimd
        def _(pool):
            pool.memset(ones[:, :], 1.0).then_inc(once["ones"], 1)
            pool.memset(gain_rows[:, :], 0.0).then_inc(once["ones"], 1)
            pool.wait_ge(once["ones"], 2)
            with pool.Fori(0, DEPTH) as L:
                pool.wait_ge(S["norm_tr"], L * PER["norm_tr"] + 4)
                pool.tensor_tensor(junk[:, 0:1], ones[:, 0:1], ones[:, 0:1], ALU.add).then_inc(once["pool_junk"], 1)
                pool.memset(xn[:, :, :], 0.0).then_inc(S["zeroed"], 1)

        @block.tensor
        def _(pe):
            for name in PRIMED["PE"]:
                pe.sem_inc(S[name], 1)
            pe.wait_ge(once["consts"], 16)
            for i in range(4):
                pe.wait_ge(once["p_memx"], 2)
                for kk in range(2):
                    for t in range(TT):
                        mm = pe.transpose(bank[4 + i][:, kk * SEQ + t * P:kk * SEQ + (t + 1) * P],
                                          memx[:, t, (2 * i + kk) * P:(2 * i + kk + 1) * P], K["ident"])
                mm.then_inc(once["p_memtr"], 1)
            pe.wait_ge(once["p_memt"], 4)

            with pe.Fori(0, DEPTH) as L:
                def after(name, n):
                    pe.wait_ge(S[name], L * PER[name] + n + (name in PRIMED_ALL))

                reader = {b: ("ffn_mul", 0) for b in range(4)}
                reader.update({b: ("res", 0) for b in range(4, 8)})

                def take(b, name, n):
                    after(*reader[b])
                    reader[b] = (name, n)

                def three(dst, st_hi, st_lo, mv_hi, mv_lo, first, last):
                    pe.matmul(dst, st_hi, mv_hi, start=first, stop=False, skip_group_check=True)
                    pe.matmul(dst, st_hi, mv_lo, start=False, stop=False, skip_group_check=True)
                    return pe.matmul(dst, st_lo, mv_hi, start=False, stop=last, skip_group_check=True)

                def feature_major(dst, n, width, c0, cols, act_hi, act_lo, norm=None):
                    for k, (ah, al) in enumerate(zip(act_hi, act_lo)):
                        if norm is not None and k % 2 == 0:
                            after("norm_lo", 4 * norm + k // 2 + 1)
                        o = k * width + c0
                        wh, wl = w_hi[:, slot_of(n), o:o + cols], w_lo[:, slot_of(n), o:o + cols]
                        mm = three(dst, wh, wl, ah, al, k == 0, k == len(act_hi) - 1)
                    return mm

                def token_major(dst, n, c0, cols, t, a_hi, a_lo):
                    for k in range(KT):
                        o = k * CW + c0
                        mm = three(dst, a_hi[:, k, t * P:(t + 1) * P], a_lo[:, k, t * P:(t + 1) * P],
                                   w_hi[:, slot_of(n), o:o + cols], w_lo[:, slot_of(n), o:o + cols], k == 0, k == KT - 1)
                    return mm

                def row_slab(n, banks, k_hi, k_lo, first, last):
                    wh = w_hi[:, slot_of(n), :].rearrange("p (k n) -> p k n", k=2)
                    wl = w_lo[:, slot_of(n), :].rearrange("p (k n) -> p k n", k=2)
                    for k in range(2):
                        for t in range(TT):
                            ah, al = k_hi[:, k, t * P:(t + 1) * P], k_lo[:, k, t * P:(t + 1) * P]
                            for st_, w, begin, end in ((ah, wh, first and k == 0, False), (ah, wl, False, False),
                                                       (al, wh, False, last and k == 1)):
                                for m in range(2):
                                    mm = pe.matmul(bank[banks[2 * t + m]][:, :], st_, w[:, k, m * 512:(m + 1) * 512],
                                                   start=begin, stop=end, skip_group_check=True)
                    return mm

                def norm(n):
                    after("norm_xn", 2 * n + 2)
                    for i in range(4):
                        take(4 + i, "norm_lo", 4 * n + i + 1)
                        for kk in range(2):
                            for t in range(TT):
                                mm = pe.transpose(bank[4 + i][:, kk * SEQ + t * P:kk * SEQ + (t + 1) * P],
                                                  xn[:, t, (2 * i + kk) * P:(2 * i + kk + 1) * P], K["ident"])
                        mm.then_inc(S["norm_tr"], 1)

                def rot(i):
                    src = proj[("ixq", "kk", "dsq")[i]]
                    after("evac", (1, 2, EVAC["dsq"])[i])
                    b = (4, 5, 4)[i]
                    take(b, "rope", i + 1)
                    w = SEQ if i == 1 else 2 * SEQ
                    pe.matmul(bank[b][:, 0:w], K["rot"], src[:, 0:w], start=True, stop=True).then_inc(S["rot"], 1)

                def swap():
                    after("rope", 2)
                    take(5, "swapped", 1)
                    for half in range(2):
                        mm = pe.matmul(bank[5][64 * half:64 * half + 64, 0:SEQ], K["ident"][:, 64 - 64 * half:P - 64 * half],
                                       proj["kk"][:, 0:SEQ], start=True, stop=True)
                    mm.then_inc(S["swap"], 1)

                def head_scores(q, kt, signal, freed):
                    for n, (t, half) in enumerate(((1, 0), (1, 1), (0, 0), (0, 1))):
                        b, nk = (4 + 2 * t + half), (t + 1) * P
                        take(b, freed, n + 1)
                        r = slice(64 * half, 64 * half + 64)
                        for hh in range(2):
                            mm = pe.matmul(bank[b][:, hh * nk:(hh + 1) * nk],
                                           q[r, hh * SEQ + t * P:hh * SEQ + (t + 1) * P],
                                           proj["kk"][r, (kt ^ half) * SEQ:(kt ^ half) * SEQ + nk], start=True, stop=True)
                        mm.then_inc(S[signal], 1)

                def index():
                    after("swapped", 1)
                    head_scores(proj["ixq"], 0, "idx", "idx_relu")

                def ds_s():
                    after("rope", 3)
                    head_scores(proj["dsq"], 1, "ds_s", "ds_p")

                def sb_z(h):
                    after("evac", EVAC["sbq"])
                    b, r, o = 4 + h % 2, slice(64 * (h % 2), 64 * (h % 2) + 64), (h // 2) * SEQ
                    take(b, "sb_keep", h + 1)
                    pe.matmul(bank[b][:, 0:SEQ], proj["sbk"][r, o:o + P], proj["sbq"][r, o:o + SEQ], start=True, stop=True)
                    pe.matmul(bank[b][:, SEQ:SEQ + P], proj["sbk"][r, o + P:o + SEQ], proj["sbq"][r, o + P:o + SEQ],
                              start=True, stop=True).then_inc(S["sb_z"], 1)

                def sb_btw(h):
                    keep = sbuf3[h % 2][1]
                    after("sb_keep", h + 1)
                    take(6, "sb_arg", h + 1)
                    pe.matmul(bank[6][:, 0:384], K["later"], keep, start=True, stop=False, skip_group_check=True)
                    pe.matmul(bank[6][:, P:2 * P], ones[:, 0:P], keep[:, 256:384], start=False, stop=True,
                              skip_group_check=True).then_inc(S["sb_btw"], 1)

                def sb_pv(h):
                    w = sbuf3[h % 2][0]
                    after("sb_w", h + 1)
                    if h == 0:
                        after("evac", EVAC["sbv"])
                        take(7, "y_lo", 1)
                    o = bank[7][64 * (h % 2):64 * (h % 2) + 64, (h // 2) * SEQ:(h // 2 + 1) * SEQ]
                    v = pair(proj["sbv"][:, :])
                    pe.matmul(o, v[:, 0, h * 64:h * 64 + 64], w[:, 0:SEQ], start=True, stop=False, skip_group_check=True)
                    pe.matmul(o[:, P:SEQ], v[:, 1, h * 64:h * 64 + 64], w[:, SEQ:384], start=False, stop=True,
                              skip_group_check=True).then_inc(S["sb_pv"], 1)

                def gl_gate():
                    after("evac", EVAC["misc"])
                    after("gate_w", 32)
                    take(5, "gl_x", 1)
                    pe.matmul(bank[5][:, 0:SEQ], w_up[:, :], gg[:, :], start=True, stop=True).then_inc(S["gl_gate"], 1)

                def level(i):
                    after("gl_qk", i + 1)
                    k = proj["glqk"][:, SEQ:2 * SEQ] if i == 8 else ke[i % 2]
                    for t in ((1,) if i == 7 else (0, 1)):
                        b = 4 + 2 * (i % 2) + t
                        n = LEVEL_COUNT[i] + t + 1 if i != 7 else LEVEL_COUNT[i] + 1
                        take(b, "gl_app", n)
                        kt = 0 if i == 7 else t
                        pe.matmul(pair(bank[b][:, :], 4), k[:, kt * P:(kt + 1) * P], qe[i % 2][:, :, t * P:(t + 1) * P],
                                  start=True, stop=True).then_inc(S["gl_lev"], 1)

                def gl_pv():
                    after("gl_app", LEVEL_COUNT[9])
                    after("evac", EVAC["glv"])
                    take(6, "gl_o", 1)
                    v = pair(proj["glv"][:, :])
                    for t in range(TT):
                        for h in range(HEADS):
                            o = bank[6][:, t * 256 + h * 64:t * 256 + (h + 1) * 64]
                            c = slice(h * 64, (h + 1) * 64)
                            mm = pe.matmul(o, att[t][:, h * P:(h + 1) * P], v[:, t, c], start=True, stop=(t == 0),
                                           skip_group_check=True)
                            if t == 1:
                                mm = pe.matmul(o, attx[:, h * P:(h + 1) * P], v[:, 0, c], start=False, stop=True,
                                               skip_group_check=True)
                    mm.then_inc(S["gl_pv"], 1)

                def gl_otr():
                    after("gl_o", 1)
                    take(7, "y_lo", Y_ORDER["c"])
                    for k in range(2):
                        for t in range(TT):
                            mm = pe.transpose(bank[7][:, k * SEQ + t * P:k * SEQ + (t + 1) * P],
                                              tmp[:, t * SEQ + k * P:t * SEQ + (k + 1) * P], K["ident"])
                    mm.then_inc(S["gl_otr"], 1)

                def ds_tr():
                    p1, p0 = pair(dprob[1], 4), pair(dprob[0], 4)
                    after("ds_norm", 2)
                    for g in range(2):
                        take(4 + g, "ds_pt", g + 1)
                        for s in range(2):
                            pe.transpose(bank[4 + g][:, s * SEQ:s * SEQ + P], p0[:, 2 * g + s, :], K["ident"])
                            mm = pe.transpose(bank[4 + g][:, s * SEQ + P:(s + 1) * SEQ], p1[:, 2 * g + s, 0:P], K["ident"])
                        mm.then_inc(S["ds_tr"], 1)
                    take(6, "ds_pt", 3)
                    for s in range(4):
                        mm = pe.transpose(bank[6][:, s * P:(s + 1) * P], p1[:, s, P:SEQ], K["ident"])
                    mm.then_inc(S["ds_tr"], 1)

                def ds_pv():
                    after("ds_pt", 3)
                    take(7, "y_lo", Y_ORDER["b"])
                    for s in range(4):
                        h = 2 * (s % 2) + s // 2
                        o = bank[7][64 * (h % 2):64 * (h % 2) + 64, (h // 2) * SEQ:(h // 2 + 1) * SEQ]
                        pe.matmul(o, dv[:, 0, :], dpt[s // 2][:, (s % 2) * SEQ:(s % 2 + 1) * SEQ], start=True, stop=False,
                                  skip_group_check=True)
                        mm = pe.matmul(o[:, P:SEQ], dv[:, 1, :], dpt[2][:, s * P:(s + 1) * P], start=False, stop=True,
                                       skip_group_check=True)
                    mm.then_inc(S["ds_pv"], 1)

                def cross():
                    after("evac", EVAC[("xq", 3)])
                    for i in range(4):
                        t = i % 2
                        take(4 + i, "x_exp", i + 1)
                        for s in range(2):
                            h = 2 * (i // 2) + s
                            for k in range(2):
                                mm = pe.matmul(bank[4 + i][:, s * SEQ:(s + 1) * SEQ], xq[:, 2 * h + k, t * P:(t + 1) * P],
                                               xk[:, 2 * h + k, :], start=(k == 0), stop=(k == 1), skip_group_check=True)
                        mm.then_inc(S["xs"], 1)
                    for i in range(4):
                        m = i % 2
                        after("x_norm", 2 * (i // 2) + 2)
                        take(4 + i, "x_pt", i + 1)
                        for s in range(2):
                            for t in range(TT):
                                src = pair(xprob[2 * (i // 2) + t])[:, s, m * P:(m + 1) * P]
                                mm = pe.transpose(bank[4 + i][:, s * SEQ + t * P:s * SEQ + (t + 1) * P], src, K["ident"])
                        mm.then_inc(S["x_tr"], 1)
                    for h in range(HEADS):
                        after("x_pt", 2 * (h // 2) + 2)
                        take(4 + h, "o_lo", h + 1)
                        for d in range(2):
                            for m in range(2):
                                mm = pe.matmul(bank[4 + h][:, d * SEQ:(d + 1) * SEQ],
                                               xv[:, m, h * X_DIM + d * P:h * X_DIM + (d + 1) * P],
                                               pair(xpt[2 * (h // 2) + m])[:, h % 2, :], start=(m == 0), stop=(m == 1),
                                               skip_group_check=True)
                        mm.then_inc(S["x_pv"], 1)

                steps = {"index": index, "swap": swap, "ds_s": ds_s, "gl_gate": gl_gate, "gl_pv": gl_pv, "gl_otr": gl_otr,
                         "ds_tr": ds_tr, "ds_pv": ds_pv}
                for i in range(3):
                    steps[f"rot{i}"] = lambda i=i: rot(i)
                for h in range(HEADS):
                    steps[f"sb_z{h}"] = lambda h=h: sb_z(h)
                    steps[f"sb_btw{h}"] = lambda h=h: sb_btw(h)
                    steps[f"sb_pv{h}"] = lambda h=h: sb_pv(h)
                for i in range(9):
                    steps[f"lev{i}"] = lambda i=i: level(i)

                def product(n):
                    kind, idx = SLABS[n]
                    b = [bank[i] for i in BANKS[n]]
                    after("slab_lo", n + 1)
                    if kind in ("mix", "xo"):
                        after("merged_lo" if kind == "mix" else "o_lo", idx + 1)
                        if idx == 0:
                            for i in BANKS[n]:
                                take(i, "res", (4 if kind == "mix" else 8))
                        mm = row_slab(n, BANKS[n], s_hi[:, 2 * idx:2 * idx + 2, :], s_lo[:, 2 * idx:2 * idx + 2, :],
                                      idx == 0, idx == 3)
                    elif kind == "y":
                        after("y_lo", 3)
                        for i, br in zip(BANKS[n], range(3)):
                            take(i, "merged_mul", 3 * idx + br + 1)
                            for f in range(2):
                                mm = feature_major(bank[i][:, f * SEQ:(f + 1) * SEQ], n, CW, 2 * br * CW + f * P, P,
                                                   [y_hi[:, br, k, :] for k in range(2)], [y_lo[:, br, k, :] for k in range(2)])
                    else:
                        for i, part in zip(BANKS[n], ("kk", "misc") if kind == "keys" else (kind,)):
                            take(i, "evac", EVAC[(part, idx)])
                        if kind in ("sbv", "glv", "glo"):
                            for t in range(TT):
                                mm = token_major(b[0][:, t * CW:(t + 1) * CW], n, 0, CW, t, h_hi, h_lo)
                        elif kind == "xv":
                            for t in range(2):
                                mm = token_major(b[0][:, t * CW:(t + 1) * CW], n, 0, CW, t, s_hi, s_lo)
                        elif kind == "keys":
                            hs = [h_hi[:, k, :] for k in range(KT)], [h_lo[:, k, :] for k in range(KT)]
                            feature_major(b[0][:, 0:SEQ], n, CW, K_IX, P, *hs)
                            for t in range(TT):
                                token_major(b[1][:, SEQ + t * 68:SEQ + (t + 1) * 68], n, K_V, 68, t, h_hi, h_lo)
                            mm = feature_major(b[1][0:GLA_RANK, 0:SEQ], n, CW, K_G, GLA_RANK, *hs)
                        else:
                            if kind == "xk":
                                after("mem_lo", KT)
                            ah, al = (s_hi, s_lo) if kind == "xk" else (h_hi, h_lo)
                            for f in range(2):
                                mm = feature_major(b[0][:, f * SEQ:(f + 1) * SEQ], n, CW, f * P, P,
                                                   [ah[:, k, :] for k in range(KT)], [al[:, k, :] for k in range(KT)],
                                                   {0: 0, AT[("xq", 0)]: 1}.get(n) if f == 0 else None)
                    mm.then_inc(S["slab_used"], 1)

                pe.wait_ge(once["ones"], 2)
                after("gain_rows", 80)
                take(0, "gain", 1)
                pe.transpose(bank[0][:, 0:P], gain_rows[:, :], K["ident"]).then_inc(S["gain_t"], 1)
                norm(0)
                for n in range(N_HEAD_SLABS):
                    if SLABS[n] == ("xq", 0):
                        norm(1)
                    if SLABS[n] == ("xo", 0):
                        cross()
                    product(n)
                    for s in PLAN.get(n, ()):
                        if s in steps:
                            steps[s]()
                norm(2)

                def ffn(kind, j, i):
                    n = N_HEAD_SLABS + ffn_index(kind, j)
                    after("slab_lo", n + 1 + 6 * i)
                    if kind == "out":
                        after("ffn_lo", j + 1 + 2 * i)
                        o = 2 * (j % 2)
                        mm = row_slab(n, (4, 5, 6, 7), s_hi[:, o:o + 2, :], s_lo[:, o:o + 2, :], j == 0, j == N_PAIRS - 1)
                    else:
                        b = 2 * (j % 2) + (kind == "up")
                        if j < 2:
                            after(*reader[b])
                        else:
                            after("ffn_mul", j - 1 + 2 * i)
                        for f in range(2):
                            mm = feature_major(bank[b][:, f * SEQ:(f + 1) * SEQ], n, CW, f * P, P,
                                               [h_hi[:, k, :] for k in range(KT)], [h_lo[:, k, :] for k in range(KT)],
                                               2 if (kind, j, f) == ("gate", 0, 0) else None)
                    mm.then_inc(S["slab_used"], 1)

                ffn_walk(pe, ffn)

        @block.scalar
        def _(act):
            def scaled_exp_of_log(ln_out, v, y, wait_ln, done_ln, done_y):
                act.activation(ln_out, v, ACT.Ln).then_inc(done_ln, 1)
                wait_ln()
                act.activation(y, ln_out, ACT.Exp, scale=-0.5).then_inc(done_y, 1)

            act.wait_ge(once["mem_raw"], 16)
            for t in range(TT):
                act.activation(xn[:, t, :], memx[:, t, :], ACT.Square, accum_out=st[:, t:t + 1]).then_inc(once["p_sq"], 1)
            act.wait_ge(once["p_v"], 1)
            scaled_exp_of_log(st[:, 4:6], st[:, 2:4], st[:, 6:8], lambda: act.wait_ge(once["p_ln"], 1), once["p_ln"], once["p_y"])
            xn_flat = xn[:, :, :].rearrange("p a b -> p (a b)")
            for i in range(4):
                act.wait_ge(once["p_memtr"], i + 1)
                act.activation(xn_flat[:, i * 512:(i + 1) * 512], bank[4 + i][:, :], ACT.Copy).then_inc(once["p_memt"], 1)
            act.wait_ge(once["p_memt"], 4)
            act.dma_start(mem_t, xn_flat).then_inc(once["mem_out"], 16)
            act.wait_ge(once["mem_out"], 16)
            act.wait_ge(once["x_in"], 16)

            with act.Fori(0, DEPTH) as L:
                links = [0]

                def after(name, n):
                    act.wait_ge(S[name], L * PER[name] + n + (name in PRIMED_ALL))

                def link(ins):
                    links[0] += 1
                    ins.then_inc(S["act_chain"], 1)
                    after("act_chain", links[0])

                def upper(n, i=0):
                    act.wait_ge(landed[slot_of(n)], L * (16 * LANDED_TOTAL[slot_of(n)]) + 16 * LANDED[n] + 32 * i)
                    after("slab_used", max(n - RING + 1, 0) + 6 * i)
                    dst, src = (r[:, slot_of(n), :] for r in (w_hi, raw))
                    kind = SLABS[n][0] if n < N_HEAD_SLABS else ""
                    if kind == "keys":
                        dst, src = (r.rearrange("p (k n) -> p k n", k=KT)[:, :, 0:K_END] for r in (dst, src))
                    elif kind == "y":
                        dst, src = dst[:, 0:6 * CW], src[:, 0:6 * CW]
                    act.activation(dst, src, ACT.Copy).then_inc(S["slab_hi"], 1)

                def norm(n):
                    act.activation(junk[:, 62:63], ones[:, 0:1], ACT.Ln)
                    if n == 1:
                        after("gl_lev", PER["gl_lev"])
                    for t in range(TT):
                        after("res", 4 * (n - 1) + 2 * t + 2 if n else 0)
                        act.activation(xn[:, t, :], x[:, t, :], ACT.Square, accum_out=st[:, t:t + 1]).then_inc(S["norm_sq"], 1)
                    after("norm_v", n + 1)
                    scaled_exp_of_log(st[:, 4:6], st[:, 2:4], st[:, 6:8], lambda: after("norm_ln", n + 1),
                                      S["norm_ln"], S["norm_y"])
                    for i in range(4):
                        after("norm_tr", 4 * n + i + 1)
                        for k in range(2):
                            f = 2 * i + k
                            ins = act.activation(h_hi[:, f, :], bank[4 + i][:, k * SEQ:(k + 1) * SEQ], ACT.Copy,
                                                 scale=gain[:, 8 * n + f:8 * n + f + 1])
                        ins.then_inc(S["norm_hi"], 1)

                def evacuate(n):
                    kind, idx = SLABS[n]
                    if kind in ("y", "mix", "xo"):
                        return
                    after("slab_used", n + 1)
                    b = bank[BANKS[n][0]]
                    if kind == "keys":
                        act.activation(proj["kk"][:, 0:SEQ], b[:, 0:SEQ], ACT.Copy).then_inc(S["evac"], 1)
                        b = bank[BANKS[n][1]]
                        act.activation(gg[:, :], b[0:GLA_RANK, 0:SEQ], ACT.Copy)
                        rest = b[:, SEQ:SEQ + 2 * 68].rearrange("p (t c) -> p t c", t=TT)
                        act.activation(dv[:, :, :], rest[:, :, 0:HEAD_DIM], ACT.Copy)
                        ins = act.activation(wi[:, :, :], rest[:, :, HEAD_DIM:68], ACT.Copy, scale=IDX_HEADS ** -0.5)
                    elif kind == "glqk":
                        act.activation(proj[kind][:, 0:SEQ], b[:, 0:SEQ], ACT.Copy, scale=GLA_DK ** -0.5)
                        ins = act.activation(proj[kind][:, SEQ:], b[:, SEQ:], ACT.Copy)
                    elif kind == "glo":
                        after("rope", 3)
                        act.activation(proj[kind][:, :], b[:, :], ACT.Copy)
                        ins = act.activation(tmp[:, :], b[:, :], ACT.Exp, scale=-1.0)
                    elif kind == "xk":
                        if idx == 0:
                            after("mem_lo", KT)
                        ins = act.activation(xk[:, 2 * idx:2 * idx + 2, :], pair(b[:, :]), ACT.Copy)
                    elif kind == "xv":
                        ins = act.activation(xv[:, :, idx * CW:(idx + 1) * CW], pair(b[:, :]), ACT.Copy)
                    elif kind == "xq":
                        ins = act.activation(xq[:, 2 * idx:2 * idx + 2, :], pair(b[:, :]), ACT.Copy)
                    elif kind == "gate":
                        j, br = idx
                        if j < 2:
                            after("ffn_lo", 0)
                        else:
                            after("merged_mul", 3 * (j - 1))
                        ins = act.activation(sig[j % 2][br], b[:, :], ACT.Sigmoid)
                    else:
                        ins = act.activation(proj[kind][:, :], b[:, :], ACT.Copy, scale=HEAD_DIM ** -0.5 if kind == "sbq" else 1.0)
                    ins.then_inc(S["evac"], 1)

                def index():
                    for n, (t, half) in enumerate(((1, 0), (1, 1), (0, 0), (0, 1))):
                        after("idx", n + 1)
                        nk = (t + 1) * P
                        act.activation(relu[t][half], bank[4 + 2 * t + half][:, 0:2 * nk], ACT.Relu,
                                       scale=HEAD_DIM ** -0.5).then_inc(S["idx_relu"], 1)

                def swapped():
                    after("swap", 1)
                    act.activation(proj["kk"][:, SEQ:], bank[5][:, 0:SEQ], ACT.Copy).then_inc(S["swapped"], 1)

                def memsplit():
                    after("mem_in", 16)
                    after("slab_used", 0)
                    for k in range(KT):
                        act.activation(s_hi[:, k, :], xk[:, k, :], ACT.Copy, scale=gain[:, 24 + k:25 + k]).then_inc(S["mem_hi"], 1)

                def sb_ln(h):
                    b = sbuf3[h % 2][0]
                    after("sb_z", h + 1)
                    if h == 0:
                        after("scored", 1)
                    if h >= 2:
                        after("sb_pv", h - 1)
                    link(act.activation(b, bank[4 + h % 2][:, 0:384], ACT.Abs))
                    link(act.activation(b, b, ACT.Exp, scale=-1.0))
                    act.activation(b, b, ACT.Ln, bias=1.0).then_inc(S["sb_ln"], 1)

                def sb_exp(h):
                    after("sb_arg", h + 1)
                    act.activation(sbuf3[h % 2][0], sbuf3[h % 2][2], ACT.Exp).then_inc(S["sb_exp"], 1)

                def branch_hi(br, done, order):
                    after(done, PER[done])
                    act.activation(y_hi[:, br, :, :], pair(bank[7][:, :]), ACT.Copy).then_inc(S["y_hi"], 1)

                def gl_ln():
                    after("gl_x", 1)
                    link(act.activation(la, lx, ACT.Abs))
                    link(act.activation(la, la, ACT.Exp, scale=-1.0))
                    act.activation(la, la, ACT.Ln, bias=1.0).then_inc(S["gl_ln"], 1)

                def decay(i):
                    after("gl_dif", i + 1)
                    link(act.activation(dec[i % 2], dec[i % 2], ACT.Abs))
                    act.activation(dec[i % 2], dec[i % 2], ACT.Exp, scale=-1.0 / GLA_TAU).then_inc(S["gl_dec"], 1)

                def gl_var():
                    after("gl_pv", 1)
                    after("gl_silu", 1)
                    act.activation(tmp[:, :], bank[6][:, :], ACT.Square).then_inc(S["gl_sq"], 1)

                def gl_root():
                    after("gl_v", 1)
                    link(act.activation(st[:, 26:34], st[:, 18:26], ACT.Ln))
                    act.activation(st[:, 26:34], st[:, 26:34], ACT.Exp, scale=-0.5).then_inc(S["gl_y"], 1)

                def ds_exp():
                    for n, t in enumerate((1, 0)):
                        after("ds_max", n + 1)
                        p = pair(dprob[t], 4)
                        for s in range(4):
                            c = 4 * n + s
                            ins = act.activation(p[:, s, :], p[:, s, :], ACT.Exp, bias=st[:, 42 + c:43 + c],
                                                 accum_out=st[:, 50 + c:51 + c])
                        ins.then_inc(S["ds_exp"], 1)

                def ds_tr():
                    for g in range(3):
                        after("ds_tr", g + 1)
                        act.activation(dpt[g], bank[4 + g][:, :], ACT.Copy).then_inc(S["ds_pt"], 1)

                def merge(j):
                    after("merged", j + 1)
                    act.activation(s_hi[:, 2 * j:2 * j + 2, :], pair(acc), ACT.Copy).then_inc(S["merged_hi"], 1)

                def cross():
                    for i in range(4):
                        after("x_max", i + 1)
                        for s in range(2):
                            c = 2 * i + s
                            ins = act.activation(pair(xprob[i])[:, s, :], bank[4 + i][:, s * SEQ:(s + 1) * SEQ], ACT.Exp,
                                                 bias=st[:, 42 + c:43 + c], scale=X_DIM ** -0.5, accum_out=st[:, 50 + c:51 + c])
                        ins.then_inc(S["x_exp"], 1)
                    for i in range(4):
                        after("x_tr", i + 1)
                        act.activation(xpt[i], bank[4 + i][:, :], ACT.Copy).then_inc(S["x_pt"], 1)
                    for h in range(HEADS):
                        after("x_pv", h + 1)
                        act.activation(s_hi[:, 2 * h:2 * h + 2, :], pair(bank[4 + h][:, :]), ACT.Copy).then_inc(S["o_hi"], 1)

                steps = {"index": index, "swapped": swapped, "memsplit": memsplit, "gl_ln": gl_ln, "gl_var": gl_var, "gl_root": gl_root,
                         "ds_exp": ds_exp, "ds_tr": ds_tr,
                         "sb_out": lambda: branch_hi(0, "sb_pv", 1), "gl_out": lambda: branch_hi(2, "gl_otr", 2),
                         "ds_out": lambda: branch_hi(1, "ds_pv", 3)}
                for h in range(HEADS):
                    steps[f"sb_ln{h}"] = lambda h=h: sb_ln(h)
                    steps[f"sb_exp{h}"] = lambda h=h: sb_exp(h)
                for i in range(8):
                    steps[f"dec{i}"] = lambda i=i: decay(i)

                upper(0)
                upper(1)
                after("gain_t", 1)
                after("norm_lo", 0)
                act.activation(gain[:, :], bank[0][:, 0:33], ACT.Copy).then_inc(S["gain"], 1)
                after("gain", 1)
                norm(0)
                for n in range(N_HEAD_SLABS):
                    late = SLABS[n] in (("xq", 0), ("xo", 0))
                    if not late:
                        upper(n + 2)
                    if n:
                        evacuate(n - 1)
                        if SLABS[n - 1][0] == "y":
                            merge(SLABS[n - 1][1])
                    if SLABS[n] == ("xq", 0):
                        norm(1)
                    if SLABS[n] == ("xo", 0):
                        cross()
                    if late:
                        upper(n + 2)
                    for s in PLAN.get(n, ()):
                        if s in steps:
                            steps[s]()
                norm(2)

                def silu_of(p, i):
                    after("slab_used", N_HEAD_SLABS + ffn_index("up", p) + 1 + 6 * i)
                    after("ffn_mul", max(p - 1, 0) + 2 * i)
                    act.activation(silu[p % 2], bank[2 * (p % 2)][:, :], ACT.Silu).then_inc(S["ffn_silu"], 1)

                def act_hi(p, i):
                    after("ffn_mul", p + 1 + 2 * i)
                    after("slab_used", N_HEAD_SLABS + max(3 * p - 1, 0) + 6 * i)
                    o = 2 * (p % 2)
                    act.activation(s_hi[:, o:o + 2, :], pair(actf[p % 2]), ACT.Copy).then_inc(S["ffn_hi"], 1)

                def ffn(kind, j, i):
                    n = N_HEAD_SLABS + ffn_index(kind, j)
                    if kind == "gate" and j:
                        silu_of(j - 1, i)
                    if kind == "up" and j:
                        act_hi(j - 1, i)
                    if n + 2 < N_SLABS:
                        upper(n + 2, i)
                    if kind == "out" and j == N_PAIRS - 2:
                        silu_of(N_PAIRS - 1, 0)
                        act_hi(N_PAIRS - 1, 0)

                ffn_walk(act, ffn)
                assert links[0] == PER["act_chain"], links[0]

            act.wait_ge(S["res"], DEPTH * PER["res"] + 1)
            for t in range(TT):
                act.activation(xn[:, t, :], x[:, t, :], ACT.Square, accum_out=st[:, t:t + 1]).then_inc(once["f_sq"], 1)
            act.wait_ge(once["f_v"], 1)
            scaled_exp_of_log(st[:, 4:6], st[:, 2:4], st[:, 6:8], lambda: act.wait_ge(once["f_ln"], 1), once["f_ln"], once["f_y"])

        @block.vector
        def _(dve):
            def mean_and_eps(v, sq, count):
                return dve.tensor_scalar(v, sq, 1.0 / count, EPS, ALU.mult, ALU.add)

            def refine(link, y, v, t):
                link(dve.tensor_tensor(t, y, y, ALU.mult))
                link(dve.tensor_tensor(t, t, v, ALU.mult))
                link(dve.tensor_scalar(t, t, -0.5, 1.5, ALU.mult, ALU.add))
                link(dve.tensor_tensor(y, y, t, ALU.mult))

            for name in PRIMED["DVE"]:
                dve.sem_inc(S[name], 1)
            outside = [0]

            def link_once(ins):
                outside[0] += 1
                ins.then_inc(once["f_chain"], 1)
                dve.wait_ge(once["f_chain"], outside[0])

            dve.wait_ge(once["p_sq"], 2)
            mean_and_eps(st[:, 2:4], st[:, 0:2], D_MODEL).then_inc(once["p_v"], 1)
            dve.wait_ge(once["p_y"], 1)
            refine(link_once, st[:, 6:8], st[:, 2:4], st[:, 8:10])
            for t in range(TT):
                dve.tensor_scalar(memx[:, t, :], memx[:, t, :], st[:, 6 + t:7 + t], None, ALU.mult).then_inc(once["p_memx"], 1)
            dve.wait_ge(once["consts"], 16)
            dve.wait_ge(once["x_in"], 16)

            with dve.Fori(0, DEPTH) as L:
                links, aparts = [0], [0]

                def after(name, n):
                    dve.wait_ge(S[name], L * PER[name] + n + (name in PRIMED_ALL))

                def link(ins):
                    links[0] += 1
                    ins.then_inc(S["dve_chain"], 1)
                    after("dve_chain", links[0])

                def apart():
                    aparts[0] += 1
                    dve.memset(junk[:, aparts[0]:aparts[0] + 1], 0.0)

                def lower(n, i=0):
                    after("slab_hi", n + 1 + 6 * i)
                    dst, src, hi = w_lo[:, slot_of(n), :], raw[:, slot_of(n), :], w_hi[:, slot_of(n), :].bitcast(F32)
                    kind = SLABS[n][0] if n < N_HEAD_SLABS else ""
                    if kind == "keys":
                        dst, src, hi = (r.rearrange("p (k n) -> p k n", k=KT)[:, :, 0:K_END] for r in (dst, src, hi))
                    elif kind == "y":
                        dst, src, hi = dst[:, 0:6 * CW], src[:, 0:6 * CW], hi[:, 0:6 * CW]
                    dve.tensor_tensor(dst, src, hi, ALU.subtract).then_inc(S["slab_lo"], 1)

                def norm(n, between=lambda: None):
                    after("norm_sq", 2 * n + 2)
                    after("norm_xn", 2 * n)
                    mean_and_eps(st[:, 2:4], st[:, 0:2], D_MODEL).then_inc(S["norm_v"], 1)
                    after("norm_y", n + 1)
                    refine(link, st[:, 6:8], st[:, 2:4], st[:, 8:10])
                    for t in range(TT):
                        dve.tensor_scalar(xn[:, t, :], x[:, t, :], st[:, 6 + t:7 + t], None, ALU.mult).then_inc(S["norm_xn"], 1)
                    between()
                    for i in range(4):
                        after("norm_hi", 4 * n + i + 1)
                        for k in range(2):
                            f = 2 * i + k
                            ins = dve.scalar_tensor_tensor(h_lo[:, f, :], bank[4 + i][:, k * SEQ:(k + 1) * SEQ],
                                                           gain[:, 8 * n + f:8 * n + f + 1], h_hi[:, f, :].bitcast(F32),
                                                           ALU.mult, ALU.subtract)
                        ins.then_inc(S["norm_lo"], 1)

                def residual(n, banks, first):
                    after("slab_used", n)
                    for t in range(TT):
                        for m in range(2):
                            r = x[:, t, m * 512:(m + 1) * 512]
                            dve.tensor_tensor(r, r, bank[banks[2 * t + m]][:, :], ALU.add).then_inc(S["res"], 1)
                    after("res", first + 4)

                def rope(i):
                    n = 1 if i == 1 else 2
                    src, t = (pair(ap[:, 0:n * SEQ], n) for ap in (proj[("ixq", "kk", "dsq")[i]], tmp))
                    after("rot", i + 1)
                    after("rope", i)
                    link(dve.tensor_tensor(t, pair(bank[(4, 5, 4)[i]][:, 0:n * SEQ], n), over(K["sin"], n), ALU.mult))
                    link(dve.tensor_tensor(src, src, over(K["cos"], n), ALU.mult))
                    dve.tensor_tensor(src, src, t, ALU.add).then_inc(S["rope"], 1)

                def index():
                    after("evac", EVAC["misc"])
                    for n, (t, half) in enumerate(((1, 0), (1, 1), (0, 0), (0, 1))):
                        after("idx_relu", n + 1)
                        nk = (t + 1) * P
                        for hh in range(2):
                            h = 2 * hh + half
                            before = K[f"adm{t}"] if half == 0 and hh == 0 else score[t]
                            ins = dve.scalar_tensor_tensor(score[t], relu[t][half][:, hh * nk:(hh + 1) * nk],
                                                           wi[:, t, h:h + 1], before, ALU.mult, ALU.add)
                            if (n, hh) != (3, 1):
                                link(ins)
                    ins.then_inc(S["scored"], 1)
                    after("scored", 1)

                def topk(t):
                    for _ in range(TOPK // 8):
                        apart()
                        link(dve.max(m8[:, t, :], score[t]))
                        apart()
                        link(dve.match_replace(score[t], m8[:, t, :], score[t], TAKEN))
                    link(dve.tensor_scalar(bias[t], score[t], TAKEN, NEG, ALU.not_equal, ALU.mult))

                def memsplit():
                    for k in range(KT):
                        after("mem_hi", k + 1)
                        dve.scalar_tensor_tensor(s_lo[:, k, :], xk[:, k, :], gain[:, 24 + k:25 + k], s_hi[:, k, :].bitcast(F32),
                                                 ALU.mult, ALU.subtract).then_inc(S["mem_lo"], 1)

                def diagonal(ap):
                    return ap.rearrange("p (a b) -> p a b", b=P)[:, 0:3:2, :]

                def sb_keep(h):
                    soft, keep, beta = sbuf3[h % 2]
                    z = bank[4 + h % 2][:, 0:384]
                    after("sb_ln", h + 1)
                    link(dve.scalar_tensor_tensor(beta, z, 0.0, soft, ALU.min, ALU.subtract))
                    link(dve.tensor_tensor(keep, beta, z, ALU.subtract))
                    dve.tensor_tensor(diagonal(keep), diagonal(keep), over(K["valid"], 2), ALU.mult).then_inc(S["sb_keep"], 1)

                def sb_arg(h):
                    beta = sbuf3[h % 2][2]
                    after("sb_btw", h + 1)
                    dve.tensor_tensor(beta, beta, bank[6][:, 0:384], ALU.add).then_inc(S["sb_arg"], 1)

                def sb_w(h):
                    w = diagonal(sbuf3[h % 2][0])
                    after("sb_exp", h + 1)
                    dve.tensor_tensor(w, w, over(K["valid"], 2), ALU.mult).then_inc(S["sb_w"], 1)

                def branch_lo(br, order):
                    after("y_hi", order)
                    dve.tensor_tensor(y_lo[:, br, :, :], pair(bank[7][:, :]), y_hi[:, br, :, :].bitcast(F32),
                                      ALU.subtract).then_inc(S["y_lo"], 1)

                def gl_gate():
                    after("gl_gate", 1)
                    dve.tensor_scalar(lx, bank[5][:, 0:SEQ], gain[:, 32:33], None, ALU.add).then_inc(S["gl_x"], 1)

                def gl_cum():
                    after("gl_ln", 1)
                    link(dve.scalar_tensor_tensor(la, lx, 0.0, la, ALU.min, ALU.subtract))
                    dve.wait_ge(once["ones"], 2)
                    link(dve.tensor_tensor_scan(cum, ones[:, :], la, 0.0, ALU.mult, ALU.add))

                def difference(i):
                    s = 1 << i
                    if i >= 2:
                        after("gl_qk", i - 1)
                    after("sb_pv", min(i + 3, 4))
                    b = cum.rearrange("p (n w) -> p n w", w=2 * s)
                    dve.tensor_tensor(dec[i % 2].rearrange("p (n w) -> p n w", w=2 * s), b,
                                      b[:, :, s - 1:s].to_broadcast([P, SEQ // (2 * s), 2 * s]),
                                      ALU.subtract).then_inc(S["gl_dif"], 1)

                def level(i):
                    q, k = proj["glqk"][:, 0:SEQ], proj["glqk"][:, SEQ:2 * SEQ]
                    after("zeroed", 1)
                    if i >= 2:
                        after("gl_lev", LEVEL_COUNT[i - 1])
                    if i < 8:
                        after("gl_dec", i + 1)
                        dve.tensor_tensor(ke[i % 2], k, dec[i % 2], ALU.mult)
                    for h in range(HEADS):
                        r = slice(32 * h, 32 * h + 32)
                        if i < 8:
                            ins = dve.tensor_tensor(qe[i % 2][r, h, :], q[r, :], dec[i % 2][r, :], ALU.mult)
                        else:
                            ins = dve.tensor_copy(qe[i % 2][r, h, :], q[r, :])
                    ins.then_inc(S["gl_qk"], 1)

                def apply(i):
                    for t in ((1,) if i == 7 else (0, 1)):
                        b = pair(bank[4 + 2 * (i % 2) + t][:, :], 4)
                        after("gl_lev", LEVEL_COUNT[i] + (t + 1 if i != 7 else 1))
                        if i:
                            after("gl_app", LEVEL_COUNT[i])
                        if i == 7:
                            ins = dve.tensor_copy(pair(attx, 4), b)
                        elif i == 0:
                            ins = dve.tensor_tensor(pair(att[t], 4), b, over(K["lev0"], 4), ALU.mult)
                        else:
                            mask = K["ident"] if i == 8 else K[f"lev{i}"]
                            apart()
                            ins = dve.copy_predicated(pair(att[t], 4), over(mask.bitcast(I32), 4), b)
                        ins.then_inc(S["gl_app"], 1)

                def gl_silu():
                    g = proj["glo"]
                    after("evac", EVAC["glo"])
                    after("gate_w", 32)
                    link(dve.tensor_scalar(tmp[:, :], tmp[:, :], 1.0, None, ALU.add))
                    link(dve.reciprocal(tmp[:, :], tmp[:, :]))
                    link(dve.tensor_tensor(g[:, :], g[:, :], tmp[:, :], ALU.mult))
                    dve.tensor_tensor(pair(g[:, :], 8), pair(g[:, :], 8), over(norm_g[:, :], 8), ALU.mult).then_inc(S["gl_silu"], 1)

                def gl_var():
                    after("gl_sq", 1)
                    link(dve.tensor_reduce(st[:, 10:18], pair(tmp[:, :], 8), AX_X, ALU.add))
                    mean_and_eps(st[:, 18:26], st[:, 10:18], HEAD_DIM).then_inc(S["gl_v"], 1)

                def gl_o():
                    after("gl_y", 1)
                    after("gl_silu", 1)
                    refine(link, st[:, 26:34], st[:, 18:26], st[:, 34:42])
                    link(dve.tensor_tensor(pair(tmp[:, :], 8), pair(bank[6][:, :], 8), spread(st[:, 26:34], HEAD_DIM), ALU.mult))
                    dve.tensor_tensor(tmp[:, :], tmp[:, :], proj["glo"][:, :], ALU.mult).then_inc(S["gl_o"], 1)

                def ds_max():
                    for n, (t, half) in enumerate(((1, 0), (1, 1), (0, 0), (0, 1))):
                        after("ds_s", n + 1)
                        nk = (t + 1) * P
                        if n == 0:
                            after("gl_pv", 1)
                        dve.scalar_tensor_tensor(pair(dprob[t][:, half * 2 * nk:(half + 1) * 2 * nk]),
                                                 pair(bank[4 + 2 * t + half][:, 0:2 * nk]), HEAD_DIM ** -0.5,
                                                 over(bias[t], 2), ALU.mult, ALU.add).then_inc(S["ds_p"], 1)
                    for n, t in enumerate((1, 0)):
                        after("ds_p", 2 * n + 2)
                        dve.tensor_reduce(st[:, 42 + 4 * n:46 + 4 * n], pair(dprob[t], 4), AX_X, ALU.max,
                                          negate=True).then_inc(S["ds_max"], 1)

                def ds_norm():
                    for n, t in enumerate((1, 0)):
                        sums = st[:, 50 + 4 * n:54 + 4 * n]
                        after("ds_exp", n + 1)
                        link(dve.reciprocal(sums, sums))
                        dve.tensor_tensor(pair(dprob[t], 4), pair(dprob[t], 4), spread(sums, (t + 1) * P), ALU.mult).then_inc(S["ds_norm"], 1)

                def merge(n):
                    j = SLABS[n][1]
                    after("slab_used", n + 1)
                    after("evac", EVAC[("gate", (j, 2))])
                    if j == 0:
                        after("gl_pv", 1)
                    if j:
                        after("merged_lo", j)
                    for br in range(3):
                        dst = part if br else acc
                        dve.tensor_tensor(dst, sig[j % 2][br], bank[BANKS[n][br]][:, :], ALU.mult).then_inc(S["merged_mul"], 1)
                        after("merged_mul", 3 * j + br + 1)
                        if br == 1:
                            link(dve.tensor_tensor(acc, acc, part, ALU.add))
                        if br == 2:
                            dve.tensor_tensor(acc, acc, part, ALU.add).then_inc(S["merged"], 1)

                def merge_lo(n):
                    j = SLABS[n][1]
                    after("merged_hi", j + 1)
                    dve.tensor_tensor(s_lo[:, 2 * j:2 * j + 2, :], pair(acc), s_hi[:, 2 * j:2 * j + 2, :].bitcast(F32),
                                      ALU.subtract).then_inc(S["merged_lo"], 1)

                def cross():
                    def maximum(i):
                        m = st[:, 42 + 2 * i:44 + 2 * i]
                        after("xs", i + 1)
                        link(dve.tensor_reduce(m, pair(bank[4 + i][:, :]), AX_X, ALU.max, negate=True))
                        dve.tensor_scalar(m, m, X_DIM ** -0.5, None, ALU.mult).then_inc(S["x_max"], 1)

                    def normalise(i):
                        sums = st[:, 50 + 2 * i:52 + 2 * i]
                        after("x_exp", i + 1)
                        link(dve.reciprocal(sums, sums))
                        dve.tensor_tensor(pair(xprob[i]), pair(xprob[i]), spread(sums, SEQ), ALU.mult).then_inc(S["x_norm"], 1)

                    maximum(0)
                    for i in range(1, 4):
                        maximum(i)
                        normalise(i - 1)
                    normalise(3)
                    for h in range(HEADS):
                        after("o_hi", h + 1)
                        dve.tensor_tensor(s_lo[:, 2 * h:2 * h + 2, :], pair(bank[4 + h][:, :]),
                                          s_hi[:, 2 * h:2 * h + 2, :].bitcast(F32), ALU.subtract).then_inc(S["o_lo"], 1)

                steps = {"index": index, "topk0": lambda: topk(0), "topk1": lambda: topk(1), "memsplit": memsplit,
                         "gl_gate": gl_gate, "gl_cum": gl_cum, "gl_silu": gl_silu, "gl_var": gl_var, "gl_o": gl_o,
                         "ds_max": ds_max, "ds_norm": ds_norm,
                         "sb_out": lambda: branch_lo(0, 1), "gl_out": lambda: branch_lo(2, 2), "ds_out": lambda: branch_lo(1, 3)}
                for i in range(3):
                    steps[f"rope{i}"] = lambda i=i: rope(i)
                for h in range(HEADS):
                    for name, f in (("sb_keep", sb_keep), ("sb_arg", sb_arg), ("sb_w", sb_w)):
                        steps[f"{name}{h}"] = lambda h=h, f=f: f(h)
                for i in range(9):
                    steps[f"dif{i}"] = lambda i=i: difference(i)
                    steps[f"lev{i}"] = lambda i=i: level(i)
                    steps[f"app{i}"] = lambda i=i: apply(i)

                norm(0, lambda: lower(0))
                lower(1)
                for n in range(N_HEAD_SLABS):
                    late = SLABS[n] in (("xq", 0), ("xo", 0))
                    if not late:
                        lower(n + 2)
                    if n and SLABS[n - 1][0] == "y":
                        merge(n - 1)
                        merge_lo(n - 1)
                    if SLABS[n] == ("xq", 0):
                        residual(n, BANKS[n - 1], 0)
                        norm(1)
                    if SLABS[n] == ("xo", 0):
                        cross()
                    if late:
                        lower(n + 2)
                    for s in PLAN.get(n, ()):
                        if s in steps:
                            steps[s]()
                residual(N_HEAD_SLABS, BANKS[N_HEAD_SLABS - 1], 4)
                norm(2)

                def multiply(p, i):
                    after("ffn_silu", p + 1 + 2 * i)
                    dve.tensor_tensor(actf[p % 2], silu[p % 2], bank[1 + 2 * (p % 2)][:, :], ALU.mult).then_inc(S["ffn_mul"], 1)

                def act_lo(p, i):
                    after("ffn_hi", p + 1 + 2 * i)
                    o = 2 * (p % 2)
                    dve.tensor_tensor(s_lo[:, o:o + 2, :], pair(actf[p % 2]), s_hi[:, o:o + 2, :].bitcast(F32),
                                      ALU.subtract).then_inc(S["ffn_lo"], 1)

                def ffn(kind, j, i):
                    n = N_HEAD_SLABS + ffn_index(kind, j)
                    if kind == "gate" and j:
                        multiply(j - 1, i)
                    if kind == "up" and j:
                        act_lo(j - 1, i)
                    if n + 2 < N_SLABS:
                        lower(n + 2, i)
                    if kind == "out" and j == N_PAIRS - 2:
                        multiply(N_PAIRS - 1, 0)
                        act_lo(N_PAIRS - 1, 0)

                ffn_walk(dve, ffn)
                residual(N_SLABS, (4, 5, 6, 7), 8)
                assert links[0] == PER["dve_chain"], links[0]

            dve.wait_ge(once["f_sq"], 2)
            mean_and_eps(st[:, 2:4], st[:, 0:2], D_MODEL).then_inc(once["f_v"], 1)
            dve.wait_ge(once["f_y"], 1)
            refine(link_once, st[:, 6:8], st[:, 2:4], st[:, 8:10])
            dve.wait_ge(once["f_g"], 16)
            for t in range(TT):
                dve.scalar_tensor_tensor(xn[:, t, :], x[:, t, :], st[:, 6 + t:7 + t],
                                         xk[:, 0:4, :].rearrange("p a b -> p (a b)"), ALU.mult, ALU.mult).then_inc(once["f_out"], 1)


_INS = ("x", "mem", "mix_norm_g", "w_in", "gla_w_up", "gla_b", "gla_norm_g", "w_br_a", "w_br_b", "w_br_c",
        "w_mix_out", "xattn_norm_g", "mem_norm_g", "w_xq", "w_xkv", "w_xo", "ffn_norm_g", "w_ffn_in",
        "w_ffn_out", "final_norm_g")


def kernel(**inputs):
    import concourse.bacc as bacc
    from concourse.bass_utils import run_bass_kernel_spmd

    nc = bacc.Bacc("TRN2", target_bir_lowering=False, num_devices=1)
    arrays, args = {}, {}
    for name in _INS:
        v = np.ascontiguousarray(inputs[name])
        arrays[f"in_{name}"] = v
        args[name] = nc.dram_tensor(f"in_{name}", v.shape, mybir.dt.from_np(v.dtype), kind="ExternalInput").ap()
    arrays["shape_constants"] = CONST_ARRAY
    args["shape_constants"] = nc.dram_tensor("shape_constants", CONST_ARRAY.shape, F32, kind="ExternalInput").ap()
    out = nc.dram_tensor("out", (1, SEQ, D_MODEL), F32, kind="ExternalOutput").ap()
    program(nc, args, out)
    return run_bass_kernel_spmd(nc, [arrays], core_ids=[0]).results[0]["out"]
```

```python
from contextlib import ExitStack

import concourse.bass as bass
import numpy as np
from concourse import mybir

F32 = mybir.dt.float32
F32R = mybir.dt.float32r
I32 = mybir.dt.int32
ALU = mybir.AluOpType
ACT = mybir.ActivationFunctionType
AX_X = mybir.AxisListType.X

P = 128
D_MODEL = 1024
SEQ = 256
DEPTH = 2
N_MEM = 256
KT = D_MODEL // P
TT = SEQ // P
D_FF = 2816
HEADS = 4
HEAD_DIM = 64
GLA_DK = 32
GLA_RANK = 16
GLA_TAU = 16.0
IDX_HEADS = 4
TOPK = 64
CHUNK = 64
X_DIM = D_MODEL // HEADS
EPS = 1e-6
ROPE_THETA = 10000.0
CW = 256
NEG = -3.0e38
TAKEN = -3.4e38

C_SBQ, C_SBK, C_SBV, C_DSQ, C_DSK, C_DSV = 0, 256, 512, 768, 1024, 1088
C_IXQ, C_IXK, C_IXW, C_GLQ, C_GLV, C_GLG, C_GLO, C_GATE = 1152, 1408, 1472, 1476, 1732, 1988, 2004, 2260
IN_WIDTH = C_GATE + 3 * D_MODEL

SLABS = [("ixq", 0), ("keys", 0), ("sbk", 0), ("sbq", 0), ("dsq", 0), ("sbv", 0),
         ("glqk", 0), ("glv", 0), ("glo", 0)]
SLABS += [("xk", j) for j in range(4)] + [("gate", (j, b)) for j in range(2) for b in range(3)] + [("xv", 0), ("xv", 1)]
SLABS += [("gate", (j, b)) for j in range(2, 4) for b in range(3)]
SLABS += [("y", 0), ("y", 1), ("mix", 0), ("y", 2), ("mix", 1), ("y", 3), ("mix", 2), ("mix", 3), ("xv", 2), ("xv", 3)]
SLABS += [("xq", j) for j in range(4)] + [("xo", j) for j in range(4)]
N_HEAD_SLABS = len(SLABS)
N_PAIRS = D_FF // CW
N_SLABS = N_HEAD_SLABS + 3 * N_PAIRS
AT = {s: i for i, s in enumerate(SLABS)}
RING = 3
K_IX, K_DS, K_V, K_W, K_G, K_END = 0, 64, 128, 192, 196, 212

PLAN = {
    0: ["mem_sq"],
    1: ["rot0", "mem_root"],
    2: ["rot1", "rope0", "rope1", "mem_tr", "mem_split"],
    3: ["swap", "swapped"],
    4: ["index"],
    5: ["rot2", "sb_z0", "sb_z1", "sb_ln0", "rope2"],
    6: ["topk1a", "lower", "sb_keep0", "sb_keep1"],
    7: ["sb_btw0", "sb_z2", "sb_arg0", "sb_exp0"],
    8: ["sb_btw1", "sb_z3", "sb_w0", "sb_arg1", "sb_exp1", "sb_ln1"],
    9: ["sb_w1", "topk1b", "lower", "sb_pv0", "sb_pv1"],
    10: ["gl_silu", "lower", "sb_keep2", "sb_keep3"],
    11: ["sb_btw2", "gl_gate", "gl_ln", "sb_arg2", "sb_exp2"],
    12: ["gl_cum", "sb_w2", "sb_pv2", "sb_btw3", "sb_arg3", "sb_exp3"],
    13: ["sb_w3", "sb_pv3", "dif0", "dec0"],
    14: ["sb_out", "dif1", "dec1", "lev0", "topk0a"],
    15: ["lev1", "dif2", "dec2", "dif3", "dec3", "app0"],
    16: ["lev2", "app1", "lev3", "dif4", "dec4"],
    17: ["app2", "lev4", "app3", "dif5", "dec5"],
    18: ["lev5", "app4", "dif6", "dec6", "lev6", "app5", "dif7", "dec7"],
    19: ["lev7", "app6", "lev8", "app7"],
    20: ["app8", "topk0b", "gl_pv", "gl_var", "gl_root"],
    21: ["ds_s", "gl_o", "ds_max", "ds_exp"],
    22: ["gl_otr", "gl_out", "ds_norm", "ds_tr", "ds_pv", "ds_out"],
}

EVAC = {}
for _kind, _idx in SLABS:
    for _part in {"y": (), "mix": (), "xo": (), "keys": ("kk", "misc")}.get(_kind, (_kind,)):
        EVAC[(_part, _idx)] = EVAC[_part] = len({k for k in EVAC if isinstance(k, tuple)}) + 1
LEVEL_COUNT = [0, 2, 4, 6, 8, 10, 12, 14, 15, 17]
Y_ORDER = {"a": 1, "c": 2, "b": 3}


def bank_plan():
    at, out = 0, []
    for kind, _ in SLABS:
        if kind == "mix":
            out.append([4, 5, 6, 7])
            continue
        n = {"y": 3, "xo": 4, "keys": 2}.get(kind, 1)
        if n == 4:
            at = 0
        out.append([(at + i) % 4 for i in range(n)])
        at = (at + n) % 4
    return out


BANKS = bank_plan()


def slab_pieces(kind, idx):
    if kind == "keys":
        return [(C_IXK, K_IX, 64), (C_DSK, K_DS, 128), (C_IXW, K_W, 4), (C_GLG, K_G, 16)]
    start = {"ixq": C_IXQ, "sbq": C_SBQ, "sbk": C_SBK, "dsq": C_DSQ, "sbv": C_SBV, "glqk": C_GLQ,
             "glv": C_GLV, "glo": C_GLO}
    if kind in start:
        return [(start[kind], 0, CW)]
    return None


def n_dmas(kind):
    return {"keys": 4, "y": 3}.get(kind, 1)


def landed_plan():
    counts, out = [0] * RING, []
    for n in range(N_SLABS):
        counts[n % RING] += n_dmas(SLABS[n][0]) if n < N_HEAD_SLABS else 1
        out.append(counts[n % RING])
    return out, counts


LANDED, LANDED_TOTAL = landed_plan()

CONST = {}


def constants():
    parts = []

    def put(name, a):
        CONST[name] = (sum(p.shape[1] for p in parts), a.shape[1])
        parts.append(a.astype(np.float32))

    r, c = np.arange(P)[:, None], np.arange(P)[None, :]
    put("ident", r == c)
    lower = (c % HEAD_DIM) < HEAD_DIM // 2
    put("rot", np.where(lower & (r == c + 32), -1.0, 0.0) + np.where(~lower & (r == c - 32), 1.0, 0.0))
    put("later", r > c)
    put("valid", r < c)
    q, k = np.arange(SEQ)[:, None], np.arange(SEQ)[None, :]
    adm = np.where(k // CHUNK <= q // CHUNK, 0.0, NEG)
    put("adm0", adm[:P, :P])
    put("adm1", adm[P:, :])
    inv = np.float32(1.0) / np.float32(ROPE_THETA) ** (np.arange(32, dtype=np.float32) * np.float32(2.0 / HEAD_DIM))
    ang = (np.arange(SEQ, dtype=np.float32)[None, :] * inv[:, None]).astype(np.float32)
    put("cos", np.tile(np.cos(ang), (4, 1)))
    put("sin", np.tile(np.sin(ang), (4, 1)))
    for lev in range(7):
        s = 1 << lev
        put(f"lev{lev}", (r // (2 * s) == c // (2 * s)) & (r % (2 * s) < s) & (c % (2 * s) >= s))
    return np.concatenate(parts, axis=1)


CONST_ARRAY = constants()

PER = dict(
    slab_hi=N_SLABS, slab_lo=N_SLABS, slab_used=N_SLABS,
    gain_rows=5 * 16, gain_t=1, gain=1, gate_w=2 * 16, mem_in=16,
    mem_sq=2, mem_v=1, mem_ln=1, mem_y=1, mem_x=2, mem_tr=4,
    norm_sq=6, norm_v=3, norm_ln=3, norm_y=3, norm_xn=6, norm_tr=12, norm_hi=12, norm_lo=12,
    evac=34, merged_mul=12, merged=4, merged_hi=4, merged_lo=4, res=12,
    rot=3, rope=3, swap=1, swapped=1, idx=4, idx_relu=4, scored=1,
    sb_z=4, sb_ln=4, sb_keep=4, sb_btw=4, sb_arg=4, sb_exp=4, sb_w=4, sb_pv=4,
    gl_gate=1, gl_x=1, gl_ln=1, gl_cum=1, gl_silu=1, zeroed=1,
    gl_dif=8, gl_dec=8, gl_qk=9, gl_lev=17, gl_app=17, gl_pv=1, gl_sq=1, gl_v=1, gl_y=1, gl_o=1, gl_otr=1,
    ds_s=4, ds_p=4, ds_max=2, ds_exp=2, ds_norm=2, ds_tr=3, ds_pt=3, ds_pv=1,
    y_hi=3, y_lo=3, mem_hi=4, mem_lo=4,
    xs=4, x_max=4, x_exp=4, x_norm=4, x_tr=4, x_pt=4, x_pv=4, o_hi=4, o_lo=4,
    ffn_silu=N_PAIRS, ffn_mul=N_PAIRS, ffn_hi=N_PAIRS, ffn_lo=N_PAIRS,
    act_chain=20, dve_chain=96,
)

PRIMED = {"PE": ("slab_used", "gain_t", "xs", "gl_gate"),
          "DVE": ("slab_lo", "norm_lo", "norm_xn", "res", "rope", "gl_silu", "ffn_mul", "ffn_lo")}
PRIMED_ALL = PRIMED["PE"] + PRIMED["DVE"]


def program(nc, a, out):
    ctx = ExitStack()
    with ctx:
        def sb(name, shape, dt=F32):
            return ctx.enter_context(nc.sbuf_tensor(name, shape, dt))

        S = {n: ctx.enter_context(nc.semaphore(f"s_{n}")) for n in PER}
        landed = [ctx.enter_context(nc.semaphore(f"s_landed{i}")) for i in range(RING)]
        once = {n: ctx.enter_context(nc.semaphore(f"s_{n}")) for n in (
            "consts", "pool_junk", "x_in", "ones", "f_sq", "f_v", "f_ln", "f_y", "f_g", "f_out", "f_chain", "stored")}

        const = sb("const", [P, CONST_ARRAY.shape[1]])
        K = {n: const[:, o:o + w] for n, (o, w) in CONST.items()}
        ones = sb("ones", [P, SEQ])
        x = sb("x", [P, TT, D_MODEL])
        xn = sb("xn", [P, TT, D_MODEL])
        h_hi, h_lo = sb("h_hi", [P, KT, SEQ], F32R), sb("h_lo", [P, KT, SEQ], F32R)
        s_hi, s_lo = sb("s_hi", [P, KT, SEQ], F32R), sb("s_lo", [P, KT, SEQ], F32R)
        y_hi, y_lo = sb("y_hi", [P, 3, 2, SEQ], F32R), sb("y_lo", [P, 3, 2, SEQ], F32R)
        raw = sb("raw", [P, RING, 8 * CW])
        w_hi, w_lo = sb("w_hi", [P, RING, 8 * CW], F32R), sb("w_lo", [P, RING, 8 * CW], F32R)
        xk, xv = sb("xk", [P, KT, SEQ]), sb("xv", [P, 2, D_MODEL])
        proj = {n: sb(n, [P, 2 * SEQ]) for n in ("ixq", "kk", "dsq", "sbq", "sbk", "sbv", "glqk", "glv", "glo")}
        gg = sb("gg", [GLA_RANK, SEQ])
        dv = sb("dv", [P, TT, HEAD_DIM])
        wi = sb("wi", [P, TT, IDX_HEADS])
        gain_rows = sb("gain_rows", [P, P])
        gain = sb("gain", [P, 33])
        w_up = sb("w_up", [GLA_RANK, P])
        norm_g = sb("norm_g", [P, HEAD_DIM])
        tmp = sb("tmp", [P, 2 * SEQ])
        scr = sb("scr", [P, 6656])
        st = sb("st", [P, 64])
        junk = sb("junk", [P, 64])
        m8 = sb("m8", [P, TT, 8])
        bank = [ctx.enter_context(nc.psum_tensor(f"bank{i}", [P, 512], F32)) for i in range(8)]

        sig = [[scr[:, (3 * j + b) * 512:(3 * j + b + 1) * 512] for b in range(3)] for j in range(4)]
        score = [scr[:, 3072:3200], scr[:, 3200:3456]]
        bias = [scr[:, 3456:3584], scr[:, 3584:3840]]
        F0 = 3840
        relu = {1: [scr[:, F0:F0 + 512], scr[:, F0 + 512:F0 + 1024]],
                0: [scr[:, F0 + 1024:F0 + 1280], scr[:, F0 + 1280:F0 + 1536]]}
        dprob = {1: scr[:, F0:F0 + 1024], 0: scr[:, F0 + 1024:F0 + 1536]}
        dpt = [scr[:, F0 + 1536:F0 + 2048], scr[:, F0 + 2048:F0 + 2560], tmp[:, :]]
        sbuf3 = [[scr[:, F0 + 1152 * p + 384 * i:F0 + 1152 * p + 384 * (i + 1)] for i in range(3)] for p in range(2)]
        dec = [scr[:, F0:F0 + 256], scr[:, F0 + 256:F0 + 512]]
        ke = [scr[:, F0 + 512:F0 + 768], scr[:, F0 + 768:F0 + 1024]]
        att = [scr[:, F0 + 1024:F0 + 1536], scr[:, F0 + 1536:F0 + 2048]]
        attx = scr[:, F0 + 2048:F0 + 2560]
        cum = scr[:, F0 + 2560:F0 + 2816]
        lx, la = tmp[:, 0:SEQ], tmp[:, SEQ:2 * SEQ]
        qe = [xn[:, i, :].rearrange("p (h t) -> p h t", h=HEADS) for i in range(2)]
        gl_raw = xn[:, 0, 0:2 * SEQ]
        xq = xn[:, :, :].rearrange("p a b -> p (a b)").rearrange("p (k t) -> p k t", k=KT)
        xprob = [scr[:, 512 * i:512 * (i + 1)] for i in range(4)]
        xpt = [scr[:, 2048 + 512 * i:2560 + 512 * i] for i in range(4)]
        acc, part = scr[:, 6144:6656], tmp[:, :]
        silu = [scr[:, 0:512], scr[:, 512:1024]]
        actf = [scr[:, 1024:1536], scr[:, 1536:2048]]
        memx = xk[:, :, :].rearrange("p a b -> p (a b)").rearrange("p (t d) -> p t d", t=TT)

        def pair(ap, n=2):
            return ap.rearrange("p (a b) -> p a b", a=n)

        def over(ap, n):
            return ap.unsqueeze(1).to_broadcast([P, n, ap.shape[1]])

        def spread(ap, n):
            return ap.unsqueeze(2).to_broadcast([P, ap.shape[1], n])

        def slot_of(n):
            return n % RING

        def ffn_index(kind, j):
            if kind == "out":
                return 3 * j + 4 if j < N_PAIRS - 1 else 3 * N_PAIRS - 1
            first = 3 * j - 1 if j else 0
            return first + (kind == "up")

        PAIRS_LOOPED = N_PAIRS - 3
        assert PAIRS_LOOPED % 2 == 0

        def ffn_walk(eng, step):
            step("gate", 0, 0)
            step("up", 0, 0)
            for kind, j in (("gate", 1), ("up", 1), ("out", 0)):
                step(kind, j, 0)
            with eng.Fori(0, PAIRS_LOOPED // 2) as i:
                for d in (1, 2):
                    for kind, j in (("gate", d + 1), ("up", d + 1), ("out", d)):
                        step(kind, j, i)
            for kind, j in (("gate", N_PAIRS - 1), ("up", N_PAIRS - 1), ("out", N_PAIRS - 2), ("out", N_PAIRS - 1)):
                step(kind, j, 0)

        block = ctx.enter_context(nc.Block())

        @block.sync
        def _(sp):
            sp.dma_start(x[:, :, :], a["x"].rearrange("b (t p) d -> p (b t) d", p=P)).then_inc(once["x_in"], 16)
            sp.dma_start(const[:, :], a["shape_constants"]).then_inc(once["consts"], 16)
            sp.wait_ge(once["ones"], 2)
            with sp.Fori(0, DEPTH) as L:
                def at(name, n):
                    return L * PER[name] + n + (name in PRIMED_ALL)

                def load_slab(n, pieces, i=0):
                    if n != RING:
                        sp.wait_ge(S["slab_lo"], at("slab_lo", max(n - RING + 1, 0) + 6 * i))
                    for dst, src in pieces:
                        sp.dma_start(dst, src).then_inc(landed[slot_of(n)], 16)

                def gains():
                    sp.wait_ge(S["gain_t"], at("gain_t", 0))
                    for r, name in enumerate(("mix_norm_g", "xattn_norm_g", "ffn_norm_g", "mem_norm_g")):
                        sp.dma_start(gain_rows[8 * r:8 * r + 8, :],
                                     a[name][L].rearrange("(k p) -> k p", p=P)).then_inc(S["gain_rows"], 16)
                    sp.dma_start(gain_rows[32:33, :], a["gla_b"][L].rearrange("(a n) -> a n", a=1)).then_inc(S["gain_rows"], 16)

                def col_slab(w, c0, cols=CW):
                    return w[L].rearrange("(k p) n -> p k n", p=P)[:, :, c0:c0 + cols]

                def head_slab(n):
                    kind, idx = SLABS[n]
                    dst = raw[:, slot_of(n), :].rearrange("p (k n) -> p k n", k=KT)
                    pieces = slab_pieces(kind, idx)
                    if pieces is not None:
                        load_slab(n, [(dst[:, :, d:d + c], col_slab(a["w_in"], s, c)) for s, d, c in pieces])
                    elif kind == "gate":
                        j, b = idx
                        load_slab(n, [(dst, col_slab(a["w_in"], C_GATE + b * D_MODEL + j * CW))])
                    elif kind == "y":
                        load_slab(n, [(dst[:, 2 * b:2 * b + 2, :], col_slab(a[w], idx * CW))
                                      for b, w in enumerate(("w_br_a", "w_br_b", "w_br_c"))])
                    elif kind in ("xk", "xv"):
                        load_slab(n, [(dst, col_slab(a["w_xkv"], (kind == "xv") * D_MODEL + idx * CW))])
                    elif kind == "xq":
                        load_slab(n, [(dst, col_slab(a["w_xq"], idx * CW))])
                    else:
                        w = a["w_mix_out" if kind == "mix" else "w_xo"]
                        load_slab(n, [(raw[:, slot_of(n), :].rearrange("p (k n) -> p k n", k=2),
                                       w[L, idx * 256:idx * 256 + 256, :].rearrange("(k p) n -> p k n", p=P))])

                gains()
                head_slab(0)
                head_slab(1)
                sp.wait_ge(S["xs"], at("xs", 0))
                sp.dma_start(memx, a["mem"].rearrange("b (t p) d -> p (b t) d", p=P)).then_inc(S["mem_in"], 16)
                head_slab(2)
                sp.wait_ge(S["gl_gate"], at("gl_gate", 0))
                sp.dma_start(w_up[:, :], a["gla_w_up"][L]).then_inc(S["gate_w"], 16)
                sp.wait_ge(S["slab_lo"], at("slab_lo", 1))
                sp.wait_ge(S["gl_silu"], at("gl_silu", 0))
                sp.dma_start(norm_g[:, :], a["gla_norm_g"][L].rearrange("(a n) -> a n", a=1)
                             .to_broadcast([P, HEAD_DIM])).then_inc(S["gate_w"], 16)
                for n in range(3, N_HEAD_SLABS):
                    head_slab(n)

                def ffn_slab(kind, j, i):
                    n = N_HEAD_SLABS + ffn_index(kind, j)
                    if kind == "out":
                        src = a["w_ffn_out"][L, bass.ds(i * 2 * CW + j * CW, CW), :].rearrange("(k p) n -> p k n", p=P)
                        dst = raw[:, slot_of(n), :].rearrange("p (k n) -> p k n", k=2)
                    else:
                        c0 = (kind == "up") * D_FF + j * CW
                        src = a["w_ffn_in"][L].rearrange("(k p) n -> p k n", p=P)[:, :, bass.ds(i * 2 * CW + c0, CW)]
                        dst = raw[:, slot_of(n), :].rearrange("p (k n) -> p k n", k=KT)
                    load_slab(n, [(dst, src)], i)

                ffn_walk(sp, ffn_slab)
            sp.wait_ge(S["xs"], DEPTH * PER["xs"] + 1)
            sp.dma_start(xk[:, 0:4, :].rearrange("p a b -> p (a b)"),
                         a["final_norm_g"].rearrange("(a n) -> a n", a=1).to_broadcast([P, D_MODEL])).then_inc(once["f_g"], 16)
            sp.wait_ge(once["f_out"], 2)
            sp.dma_start(out.rearrange("b (t p) d -> p (b t) d", p=P), xn[:, :, :]).then_inc(once["stored"], 16)
            sp.wait_ge(once["stored"], 16)

        @block.gpsimd
        def _(pool):
            pool.memset(ones[:, :], 1.0).then_inc(once["ones"], 1)
            pool.memset(gain_rows[:, :], 0.0).then_inc(once["ones"], 1)
            pool.wait_ge(once["ones"], 2)
            with pool.Fori(0, DEPTH) as L:
                pool.wait_ge(S["mem_sq"], L * PER["mem_sq"] + 2)
                pool.tensor_tensor(junk[:, 0:1], ones[:, 0:1], ones[:, 0:1], ALU.add).then_inc(once["pool_junk"], 1)
                pool.memset(xn[:, :, :], 0.0).then_inc(S["zeroed"], 1)

        @block.tensor
        def _(pe):
            for name in PRIMED["PE"]:
                pe.sem_inc(S[name], 1)
            pe.wait_ge(once["consts"], 16)
            with pe.Fori(0, DEPTH) as L:
                def at(name, n):
                    return L * PER[name] + n + (name in PRIMED_ALL)

                reader = {b: ("ffn_mul", 0) for b in range(4)}
                reader.update({b: ("res", 0) for b in range(4, 8)})

                def take(b, name, n):
                    pe.wait_ge(S[reader[b][0]], at(*reader[b]))
                    reader[b] = (name, n)

                def three(dst, st_hi, st_lo, mv_hi, mv_lo, first, last):
                    pe.matmul(dst, st_hi, mv_hi, start=first, stop=False, skip_group_check=True)
                    pe.matmul(dst, st_hi, mv_lo, start=False, stop=False, skip_group_check=True)
                    return pe.matmul(dst, st_lo, mv_hi, start=False, stop=last, skip_group_check=True)

                def feature_major(dst, n, width, c0, cols, act_hi, act_lo, norm=None):
                    for k, (ah, al) in enumerate(zip(act_hi, act_lo)):
                        if norm is not None and k % 2 == 0:
                            pe.wait_ge(S["norm_lo"], at("norm_lo", 4 * norm + k // 2 + 1))
                        o = k * width + c0
                        wh, wl = w_hi[:, slot_of(n), o:o + cols], w_lo[:, slot_of(n), o:o + cols]
                        mm = three(dst, wh, wl, ah, al, k == 0, k == len(act_hi) - 1)
                    return mm

                def token_major(dst, n, c0, cols, t, a_hi, a_lo):
                    for k in range(KT):
                        o = k * CW + c0
                        mm = three(dst, a_hi[:, k, t * P:(t + 1) * P], a_lo[:, k, t * P:(t + 1) * P],
                                   w_hi[:, slot_of(n), o:o + cols], w_lo[:, slot_of(n), o:o + cols], k == 0, k == KT - 1)
                    return mm

                def row_slab(n, banks, k_hi, k_lo, first, last):
                    wh = w_hi[:, slot_of(n), :].rearrange("p (k n) -> p k n", k=2)
                    wl = w_lo[:, slot_of(n), :].rearrange("p (k n) -> p k n", k=2)
                    for k in range(2):
                        for t in range(TT):
                            ah, al = k_hi[:, k, t * P:(t + 1) * P], k_lo[:, k, t * P:(t + 1) * P]
                            for st_, w, begin, end in ((ah, wh, first and k == 0, False), (ah, wl, False, False),
                                                       (al, wh, False, last and k == 1)):
                                for m in range(2):
                                    mm = pe.matmul(bank[banks[2 * t + m]][:, :], st_, w[:, k, m * 512:(m + 1) * 512],
                                                   start=begin, stop=end, skip_group_check=True)
                    return mm

                def to_features(src, signal, freed, n):
                    for i in range(4):
                        take(4 + i, freed, n + i + 1)
                        for kk in range(2):
                            for t in range(TT):
                                mm = pe.transpose(bank[4 + i][:, kk * SEQ + t * P:kk * SEQ + (t + 1) * P],
                                                  src[:, t, (2 * i + kk) * P:(2 * i + kk + 1) * P], K["ident"])
                        mm.then_inc(S[signal], 1)

                def norm(n):
                    pe.wait_ge(S["norm_xn"], at("norm_xn", 2 * n + 2))
                    to_features(xn, "norm_tr", "norm_lo", 4 * n)

                def mem_tr():
                    pe.wait_ge(S["mem_x"], at("mem_x", 2))
                    to_features(memx, "mem_tr", "mem_lo", 0)

                def rot(i):
                    src = proj[("ixq", "kk", "dsq")[i]]
                    pe.wait_ge(S["evac"], at("evac", (1, 2, EVAC["dsq"])[i]))
                    b = (4, 5, 7)[i]
                    take(b, "rope", i + 1)
                    w = SEQ if i == 1 else 2 * SEQ
                    pe.matmul(bank[b][:, 0:w], K["rot"], src[:, 0:w], start=True, stop=True).then_inc(S["rot"], 1)

                def swap():
                    pe.wait_ge(S["rope"], at("rope", 2))
                    take(5, "swapped", 1)
                    for half in range(2):
                        mm = pe.matmul(bank[5][64 * half:64 * half + 64, 0:SEQ], K["ident"][:, 64 - 64 * half:P - 64 * half],
                                       proj["kk"][:, 0:SEQ], start=True, stop=True)
                    mm.then_inc(S["swap"], 1)

                def head_scores(q, kt, signal, freed):
                    for n, (t, half) in enumerate(((1, 0), (1, 1), (0, 0), (0, 1))):
                        b, nk = (4 + 2 * t + half), (t + 1) * P
                        take(b, freed, n + 1)
                        r = slice(64 * half, 64 * half + 64)
                        for hh in range(2):
                            mm = pe.matmul(bank[b][:, hh * nk:(hh + 1) * nk],
                                           q[r, hh * SEQ + t * P:hh * SEQ + (t + 1) * P],
                                           proj["kk"][r, (kt ^ half) * SEQ:(kt ^ half) * SEQ + nk], start=True, stop=True)
                        mm.then_inc(S[signal], 1)

                def index():
                    pe.wait_ge(S["swapped"], at("swapped", 1))
                    head_scores(proj["ixq"], 0, "idx", "idx_relu")

                def ds_s():
                    pe.wait_ge(S["rope"], at("rope", 3))
                    head_scores(proj["dsq"], 1, "ds_s", "ds_p")

                def sb_z(h):
                    pe.wait_ge(S["evac"], at("evac", EVAC["sbq"]))
                    b, r, o = 4 + h % 2, slice(64 * (h % 2), 64 * (h % 2) + 64), (h // 2) * SEQ
                    take(b, "sb_keep", h + 1)
                    pe.matmul(bank[b][:, 0:SEQ], proj["sbk"][r, o:o + P], proj["sbq"][r, o:o + SEQ], start=True, stop=True)
                    pe.matmul(bank[b][:, SEQ:SEQ + P], proj["sbk"][r, o + P:o + SEQ], proj["sbq"][r, o + P:o + SEQ],
                              start=True, stop=True).then_inc(S["sb_z"], 1)

                def sb_btw(h):
                    keep = sbuf3[h % 2][1]
                    pe.wait_ge(S["sb_keep"], at("sb_keep", h + 1))
                    take(6, "sb_arg", h + 1)
                    pe.matmul(bank[6][:, 0:384], K["later"], keep, start=True, stop=False, skip_group_check=True)
                    pe.matmul(bank[6][:, P:2 * P], ones[:, 0:P], keep[:, 256:384], start=False, stop=True,
                              skip_group_check=True).then_inc(S["sb_btw"], 1)

                def sb_pv(h):
                    w = sbuf3[h % 2][0]
                    pe.wait_ge(S["sb_w"], at("sb_w", h + 1))
                    if h == 0:
                        pe.wait_ge(S["evac"], at("evac", EVAC["sbv"]))
                        take(7, "y_lo", 1)
                    o = bank[7][64 * (h % 2):64 * (h % 2) + 64, (h // 2) * SEQ:(h // 2 + 1) * SEQ]
                    v = pair(proj["sbv"][:, :])
                    pe.matmul(o, v[:, 0, h * 64:h * 64 + 64], w[:, 0:SEQ], start=True, stop=False, skip_group_check=True)
                    pe.matmul(o[:, P:SEQ], v[:, 1, h * 64:h * 64 + 64], w[:, SEQ:384], start=False, stop=True,
                              skip_group_check=True).then_inc(S["sb_pv"], 1)

                def gl_gate():
                    pe.wait_ge(S["evac"], at("evac", EVAC["misc"]))
                    pe.wait_ge(S["gate_w"], at("gate_w", 32))
                    take(5, "gl_x", 1)
                    pe.matmul(bank[5][:, 0:SEQ], w_up[:, :], gg[:, :], start=True, stop=True).then_inc(S["gl_gate"], 1)

                def level(i):
                    pe.wait_ge(S["gl_qk"], at("gl_qk", i + 1))
                    k = proj["glqk"][:, SEQ:2 * SEQ] if i == 8 else ke[i % 2]
                    for t in ((1,) if i == 7 else (0, 1)):
                        b = 4 + 2 * (i % 2) + t
                        n = LEVEL_COUNT[i] + t + 1 if i != 7 else LEVEL_COUNT[i] + 1
                        take(b, "gl_app", n)
                        kt = 0 if i == 7 else t
                        pe.matmul(pair(bank[b][:, :], 4), k[:, kt * P:(kt + 1) * P], qe[i % 2][:, :, t * P:(t + 1) * P],
                                  start=True, stop=True).then_inc(S["gl_lev"], 1)

                def gl_pv():
                    pe.wait_ge(S["gl_app"], at("gl_app", LEVEL_COUNT[9]))
                    pe.wait_ge(S["evac"], at("evac", EVAC["glv"]))
                    take(6, "gl_sq", 1)
                    v = pair(proj["glv"][:, :])
                    for t in range(TT):
                        for h in range(HEADS):
                            o = bank[6][:, t * 256 + h * 64:t * 256 + (h + 1) * 64]
                            c = slice(h * 64, (h + 1) * 64)
                            mm = pe.matmul(o, att[t][:, h * P:(h + 1) * P], v[:, t, c], start=True, stop=(t == 0),
                                           skip_group_check=True)
                            if t == 1:
                                mm = pe.matmul(o, attx[:, h * P:(h + 1) * P], v[:, 0, c], start=False, stop=True,
                                               skip_group_check=True)
                    mm.then_inc(S["gl_pv"], 1)

                def gl_otr():
                    pe.wait_ge(S["gl_o"], at("gl_o", 1))
                    take(7, "y_lo", Y_ORDER["c"])
                    for k in range(2):
                        for t in range(TT):
                            mm = pe.transpose(bank[7][:, k * SEQ + t * P:k * SEQ + (t + 1) * P],
                                              tmp[:, t * SEQ + k * P:t * SEQ + (k + 1) * P], K["ident"])
                    mm.then_inc(S["gl_otr"], 1)

                def ds_tr():
                    p1, p0 = pair(dprob[1], 4), pair(dprob[0], 4)
                    pe.wait_ge(S["ds_norm"], at("ds_norm", 2))
                    for g in range(2):
                        take(4 + g, "ds_pt", g + 1)
                        for s in range(2):
                            pe.transpose(bank[4 + g][:, s * SEQ:s * SEQ + P], p0[:, 2 * g + s, :], K["ident"])
                            mm = pe.transpose(bank[4 + g][:, s * SEQ + P:(s + 1) * SEQ], p1[:, 2 * g + s, 0:P], K["ident"])
                        mm.then_inc(S["ds_tr"], 1)
                    take(6, "ds_pt", 3)
                    for s in range(4):
                        mm = pe.transpose(bank[6][:, s * P:(s + 1) * P], p1[:, s, P:SEQ], K["ident"])
                    mm.then_inc(S["ds_tr"], 1)

                def ds_pv():
                    pe.wait_ge(S["ds_pt"], at("ds_pt", 3))
                    take(7, "y_lo", Y_ORDER["b"])
                    for s in range(4):
                        h = 2 * (s % 2) + s // 2
                        o = bank[7][64 * (h % 2):64 * (h % 2) + 64, (h // 2) * SEQ:(h // 2 + 1) * SEQ]
                        pe.matmul(o, dv[:, 0, :], dpt[s // 2][:, (s % 2) * SEQ:(s % 2 + 1) * SEQ], start=True, stop=False,
                                  skip_group_check=True)
                        mm = pe.matmul(o[:, P:SEQ], dv[:, 1, :], dpt[2][:, s * P:(s + 1) * P], start=False, stop=True,
                                       skip_group_check=True)
                    mm.then_inc(S["ds_pv"], 1)

                def cross():
                    pe.wait_ge(S["evac"], at("evac", EVAC[("xq", 3)]))
                    for i in range(4):
                        t = i % 2
                        take(4 + i, "x_exp", i + 1)
                        for s in range(2):
                            h = 2 * (i // 2) + s
                            for k in range(2):
                                mm = pe.matmul(bank[4 + i][:, s * SEQ:(s + 1) * SEQ], xq[:, 2 * h + k, t * P:(t + 1) * P],
                                               xk[:, 2 * h + k, :], start=(k == 0), stop=(k == 1), skip_group_check=True)
                        mm.then_inc(S["xs"], 1)
                    for i in range(4):
                        m = i % 2
                        pe.wait_ge(S["x_norm"], at("x_norm", 2 * (i // 2) + 2))
                        take(4 + i, "x_pt", i + 1)
                        for s in range(2):
                            for t in range(TT):
                                src = pair(xprob[2 * (i // 2) + t])[:, s, m * P:(m + 1) * P]
                                mm = pe.transpose(bank[4 + i][:, s * SEQ + t * P:s * SEQ + (t + 1) * P], src, K["ident"])
                        mm.then_inc(S["x_tr"], 1)
                    for h in range(HEADS):
                        pe.wait_ge(S["x_pt"], at("x_pt", 2 * (h // 2) + 2))
                        take(4 + h, "o_lo", h + 1)
                        for d in range(2):
                            for m in range(2):
                                mm = pe.matmul(bank[4 + h][:, d * SEQ:(d + 1) * SEQ],
                                               xv[:, m, h * X_DIM + d * P:h * X_DIM + (d + 1) * P],
                                               pair(xpt[2 * (h // 2) + m])[:, h % 2, :], start=(m == 0), stop=(m == 1),
                                               skip_group_check=True)
                        mm.then_inc(S["x_pv"], 1)

                steps = {"index": index, "mem_tr": mem_tr, "swap": swap, "ds_s": ds_s, "gl_gate": gl_gate, "gl_pv": gl_pv, "gl_otr": gl_otr,
                         "ds_tr": ds_tr, "ds_pv": ds_pv}
                for i in range(3):
                    steps[f"rot{i}"] = lambda i=i: rot(i)
                for h in range(HEADS):
                    steps[f"sb_z{h}"] = lambda h=h: sb_z(h)
                    steps[f"sb_btw{h}"] = lambda h=h: sb_btw(h)
                    steps[f"sb_pv{h}"] = lambda h=h: sb_pv(h)
                for i in range(9):
                    steps[f"lev{i}"] = lambda i=i: level(i)

                def product(n):
                    kind, idx = SLABS[n]
                    b = [bank[i] for i in BANKS[n]]
                    pe.wait_ge(S["slab_lo"], at("slab_lo", n + 1))
                    if kind in ("mix", "xo"):
                        if kind == "mix":
                            pe.wait_ge(S["merged_lo"], at("merged_lo", idx + 1))
                        else:
                            pe.wait_ge(S["o_lo"], at("o_lo", idx + 1))
                        if idx == 0:
                            for i in BANKS[n]:
                                if kind == "mix":
                                    reader[i] = ("res", 4)
                                else:
                                    take(i, "res", 8)
                        ah, al = (h_hi, h_lo) if kind == "mix" else (s_hi, s_lo)
                        mm = row_slab(n, BANKS[n], ah[:, 2 * idx:2 * idx + 2, :], al[:, 2 * idx:2 * idx + 2, :],
                                      idx == 0, idx == 3)
                    elif kind == "y":
                        pe.wait_ge(S["y_lo"], at("y_lo", 3))
                        for i, br in zip(BANKS[n], range(3)):
                            take(i, "merged_mul", 3 * idx + br + 1)
                            for f in range(2):
                                mm = feature_major(bank[i][:, f * SEQ:(f + 1) * SEQ], n, CW, 2 * br * CW + f * P, P,
                                                   [y_hi[:, br, k, :] for k in range(2)], [y_lo[:, br, k, :] for k in range(2)])
                    else:
                        for i, part in zip(BANKS[n], ("kk", "misc") if kind == "keys" else (kind,)):
                            take(i, "evac", EVAC[(part, idx)])
                        if kind in ("sbv", "glv", "glo"):
                            for t in range(TT):
                                mm = token_major(b[0][:, t * CW:(t + 1) * CW], n, 0, CW, t, h_hi, h_lo)
                        elif kind == "xv":
                            for t in range(2):
                                mm = token_major(b[0][:, t * CW:(t + 1) * CW], n, 0, CW, t, s_hi, s_lo)
                        elif kind == "keys":
                            hs = [h_hi[:, k, :] for k in range(KT)], [h_lo[:, k, :] for k in range(KT)]
                            feature_major(b[0][:, 0:SEQ], n, CW, K_IX, P, *hs)
                            for t in range(TT):
                                token_major(b[1][:, SEQ + t * 68:SEQ + (t + 1) * 68], n, K_V, 68, t, h_hi, h_lo)
                            mm = feature_major(b[1][0:GLA_RANK, 0:SEQ], n, CW, K_G, GLA_RANK, *hs)
                        else:
                            if kind == "xk":
                                pe.wait_ge(S["mem_lo"], at("mem_lo", 4))
                            ah, al = (s_hi, s_lo) if kind == "xk" else (h_hi, h_lo)
                            for f in range(2):
                                mm = feature_major(b[0][:, f * SEQ:(f + 1) * SEQ], n, CW, f * P, P,
                                                   [ah[:, k, :] for k in range(KT)], [al[:, k, :] for k in range(KT)],
                                                   {0: 0, AT[("xq", 0)]: 1}.get(n) if f == 0 else None)
                    mm.then_inc(S["slab_used"], 1)

                pe.wait_ge(once["ones"], 2)
                pe.wait_ge(S["gain_rows"], at("gain_rows", 80))
                take(0, "gain", 1)
                pe.transpose(bank[0][:, 0:P], gain_rows[:, :], K["ident"]).then_inc(S["gain_t"], 1)
                norm(0)
                for n in range(N_HEAD_SLABS):
                    if SLABS[n] == ("xq", 0):
                        norm(1)
                    if SLABS[n] == ("xo", 0):
                        cross()
                    product(n)
                    for s in PLAN.get(n, ()):
                        if s in steps:
                            steps[s]()
                norm(2)

                def ffn(kind, j, i):
                    n = N_HEAD_SLABS + ffn_index(kind, j)
                    pe.wait_ge(S["slab_lo"], at("slab_lo", n + 1 + 6 * i))
                    if kind == "out":
                        pe.wait_ge(S["ffn_lo"], at("ffn_lo", j + 1 + 2 * i))
                        o = 2 * (j % 2)
                        mm = row_slab(n, (4, 5, 6, 7), s_hi[:, o:o + 2, :], s_lo[:, o:o + 2, :], j == 0, j == N_PAIRS - 1)
                    else:
                        b = 2 * (j % 2) + (kind == "up")
                        if j < 2:
                            pe.wait_ge(S[reader[b][0]], at(*reader[b]))
                        else:
                            pe.wait_ge(S["ffn_mul"], at("ffn_mul", j - 1 + 2 * i))
                        for f in range(2):
                            mm = feature_major(bank[b][:, f * SEQ:(f + 1) * SEQ], n, CW, f * P, P,
                                               [h_hi[:, k, :] for k in range(KT)], [h_lo[:, k, :] for k in range(KT)],
                                               2 if (kind, j, f) == ("gate", 0, 0) else None)
                    mm.then_inc(S["slab_used"], 1)

                ffn_walk(pe, ffn)

        @block.scalar
        def _(act):
            def scaled_exp_of_log(ln_out, v, y, wait_ln, done_ln, done_y):
                act.activation(ln_out, v, ACT.Ln).then_inc(done_ln, 1)
                wait_ln()
                act.activation(y, ln_out, ACT.Exp, scale=-0.5).then_inc(done_y, 1)

            act.wait_ge(once["ones"], 2)
            act.wait_ge(once["x_in"], 16)

            with act.Fori(0, DEPTH) as L:
                links = [0]

                def at(name, n):
                    return L * PER[name] + n + (name in PRIMED_ALL)

                def link(ins):
                    links[0] += 1
                    ins.then_inc(S["act_chain"], 1)
                    act.wait_ge(S["act_chain"], at("act_chain", links[0]))

                def upper(n, i=0):
                    act.wait_ge(landed[slot_of(n)], L * (16 * LANDED_TOTAL[slot_of(n)]) + 16 * LANDED[n] + 32 * i)
                    act.wait_ge(S["slab_used"], at("slab_used", max(n - RING + 1, 0) + 6 * i))
                    dst, src = (r[:, slot_of(n), :] for r in (w_hi, raw))
                    kind = SLABS[n][0] if n < N_HEAD_SLABS else ""
                    if kind == "keys":
                        dst, src = (r.rearrange("p (k n) -> p k n", k=KT)[:, :, 0:K_END] for r in (dst, src))
                    elif kind == "y":
                        dst, src = dst[:, 0:6 * CW], src[:, 0:6 * CW]
                    act.activation(dst, src, ACT.Copy).then_inc(S["slab_hi"], 1)

                def norm_rows(n):
                    act.activation(junk[:, 62:63], ones[:, 0:1], ACT.Ln)
                    if n == 1:
                        act.wait_ge(S["gl_lev"], at("gl_lev", PER["gl_lev"]))
                    for t in range(TT):
                        act.wait_ge(S["res"], at("res", 4 * (n - 1) + 2 * t + 2 if n else 0))
                        act.activation(xn[:, t, :], x[:, t, :], ACT.Square, accum_out=st[:, t:t + 1]).then_inc(S["norm_sq"], 1)
                    act.wait_ge(S["norm_v"], at("norm_v", n + 1))
                    scaled_exp_of_log(st[:, 4:6], st[:, 2:4], st[:, 6:8], lambda: act.wait_ge(S["norm_ln"], at("norm_ln", n + 1)),
                                      S["norm_ln"], S["norm_y"])

                def norm_features(n):
                    for i in range(4):
                        act.wait_ge(S["norm_tr"], at("norm_tr", 4 * n + i + 1))
                        for k in range(2):
                            f = 2 * i + k
                            ins = act.activation(h_hi[:, f, :], bank[4 + i][:, k * SEQ:(k + 1) * SEQ], ACT.Copy,
                                                 scale=gain[:, 8 * n + f:8 * n + f + 1])
                        ins.then_inc(S["norm_hi"], 1)

                def evacuate(n):
                    kind, idx = SLABS[n]
                    if kind in ("y", "mix", "xo"):
                        return
                    act.wait_ge(S["slab_used"], at("slab_used", n + 1))
                    b = bank[BANKS[n][0]]
                    if kind == "keys":
                        act.activation(proj["kk"][:, 0:SEQ], b[:, 0:SEQ], ACT.Copy).then_inc(S["evac"], 1)
                        b = bank[BANKS[n][1]]
                        act.activation(gg[:, :], b[0:GLA_RANK, 0:SEQ], ACT.Copy)
                        rest = b[:, SEQ:SEQ + 2 * 68].rearrange("p (t c) -> p t c", t=TT)
                        act.activation(dv[:, :, :], rest[:, :, 0:HEAD_DIM], ACT.Copy)
                        ins = act.activation(wi[:, :, :], rest[:, :, HEAD_DIM:68], ACT.Copy, scale=IDX_HEADS ** -0.5)
                    elif kind == "glqk":
                        act.activation(proj[kind][:, 0:SEQ], b[:, 0:SEQ], ACT.Copy, scale=GLA_DK ** -0.5)
                        ins = act.activation(proj[kind][:, SEQ:], b[:, SEQ:], ACT.Copy)
                    elif kind == "glo":
                        act.wait_ge(S["rope"], at("rope", 3))
                        act.activation(proj[kind][:, :], b[:, :], ACT.Copy)
                        ins = act.activation(tmp[:, :], b[:, :], ACT.Exp, scale=-1.0)
                    elif kind == "xk":
                        if idx == 0:
                            act.wait_ge(S["mem_tr"], at("mem_tr", 4))
                        ins = act.activation(xk[:, 2 * idx:2 * idx + 2, :], pair(b[:, :]), ACT.Copy)
                    elif kind == "xv":
                        ins = act.activation(xv[:, :, idx * CW:(idx + 1) * CW], pair(b[:, :]), ACT.Copy)
                    elif kind == "xq":
                        ins = act.activation(xq[:, 2 * idx:2 * idx + 2, :], pair(b[:, :]), ACT.Copy)
                    elif kind == "gate":
                        j, br = idx
                        if j < 2:
                            act.wait_ge(S["ffn_lo"], at("ffn_lo", 0))
                        else:
                            act.wait_ge(S["ds_pv"], at("ds_pv", 1))
                        ins = act.activation(sig[j][br], b[:, :], ACT.Sigmoid)
                    else:
                        ins = act.activation(proj[kind][:, :], b[:, :], ACT.Copy, scale=HEAD_DIM ** -0.5 if kind == "sbq" else 1.0)
                    ins.then_inc(S["evac"], 1)

                def index():
                    for n, (t, half) in enumerate(((1, 0), (1, 1), (0, 0), (0, 1))):
                        act.wait_ge(S["idx"], at("idx", n + 1))
                        nk = (t + 1) * P
                        act.activation(relu[t][half], bank[4 + 2 * t + half][:, 0:2 * nk], ACT.Relu,
                                       scale=HEAD_DIM ** -0.5).then_inc(S["idx_relu"], 1)

                def swapped():
                    act.wait_ge(S["swap"], at("swap", 1))
                    act.activation(proj["kk"][:, SEQ:], bank[5][:, 0:SEQ], ACT.Copy).then_inc(S["swapped"], 1)

                def mem_sq():
                    act.wait_ge(S["mem_in"], at("mem_in", 16))
                    act.wait_ge(S["norm_tr"], at("norm_tr", 4))
                    for t in range(TT):
                        act.activation(xn[:, t, :], memx[:, t, :], ACT.Square, accum_out=st[:, 58 + t:59 + t]).then_inc(S["mem_sq"], 1)

                def mem_root():
                    act.wait_ge(S["mem_v"], at("mem_v", 1))
                    scaled_exp_of_log(st[:, 62:64], st[:, 60:62], st[:, 62:64], lambda: act.wait_ge(S["mem_ln"], at("mem_ln", 1)), S["mem_ln"], S["mem_y"])

                def mem_split():
                    act.wait_ge(S["slab_used"], at("slab_used", 0))
                    for i in range(4):
                        act.wait_ge(S["mem_tr"], at("mem_tr", i + 1))
                        for k in range(2):
                            f = 2 * i + k
                            ins = act.activation(s_hi[:, f, :], bank[4 + i][:, k * SEQ:(k + 1) * SEQ], ACT.Copy,
                                                 scale=gain[:, 24 + f:25 + f])
                        ins.then_inc(S["mem_hi"], 1)

                def sb_ln(p):
                    if p == 0:
                        act.wait_ge(S["scored"], at("scored", 1))
                    for h in (2 * p, 2 * p + 1):
                        act.wait_ge(S["sb_z"], at("sb_z", h + 1))
                        if h >= 2:
                            act.wait_ge(S["sb_pv"], at("sb_pv", h - 1))
                        link(act.activation(sbuf3[h % 2][0], bank[4 + h % 2][:, 0:384], ACT.Abs))
                        link(act.activation(sbuf3[h % 2][0], sbuf3[h % 2][0], ACT.Exp, scale=-1.0))
                    for b in (sbuf3[0][0], sbuf3[1][0]):
                        act.activation(b, b, ACT.Ln, bias=1.0).then_inc(S["sb_ln"], 1)

                def sb_exp(h):
                    act.wait_ge(S["sb_arg"], at("sb_arg", h + 1))
                    act.activation(sbuf3[h % 2][0], sbuf3[h % 2][2], ACT.Exp).then_inc(S["sb_exp"], 1)

                def branch_hi(br, done, order):
                    act.wait_ge(S[done], at(done, PER[done]))
                    act.activation(y_hi[:, br, :, :], pair(bank[7][:, :]), ACT.Copy).then_inc(S["y_hi"], 1)

                def gl_ln():
                    act.wait_ge(S["gl_x"], at("gl_x", 1))
                    link(act.activation(la, lx, ACT.Abs))
                    link(act.activation(la, la, ACT.Exp, scale=-1.0))
                    act.activation(la, la, ACT.Ln, bias=1.0).then_inc(S["gl_ln"], 1)

                def decay(i):
                    act.wait_ge(S["gl_dif"], at("gl_dif", i + 1))
                    link(act.activation(dec[i % 2], dec[i % 2], ACT.Abs))
                    act.activation(dec[i % 2], dec[i % 2], ACT.Exp, scale=-1.0 / GLA_TAU).then_inc(S["gl_dec"], 1)

                def gl_var():
                    act.wait_ge(S["gl_pv"], at("gl_pv", 1))
                    act.wait_ge(S["gl_silu"], at("gl_silu", 1))
                    link(act.activation(gl_raw, bank[6][:, :], ACT.Copy))
                    act.activation(tmp[:, :], gl_raw, ACT.Square).then_inc(S["gl_sq"], 1)

                def gl_root():
                    act.wait_ge(S["gl_v"], at("gl_v", 1))
                    link(act.activation(st[:, 26:34], st[:, 18:26], ACT.Ln))
                    act.activation(st[:, 26:34], st[:, 26:34], ACT.Exp, scale=-0.5).then_inc(S["gl_y"], 1)

                def ds_exp():
                    for n, t in enumerate((1, 0)):
                        act.wait_ge(S["ds_max"], at("ds_max", n + 1))
                        p = pair(dprob[t], 4)
                        for s in range(4):
                            c = 4 * n + s
                            ins = act.activation(p[:, s, :], p[:, s, :], ACT.Exp, bias=st[:, 42 + c:43 + c],
                                                 accum_out=st[:, 50 + c:51 + c])
                        ins.then_inc(S["ds_exp"], 1)

                def ds_tr():
                    for g in range(3):
                        act.wait_ge(S["ds_tr"], at("ds_tr", g + 1))
                        act.activation(dpt[g], bank[4 + g][:, :], ACT.Copy).then_inc(S["ds_pt"], 1)

                def merge(j):
                    act.wait_ge(S["merged"], at("merged", j + 1))
                    act.activation(h_hi[:, 2 * j:2 * j + 2, :], pair(acc), ACT.Copy).then_inc(S["merged_hi"], 1)

                def cross():
                    for i in range(4):
                        act.wait_ge(S["x_max"], at("x_max", i + 1))
                        for s in range(2):
                            c = 2 * i + s
                            ins = act.activation(pair(xprob[i])[:, s, :], bank[4 + i][:, s * SEQ:(s + 1) * SEQ], ACT.Exp,
                                                 bias=st[:, 42 + c:43 + c], scale=X_DIM ** -0.5, accum_out=st[:, 50 + c:51 + c])
                        ins.then_inc(S["x_exp"], 1)
                    for i in range(4):
                        act.wait_ge(S["x_tr"], at("x_tr", i + 1))
                        act.activation(xpt[i], bank[4 + i][:, :], ACT.Copy).then_inc(S["x_pt"], 1)
                    for h in range(HEADS):
                        act.wait_ge(S["x_pv"], at("x_pv", h + 1))
                        act.activation(s_hi[:, 2 * h:2 * h + 2, :], pair(bank[4 + h][:, :]), ACT.Copy).then_inc(S["o_hi"], 1)

                steps = {"index": index, "swapped": swapped, "mem_sq": mem_sq, "mem_root": mem_root,
                         "mem_split": mem_split, "gl_ln": gl_ln, "gl_var": gl_var, "gl_root": gl_root,
                         "ds_exp": ds_exp, "ds_tr": ds_tr,
                         "sb_out": lambda: branch_hi(0, "sb_pv", 1), "gl_out": lambda: branch_hi(2, "gl_otr", 2),
                         "ds_out": lambda: branch_hi(1, "ds_pv", 3)}
                for p in range(2):
                    steps[f"sb_ln{p}"] = lambda p=p: sb_ln(p)
                for h in range(HEADS):
                    steps[f"sb_exp{h}"] = lambda h=h: sb_exp(h)
                for i in range(8):
                    steps[f"dec{i}"] = lambda i=i: decay(i)

                norm_rows(0)
                upper(0)
                act.wait_ge(S["gain_t"], at("gain_t", 1))
                act.wait_ge(S["norm_lo"], at("norm_lo", 0))
                act.activation(gain[:, :], bank[0][:, 0:33], ACT.Copy).then_inc(S["gain"], 1)
                act.wait_ge(S["gain"], at("gain", 1))
                norm_features(0)
                upper(1)
                for n in range(N_HEAD_SLABS):
                    steps["upper"] = lambda n=n: upper(n + 2)
                    if SLABS[n] != ("xo", 0) and "upper" not in PLAN.get(n, ()):
                        upper(n + 2)
                    steps_first = SLABS[n - 1][0] == "gate" and SLABS[n - 1][1][0] == 2
                    if n and not steps_first:
                        evacuate(n - 1)
                    if SLABS[n - 1][0] == "y":
                        merge(SLABS[n - 1][1])
                    if SLABS[n - 1] == ("mix", 3):
                        norm_rows(1)
                    if SLABS[n] == ("xq", 0):
                        norm_features(1)
                    if SLABS[n] == ("xo", 0):
                        cross()
                        upper(n + 2)
                    for s in PLAN.get(n, ()):
                        if s in steps:
                            steps[s]()
                    if steps_first:
                        evacuate(n - 1)
                norm_rows(2)
                norm_features(2)

                def silu_of(p, i):
                    act.wait_ge(S["slab_used"], at("slab_used", N_HEAD_SLABS + ffn_index("up", p) + 1 + 6 * i))
                    act.wait_ge(S["ffn_mul"], at("ffn_mul", max(p - 1, 0) + 2 * i))
                    act.activation(silu[p % 2], bank[2 * (p % 2)][:, :], ACT.Silu).then_inc(S["ffn_silu"], 1)

                def act_hi(p, i):
                    act.wait_ge(S["ffn_mul"], at("ffn_mul", p + 1 + 2 * i))
                    act.wait_ge(S["slab_used"], at("slab_used", N_HEAD_SLABS + max(3 * p - 1, 0) + 6 * i))
                    o = 2 * (p % 2)
                    act.activation(s_hi[:, o:o + 2, :], pair(actf[p % 2]), ACT.Copy).then_inc(S["ffn_hi"], 1)

                def ffn(kind, j, i):
                    n = N_HEAD_SLABS + ffn_index(kind, j)
                    if kind == "gate" and j:
                        silu_of(j - 1, i)
                    if kind == "up" and j:
                        act_hi(j - 1, i)
                    if n + 2 < N_SLABS:
                        upper(n + 2, i)
                    if kind == "out" and j == N_PAIRS - 2:
                        silu_of(N_PAIRS - 1, 0)
                        act_hi(N_PAIRS - 1, 0)

                ffn_walk(act, ffn)
                assert links[0] == PER["act_chain"], links[0]

            act.wait_ge(S["res"], DEPTH * PER["res"] + 1)
            for t in range(TT):
                act.activation(xn[:, t, :], x[:, t, :], ACT.Square, accum_out=st[:, t:t + 1]).then_inc(once["f_sq"], 1)
            act.wait_ge(once["f_v"], 1)
            scaled_exp_of_log(st[:, 4:6], st[:, 2:4], st[:, 6:8], lambda: act.wait_ge(once["f_ln"], 1), once["f_ln"], once["f_y"])

        @block.vector
        def _(dve):
            def mean_and_eps(v, sq, count):
                return dve.tensor_scalar(v, sq, 1.0 / count, EPS, ALU.mult, ALU.add)

            def refine(link, y, v, t):
                link(dve.tensor_tensor(t, y, y, ALU.mult))
                link(dve.tensor_tensor(t, t, v, ALU.mult))
                link(dve.tensor_scalar(t, t, -0.5, 1.5, ALU.mult, ALU.add))
                link(dve.tensor_tensor(y, y, t, ALU.mult))

            for name in PRIMED["DVE"]:
                dve.sem_inc(S[name], 1)
            outside = [0]

            def link_once(ins):
                outside[0] += 1
                ins.then_inc(once["f_chain"], 1)
                dve.wait_ge(once["f_chain"], outside[0])

            dve.wait_ge(once["consts"], 16)
            dve.wait_ge(once["x_in"], 16)

            with dve.Fori(0, DEPTH) as L:
                links, aparts = [0], [0]

                def at(name, n):
                    return L * PER[name] + n + (name in PRIMED_ALL)

                def link(ins):
                    links[0] += 1
                    ins.then_inc(S["dve_chain"], 1)
                    dve.wait_ge(S["dve_chain"], at("dve_chain", links[0]))

                def apart():
                    aparts[0] += 1
                    dve.memset(junk[:, aparts[0]:aparts[0] + 1], 0.0)

                def lower(n, i=0):
                    dve.wait_ge(S["slab_hi"], at("slab_hi", n + 1 + 6 * i))
                    dst, src, hi = w_lo[:, slot_of(n), :], raw[:, slot_of(n), :], w_hi[:, slot_of(n), :].bitcast(F32)
                    kind = SLABS[n][0] if n < N_HEAD_SLABS else ""
                    if kind == "keys":
                        dst, src, hi = (r.rearrange("p (k n) -> p k n", k=KT)[:, :, 0:K_END] for r in (dst, src, hi))
                    elif kind == "y":
                        dst, src, hi = dst[:, 0:6 * CW], src[:, 0:6 * CW], hi[:, 0:6 * CW]
                    dve.tensor_tensor(dst, src, hi, ALU.subtract).then_inc(S["slab_lo"], 1)

                def features_lo(lo, hi, g, done, first, signal):
                    for i in range(4):
                        dve.wait_ge(S[done], at(done, first + i + 1))
                        for k in range(2):
                            f = 2 * i + k
                            ins = dve.scalar_tensor_tensor(lo[:, f, :], bank[4 + i][:, k * SEQ:(k + 1) * SEQ],
                                                           gain[:, g + f:g + f + 1], hi[:, f, :].bitcast(F32),
                                                           ALU.mult, ALU.subtract)
                        ins.then_inc(S[signal], 1)

                def norm_rows(n):
                    dve.wait_ge(S["norm_sq"], at("norm_sq", 2 * n + 2))
                    dve.wait_ge(S["norm_xn"], at("norm_xn", 2 * n))
                    mean_and_eps(st[:, 2:4], st[:, 0:2], D_MODEL).then_inc(S["norm_v"], 1)
                    dve.wait_ge(S["norm_y"], at("norm_y", n + 1))
                    refine(link, st[:, 6:8], st[:, 2:4], st[:, 8:10])
                    for t in range(TT):
                        dve.tensor_scalar(xn[:, t, :], x[:, t, :], st[:, 6 + t:7 + t], None, ALU.mult).then_inc(S["norm_xn"], 1)

                def norm_features(n):
                    features_lo(h_lo, h_hi, 8 * n, "norm_hi", 4 * n, "norm_lo")

                def residual(n, banks, first):
                    dve.wait_ge(S["slab_used"], at("slab_used", n))
                    for t in range(TT):
                        for m in range(2):
                            r = x[:, t, m * 512:(m + 1) * 512]
                            dve.tensor_tensor(r, r, bank[banks[2 * t + m]][:, :], ALU.add).then_inc(S["res"], 1)
                    dve.wait_ge(S["res"], at("res", first + 4))

                def rope(i):
                    n = 1 if i == 1 else 2
                    src, t = (pair(ap[:, 0:n * SEQ], n) for ap in (proj[("ixq", "kk", "dsq")[i]], tmp))
                    dve.wait_ge(S["rot"], at("rot", i + 1))
                    dve.wait_ge(S["rope"], at("rope", i))
                    link(dve.tensor_tensor(t, pair(bank[(4, 5, 7)[i]][:, 0:n * SEQ], n), over(K["sin"], n), ALU.mult))
                    link(dve.tensor_tensor(src, src, over(K["cos"], n), ALU.mult))
                    dve.tensor_tensor(src, src, t, ALU.add).then_inc(S["rope"], 1)

                def index():
                    dve.wait_ge(S["evac"], at("evac", EVAC["misc"]))
                    for n, (t, half) in enumerate(((1, 0), (1, 1), (0, 0), (0, 1))):
                        dve.wait_ge(S["idx_relu"], at("idx_relu", n + 1))
                        nk = (t + 1) * P
                        for hh in range(2):
                            h = 2 * hh + half
                            before = K[f"adm{t}"] if half == 0 and hh == 0 else score[t]
                            ins = dve.scalar_tensor_tensor(score[t], relu[t][half][:, hh * nk:(hh + 1) * nk],
                                                           wi[:, t, h:h + 1], before, ALU.mult, ALU.add)
                            if (n, hh) != (3, 1):
                                link(ins)
                    ins.then_inc(S["scored"], 1)
                    dve.wait_ge(S["scored"], at("scored", 1))

                def topk(t, part):
                    for _ in range(TOPK // 16):
                        apart()
                        link(dve.max(m8[:, t, :], score[t]))
                        apart()
                        link(dve.match_replace(score[t], m8[:, t, :], score[t], TAKEN))
                    if part == 1:
                        link(dve.tensor_scalar(bias[t], score[t], TAKEN, NEG, ALU.not_equal, ALU.mult))

                def mem_sq():
                    dve.wait_ge(S["mem_sq"], at("mem_sq", 2))
                    mean_and_eps(st[:, 60:62], st[:, 58:60], D_MODEL).then_inc(S["mem_v"], 1)

                def mem_root():
                    dve.wait_ge(S["mem_y"], at("mem_y", 1))
                    refine(link, st[:, 62:64], st[:, 60:62], st[:, 58:60])
                    for t in range(TT):
                        dve.tensor_scalar(memx[:, t, :], memx[:, t, :], st[:, 62 + t:63 + t], None, ALU.mult).then_inc(S["mem_x"], 1)

                def mem_split():
                    features_lo(s_lo, s_hi, 24, "mem_hi", 0, "mem_lo")

                def diagonal(ap):
                    return ap.rearrange("p (a b) -> p a b", b=P)[:, 0:3:2, :]

                def sb_keep(h):
                    soft, keep, beta = sbuf3[h % 2]
                    z = bank[4 + h % 2][:, 0:384]
                    dve.wait_ge(S["sb_ln"], at("sb_ln", h + 1))
                    link(dve.scalar_tensor_tensor(beta, z, 0.0, soft, ALU.min, ALU.subtract))
                    link(dve.tensor_tensor(keep, beta, z, ALU.subtract))
                    dve.tensor_tensor(diagonal(keep), diagonal(keep), over(K["valid"], 2), ALU.mult).then_inc(S["sb_keep"], 1)

                def sb_arg(h):
                    beta = sbuf3[h % 2][2]
                    dve.wait_ge(S["sb_btw"], at("sb_btw", h + 1))
                    dve.tensor_tensor(beta, beta, bank[6][:, 0:384], ALU.add).then_inc(S["sb_arg"], 1)

                def sb_w(h):
                    w = diagonal(sbuf3[h % 2][0])
                    dve.wait_ge(S["sb_exp"], at("sb_exp", h + 1))
                    dve.tensor_tensor(w, w, over(K["valid"], 2), ALU.mult).then_inc(S["sb_w"], 1)

                def branch_lo(br, order):
                    dve.wait_ge(S["y_hi"], at("y_hi", order))
                    dve.tensor_tensor(y_lo[:, br, :, :], pair(bank[7][:, :]), y_hi[:, br, :, :].bitcast(F32),
                                      ALU.subtract).then_inc(S["y_lo"], 1)

                def gl_gate():
                    dve.wait_ge(S["gl_gate"], at("gl_gate", 1))
                    dve.tensor_scalar(lx, bank[5][:, 0:SEQ], gain[:, 32:33], None, ALU.add).then_inc(S["gl_x"], 1)

                def gl_cum():
                    dve.wait_ge(S["gl_ln"], at("gl_ln", 1))
                    link(dve.scalar_tensor_tensor(la, lx, 0.0, la, ALU.min, ALU.subtract))
                    dve.wait_ge(once["ones"], 2)
                    link(dve.tensor_tensor_scan(cum, ones[:, :], la, 0.0, ALU.mult, ALU.add))

                def difference(i):
                    s = 1 << i
                    if i >= 2:
                        dve.wait_ge(S["gl_qk"], at("gl_qk", i - 1))
                    dve.wait_ge(S["sb_pv"], at("sb_pv", min(i + 3, 4)))
                    b = cum.rearrange("p (n w) -> p n w", w=2 * s)
                    dve.tensor_tensor(dec[i % 2].rearrange("p (n w) -> p n w", w=2 * s), b,
                                      b[:, :, s - 1:s].to_broadcast([P, SEQ // (2 * s), 2 * s]),
                                      ALU.subtract).then_inc(S["gl_dif"], 1)

                def level(i):
                    q, k = proj["glqk"][:, 0:SEQ], proj["glqk"][:, SEQ:2 * SEQ]
                    dve.wait_ge(S["zeroed"], at("zeroed", 1))
                    if i >= 2:
                        dve.wait_ge(S["gl_lev"], at("gl_lev", LEVEL_COUNT[i - 1]))
                    if i < 8:
                        dve.wait_ge(S["gl_dec"], at("gl_dec", i + 1))
                        dve.tensor_tensor(ke[i % 2], k, dec[i % 2], ALU.mult)
                    for h in range(HEADS):
                        r = slice(32 * h, 32 * h + 32)
                        if i < 8:
                            ins = dve.tensor_tensor(qe[i % 2][r, h, :], q[r, :], dec[i % 2][r, :], ALU.mult)
                        else:
                            ins = dve.tensor_copy(qe[i % 2][r, h, :], q[r, :])
                    ins.then_inc(S["gl_qk"], 1)

                def apply(i):
                    for t in ((1,) if i == 7 else (0, 1)):
                        b = pair(bank[4 + 2 * (i % 2) + t][:, :], 4)
                        dve.wait_ge(S["gl_lev"], at("gl_lev", LEVEL_COUNT[i] + (t + 1 if i != 7 else 1)))
                        if i:
                            dve.wait_ge(S["gl_app"], at("gl_app", LEVEL_COUNT[i]))
                        if i == 7:
                            ins = dve.tensor_copy(pair(attx, 4), b)
                        elif i == 0:
                            ins = dve.tensor_tensor(pair(att[t], 4), b, over(K["lev0"], 4), ALU.mult)
                        else:
                            mask = K["ident"] if i == 8 else K[f"lev{i}"]
                            apart()
                            ins = dve.copy_predicated(pair(att[t], 4), over(mask.bitcast(I32), 4), b)
                        ins.then_inc(S["gl_app"], 1)

                def gl_silu():
                    g = proj["glo"]
                    dve.wait_ge(S["evac"], at("evac", EVAC["glo"]))
                    dve.wait_ge(S["gate_w"], at("gate_w", 32))
                    link(dve.tensor_scalar(tmp[:, :], tmp[:, :], 1.0, None, ALU.add))
                    link(dve.reciprocal(tmp[:, :], tmp[:, :]))
                    link(dve.tensor_tensor(g[:, :], g[:, :], tmp[:, :], ALU.mult))
                    dve.tensor_tensor(pair(g[:, :], 8), pair(g[:, :], 8), over(norm_g[:, :], 8), ALU.mult).then_inc(S["gl_silu"], 1)

                def gl_var():
                    dve.wait_ge(S["gl_sq"], at("gl_sq", 1))
                    link(dve.tensor_reduce(st[:, 10:18], pair(tmp[:, :], 8), AX_X, ALU.add))
                    mean_and_eps(st[:, 18:26], st[:, 10:18], HEAD_DIM).then_inc(S["gl_v"], 1)

                def gl_o():
                    dve.wait_ge(S["gl_y"], at("gl_y", 1))
                    dve.wait_ge(S["gl_silu"], at("gl_silu", 1))
                    refine(link, st[:, 26:34], st[:, 18:26], st[:, 34:42])
                    link(dve.tensor_tensor(pair(tmp[:, :], 8), pair(gl_raw, 8), spread(st[:, 26:34], HEAD_DIM), ALU.mult))
                    dve.tensor_tensor(tmp[:, :], tmp[:, :], proj["glo"][:, :], ALU.mult).then_inc(S["gl_o"], 1)

                def ds_max():
                    for n, (t, half) in enumerate(((1, 0), (1, 1), (0, 0), (0, 1))):
                        dve.wait_ge(S["ds_s"], at("ds_s", n + 1))
                        nk = (t + 1) * P
                        if n == 0:
                            dve.wait_ge(S["gl_pv"], at("gl_pv", 1))
                        dve.scalar_tensor_tensor(pair(dprob[t][:, half * 2 * nk:(half + 1) * 2 * nk]),
                                                 pair(bank[4 + 2 * t + half][:, 0:2 * nk]), HEAD_DIM ** -0.5,
                                                 over(bias[t], 2), ALU.mult, ALU.add).then_inc(S["ds_p"], 1)
                    for n, t in enumerate((1, 0)):
                        dve.wait_ge(S["ds_p"], at("ds_p", 2 * n + 2))
                        dve.tensor_reduce(st[:, 42 + 4 * n:46 + 4 * n], pair(dprob[t], 4), AX_X, ALU.max,
                                          negate=True).then_inc(S["ds_max"], 1)

                def ds_norm():
                    for n, t in enumerate((1, 0)):
                        sums = st[:, 50 + 4 * n:54 + 4 * n]
                        dve.wait_ge(S["ds_exp"], at("ds_exp", n + 1))
                        link(dve.reciprocal(sums, sums))
                        dve.tensor_tensor(pair(dprob[t], 4), pair(dprob[t], 4), spread(sums, (t + 1) * P), ALU.mult).then_inc(S["ds_norm"], 1)

                def merge(n):
                    j = SLABS[n][1]
                    dve.wait_ge(S["slab_used"], at("slab_used", n + 1))
                    dve.wait_ge(S["evac"], at("evac", EVAC[("gate", (j, 2))]))
                    if j:
                        dve.wait_ge(S["merged_lo"], at("merged_lo", j))
                    for br in range(3):
                        dst = part if br else acc
                        dve.tensor_tensor(dst, sig[j][br], bank[BANKS[n][br]][:, :], ALU.mult).then_inc(S["merged_mul"], 1)
                        dve.wait_ge(S["merged_mul"], at("merged_mul", 3 * j + br + 1))
                        if br == 1:
                            link(dve.tensor_tensor(acc, acc, part, ALU.add))
                        if br == 2:
                            dve.tensor_tensor(acc, acc, part, ALU.add).then_inc(S["merged"], 1)

                def merge_lo(n):
                    j = SLABS[n][1]
                    dve.wait_ge(S["merged_hi"], at("merged_hi", j + 1))
                    dve.tensor_tensor(h_lo[:, 2 * j:2 * j + 2, :], pair(acc), h_hi[:, 2 * j:2 * j + 2, :].bitcast(F32),
                                      ALU.subtract).then_inc(S["merged_lo"], 1)

                def cross():
                    def maximum(i):
                        m = st[:, 42 + 2 * i:44 + 2 * i]
                        dve.wait_ge(S["xs"], at("xs", i + 1))
                        link(dve.tensor_reduce(m, pair(bank[4 + i][:, :]), AX_X, ALU.max, negate=True))
                        dve.tensor_scalar(m, m, X_DIM ** -0.5, None, ALU.mult).then_inc(S["x_max"], 1)

                    def normalise(i):
                        sums = st[:, 50 + 2 * i:52 + 2 * i]
                        dve.wait_ge(S["x_exp"], at("x_exp", i + 1))
                        link(dve.reciprocal(sums, sums))
                        dve.tensor_tensor(pair(xprob[i]), pair(xprob[i]), spread(sums, SEQ), ALU.mult).then_inc(S["x_norm"], 1)

                    maximum(0)
                    for i in range(1, 4):
                        maximum(i)
                        normalise(i - 1)
                    normalise(3)
                    for h in range(HEADS):
                        dve.wait_ge(S["o_hi"], at("o_hi", h + 1))
                        dve.tensor_tensor(s_lo[:, 2 * h:2 * h + 2, :], pair(bank[4 + h][:, :]),
                                          s_hi[:, 2 * h:2 * h + 2, :].bitcast(F32), ALU.subtract).then_inc(S["o_lo"], 1)

                steps = {"index": index, "mem_sq": mem_sq,
                         "mem_root": mem_root, "mem_split": mem_split,
                         "gl_gate": gl_gate, "gl_cum": gl_cum, "gl_silu": gl_silu, "gl_var": gl_var, "gl_o": gl_o,
                         "ds_max": ds_max, "ds_norm": ds_norm,
                         "sb_out": lambda: branch_lo(0, 1), "gl_out": lambda: branch_lo(2, 2), "ds_out": lambda: branch_lo(1, 3)}
                for t in range(TT):
                    steps[f"topk{t}a"] = lambda t=t: topk(t, 0)
                    steps[f"topk{t}b"] = lambda t=t: topk(t, 1)
                for i in range(3):
                    steps[f"rope{i}"] = lambda i=i: rope(i)
                for h in range(HEADS):
                    for name, f in (("sb_keep", sb_keep), ("sb_arg", sb_arg), ("sb_w", sb_w)):
                        steps[f"{name}{h}"] = lambda h=h, f=f: f(h)
                for i in range(9):
                    steps[f"dif{i}"] = lambda i=i: difference(i)
                    steps[f"lev{i}"] = lambda i=i: level(i)
                    steps[f"app{i}"] = lambda i=i: apply(i)

                norm_rows(0)
                lower(0)
                norm_features(0)
                lower(1)
                for n in range(N_HEAD_SLABS):
                    if SLABS[n - 1][0] == "y":
                        merge(n - 1)
                    if SLABS[n - 1] == ("mix", 3):
                        residual(n, BANKS[n - 1], 0)
                        norm_rows(1)
                    if SLABS[n] == ("xq", 0):
                        norm_features(1)
                    if SLABS[n] == ("xo", 0):
                        cross()
                    steps["lower"] = lambda n=n: lower(n + 2)
                    if "lower" not in PLAN.get(n, ()):
                        lower(n + 2)
                    if SLABS[n - 1][0] == "y":
                        merge_lo(n - 1)
                    for s in PLAN.get(n, ()):
                        if s in steps:
                            steps[s]()
                residual(N_HEAD_SLABS, BANKS[N_HEAD_SLABS - 1], 4)
                norm_rows(2)
                norm_features(2)

                def multiply(p, i):
                    dve.wait_ge(S["ffn_silu"], at("ffn_silu", p + 1 + 2 * i))
                    dve.tensor_tensor(actf[p % 2], silu[p % 2], bank[1 + 2 * (p % 2)][:, :], ALU.mult).then_inc(S["ffn_mul"], 1)

                def act_lo(p, i):
                    dve.wait_ge(S["ffn_hi"], at("ffn_hi", p + 1 + 2 * i))
                    o = 2 * (p % 2)
                    dve.tensor_tensor(s_lo[:, o:o + 2, :], pair(actf[p % 2]), s_hi[:, o:o + 2, :].bitcast(F32),
                                      ALU.subtract).then_inc(S["ffn_lo"], 1)

                def ffn(kind, j, i):
                    n = N_HEAD_SLABS + ffn_index(kind, j)
                    if kind == "gate" and j:
                        multiply(j - 1, i)
                    if kind == "up" and j:
                        act_lo(j - 1, i)
                    if n + 2 < N_SLABS:
                        lower(n + 2, i)
                    if kind == "out" and j == N_PAIRS - 2:
                        multiply(N_PAIRS - 1, 0)
                        act_lo(N_PAIRS - 1, 0)

                ffn_walk(dve, ffn)
                residual(N_SLABS, (4, 5, 6, 7), 8)
                assert links[0] == PER["dve_chain"], links[0]

            dve.wait_ge(once["f_sq"], 2)
            mean_and_eps(st[:, 2:4], st[:, 0:2], D_MODEL).then_inc(once["f_v"], 1)
            dve.wait_ge(once["f_y"], 1)
            refine(link_once, st[:, 6:8], st[:, 2:4], st[:, 8:10])
            dve.wait_ge(once["f_g"], 16)
            for t in range(TT):
                dve.scalar_tensor_tensor(xn[:, t, :], x[:, t, :], st[:, 6 + t:7 + t],
                                         xk[:, 0:4, :].rearrange("p a b -> p (a b)"), ALU.mult, ALU.mult).then_inc(once["f_out"], 1)


_INS = ("x", "mem", "mix_norm_g", "w_in", "gla_w_up", "gla_b", "gla_norm_g", "w_br_a", "w_br_b", "w_br_c",
        "w_mix_out", "xattn_norm_g", "mem_norm_g", "w_xq", "w_xkv", "w_xo", "ffn_norm_g", "w_ffn_in",
        "w_ffn_out", "final_norm_g")


def kernel(**inputs):
    import concourse.bacc as bacc
    from concourse.bass_utils import run_bass_kernel_spmd

    nc = bacc.Bacc("TRN2", target_bir_lowering=False, num_devices=1)
    arrays, args = {}, {}
    for name in _INS:
        v = np.ascontiguousarray(inputs[name])
        arrays[f"in_{name}"] = v
        args[name] = nc.dram_tensor(f"in_{name}", v.shape, mybir.dt.from_np(v.dtype), kind="ExternalInput").ap()
    arrays["shape_constants"] = CONST_ARRAY
    args["shape_constants"] = nc.dram_tensor("shape_constants", CONST_ARRAY.shape, F32, kind="ExternalInput").ap()
    out = nc.dram_tensor("out", (1, SEQ, D_MODEL), F32, kind="ExternalOutput").ap()
    program(nc, args, out)
    return run_bass_kernel_spmd(nc, [arrays], core_ids=[0]).results[0]["out"]
```

```python
from contextlib import ExitStack

import concourse.bass as bass
import numpy as np
from concourse import mybir

F32 = mybir.dt.float32
F32R = mybir.dt.float32r
I32 = mybir.dt.int32
ALU = mybir.AluOpType
ACT = mybir.ActivationFunctionType
AX_X = mybir.AxisListType.X

P = 128
D_MODEL = 1024
SEQ = 256
DEPTH = 2
N_MEM = 256
KT = D_MODEL // P
TT = SEQ // P
D_FF = 2816
HEADS = 4
HEAD_DIM = 64
GLA_DK = 32
GLA_RANK = 16
GLA_TAU = 16.0
IDX_HEADS = 4
TOPK = 64
CHUNK = 64
X_DIM = D_MODEL // HEADS
EPS = 1e-6
ROPE_THETA = 10000.0
CW = 256
NEG = -3.0e38
TAKEN = -3.4e38

C_SBQ, C_SBK, C_SBV, C_DSQ, C_DSK, C_DSV = 0, 256, 512, 768, 1024, 1088
C_IXQ, C_IXK, C_IXW, C_GLQ, C_GLV, C_GLG, C_GLO, C_GATE = 1152, 1408, 1472, 1476, 1732, 1988, 2004, 2260
IN_WIDTH = C_GATE + 3 * D_MODEL

SLABS = [("ixq", 0), ("keys", 0), ("sbk", 0), ("sbq", 0), ("dsq", 0), ("sbv", 0),
         ("glqk", 0), ("glv", 0), ("glo", 0)]
SLABS += [("xk", j) for j in range(4)] + [("gate", (j, b)) for j in range(2) for b in range(3)] + [("xv", 0)]
SLABS += [("gate", (j, b)) for j in range(2, 4) for b in range(3)]
SLABS += [("y", 0), ("y", 1), ("xv", 1), ("mix", 0), ("y", 2), ("mix", 1), ("y", 3), ("mix", 2), ("mix", 3), ("xv", 2), ("xv", 3)]
SLABS += [("xq", j) for j in range(4)] + [("xo", j) for j in range(4)]
N_HEAD_SLABS = len(SLABS)
N_PAIRS = D_FF // CW
N_SLABS = N_HEAD_SLABS + 3 * N_PAIRS
AT = {s: i for i, s in enumerate(SLABS)}
RING = 3
K_IX, K_DS, K_V, K_W, K_G, K_END = 0, 64, 128, 192, 196, 212

PLAN = {
    0: ["mem_sq"],
    1: ["rot0", "rope0", "mem_root"],
    2: ["rot1", "rope1"],
    3: ["swap", "swapped", "mem_tr", "mem_split"],
    4: ["index"],
    5: ["rot2", "sb_z0", "sb_z1", "sb_ln0", "topk1a"],
    6: ["rope2", "gl_gate", "sb_keep0", "sb_keep1", "lower"],
    7: ["sb_btw0", "sb_btw1", "sb_arg0", "sb_exp0", "sb_arg1", "sb_exp1", "gl_x", "gl_ln", "form0"],
    8: ["sb_w0", "sb_w1", "gl_cum", "dif1", "dif2", "lower", "dec1", "dec2", "sb_pv0", "sb_pv1", "sb_z2", "sb_z3", "lev0", "sb_ln1"],
    9: ["app0", "form1", "topk1b", "lower", "lev1"],
    10: ["app1", "form2", "sb_keep2", "sb_keep3", "dif3", "lower", "dec3", "lev2", "sb_btw2", "sb_btw3"],
    11: ["app2", "form3", "lower", "sb_arg2", "sb_exp2", "sb_arg3", "sb_exp3", "lev3"],
    12: ["sb_w2", "sb_w3", "app3", "dif4", "dif5", "dec4", "dec5", "lower", "sb_pv2", "sb_pv3", "sb_out"],
    13: ["form4", "lower", "form5", "lev4", "gl_silu"],
    14: ["app4", "dif6", "dec6", "dif7", "dec7", "lower", "lev5"],
    15: ["app5", "form6", "lower", "lev6", "form7"],
    16: ["app6", "dif8", "dec8", "lower", "lev7", "form8", "app7", "lev8"],
    17: ["app8", "lower", "topk0a", "gl_pv", "gl_var", "gl_root"],
    18: ["topk0b", "lower", "ds_s", "gl_o", "ds_max", "ds_exp"],
    19: ["ds_norm", "lower", "gl_otr", "gl_out"],
    20: ["ds_tr"],
    21: ["ds_pv", "ds_out"],
}

EVAC = {}
for _kind, _idx in SLABS:
    for _part in {"y": (), "mix": (), "xo": (), "keys": ("kk", "misc")}.get(_kind, (_kind,)):
        EVAC[(_part, _idx)] = EVAC[_part] = len({k for k in EVAC if isinstance(k, tuple)}) + 1
LEVEL_COUNT = [0, 2, 4, 6, 8, 10, 12, 14, 16, 17]
LEVEL_BANKS = [(6, 3)] * 4 + [(6, 3), (4, 5)] * 3
Y_ORDER = {"a": 1, "c": 2, "b": 3}


def bank_plan():
    at, out = 0, []
    for kind, _ in SLABS:
        if kind == "mix":
            out.append([4, 5, 6, 7])
            continue
        n = {"y": 3, "xo": 4, "keys": 2}.get(kind, 1)
        if n == 4:
            at = 0
        ring = 4 if kind in ("y", "xo", "xq") else 3
        out.append([(at + i) % ring for i in range(n)])
        at = (at + n) % ring
    return out


BANKS = bank_plan()


def slab_pieces(kind, idx):
    if kind == "keys":
        return [(C_IXK, K_IX, 64), (C_DSK, K_DS, 128), (C_IXW, K_W, 4), (C_GLG, K_G, 16)]
    start = {"ixq": C_IXQ, "sbq": C_SBQ, "sbk": C_SBK, "dsq": C_DSQ, "sbv": C_SBV, "glqk": C_GLQ,
             "glv": C_GLV, "glo": C_GLO}
    if kind in start:
        return [(start[kind], 0, CW)]
    return None


def n_dmas(kind):
    return {"keys": 4, "y": 3}.get(kind, 1)


def landed_plan():
    counts, out = [0] * RING, []
    for n in range(N_SLABS):
        counts[n % RING] += n_dmas(SLABS[n][0]) if n < N_HEAD_SLABS else 1
        out.append(counts[n % RING])
    return out, counts


LANDED, LANDED_TOTAL = landed_plan()

CONST = {}


def constants():
    parts = []

    def put(name, a):
        CONST[name] = (sum(p.shape[1] for p in parts), a.shape[1])
        parts.append(a.astype(np.float32))

    r, c = np.arange(P)[:, None], np.arange(P)[None, :]
    put("ident", r == c)
    lower = (c % HEAD_DIM) < HEAD_DIM // 2
    put("rot", np.where(lower & (r == c + 32), -1.0, 0.0) + np.where(~lower & (r == c - 32), 1.0, 0.0))
    put("later", r > c)
    put("valid", r < c)
    q, k = np.arange(SEQ)[:, None], np.arange(SEQ)[None, :]
    adm = np.where(k // CHUNK <= q // CHUNK, 0.0, NEG)
    put("adm0", adm[:P, :P])
    put("adm1", adm[P:, :])
    inv = np.float32(1.0) / np.float32(ROPE_THETA) ** (np.arange(32, dtype=np.float32) * np.float32(2.0 / HEAD_DIM))
    ang = (np.arange(SEQ, dtype=np.float32)[None, :] * inv[:, None]).astype(np.float32)
    put("cos", np.tile(np.cos(ang), (4, 1)))
    put("sin", np.tile(np.sin(ang), (4, 1)))
    for lev in range(7):
        s = 1 << lev
        put(f"lev{lev}", (r // (2 * s) == c // (2 * s)) & (r % (2 * s) < s) & (c % (2 * s) >= s))
    return np.concatenate(parts, axis=1)


CONST_ARRAY = constants()

PER = dict(
    slab_hi=N_SLABS, slab_lo=N_SLABS, slab_used=N_SLABS,
    gain_rows=5 * 16, gain_t=1, gain=1, gate_w=2 * 16, mem_in=16,
    mem_sq=2, mem_v=1, mem_y=1, mem_x=2, mem_tr=4,
    norm_sq=6, norm_v=3, norm_y=3, norm_xn=6, norm_tr=12, norm_hi=12, norm_lo=12,
    evac=34, merged_mul=12, merged=4, merged_hi=4, merged_lo=4, tile0_out=3, res=12,
    rot=3, rope=3, swap=1, swapped=1, idx=4, idx_relu=4, scored=1,
    sb_z=4, sb_ln=4, sb_keep=4, sb_btw=4, sb_arg=4, sb_exp=4, sb_w=4, sb_pv=4,
    gl_gate=1, gl_x=1, gl_ln=1, gl_cum=1, gl_silu=1, zeroed=1,
    gl_dif=8, gl_dec=8, gl_qk=9, gl_lev=17, gl_app=17, gl_pv=1, gl_sq=1, gl_v=1, gl_y=1, gl_o=1, gl_otr=1,
    ds_s=4, ds_p=4, ds_max=2, ds_exp=2, ds_norm=2, ds_tr=3, ds_pt=3, ds_pv=1,
    y_hi=3, y_lo=3, mem_hi=4, mem_lo=4,
    xs=4, x_max=4, x_exp=4, x_norm=4, x_tr=4, x_pt=4, x_pv=4, o_hi=4, o_lo=4,
    ffn_silu=N_PAIRS, ffn_mul=N_PAIRS, ffn_hi=N_PAIRS, ffn_lo=N_PAIRS,
    act_chain=19, dve_chain=95,
)

PRIMED_BY_PE = {"slab_used": 1, "gain_t": 1, "xs": 1, "gl_gate": 1}
PRIMED_BY_DVE = {"slab_lo": 1, "norm_lo": 1, "norm_xn": 1, "res": 3, "rope": 1, "gl_silu": 1, "ffn_mul": 1, "ffn_lo": 1}
PRIMED = {**PRIMED_BY_PE, **PRIMED_BY_DVE}


def program(nc, a, out):
    ctx = ExitStack()
    with ctx:
        def sb(name, shape, dt=F32):
            return ctx.enter_context(nc.sbuf_tensor(name, shape, dt))

        S = {n: ctx.enter_context(nc.semaphore(f"s_{n}")) for n in PER}
        landed = [ctx.enter_context(nc.semaphore(f"s_landed{i}")) for i in range(RING)]
        once = {n: ctx.enter_context(nc.semaphore(f"s_{n}")) for n in (
            "consts", "pool_junk", "x_in", "ones", "f_sq", "f_v", "f_y", "f_g", "f_out", "f_chain", "stored")}

        const = sb("const", [P, CONST_ARRAY.shape[1]])
        K = {n: const[:, o:o + w] for n, (o, w) in CONST.items()}
        ones = sb("ones", [P, SEQ])
        x = sb("x", [P, TT, D_MODEL])
        xn = sb("xn", [P, TT, D_MODEL])
        h_hi, h_lo = sb("h_hi", [P, KT, SEQ], F32R), sb("h_lo", [P, KT, SEQ], F32R)
        s_hi, s_lo = sb("s_hi", [P, KT, SEQ], F32R), sb("s_lo", [P, KT, SEQ], F32R)
        y_hi, y_lo = sb("y_hi", [P, 3, 2, SEQ], F32R), sb("y_lo", [P, 3, 2, SEQ], F32R)
        raw = sb("raw", [P, RING, 8 * CW])
        w_hi, w_lo = sb("w_hi", [P, RING, 8 * CW], F32R), sb("w_lo", [P, RING, 8 * CW], F32R)
        xk, xv = sb("xk", [P, KT, SEQ]), sb("xv", [P, 2, D_MODEL])
        proj = {n: sb(n, [P, 2 * SEQ]) for n in ("ixq", "kk", "dsq", "sbq", "sbk", "sbv", "glqk", "glv", "glo")}
        gg = sb("gg", [GLA_RANK, SEQ])
        dv = sb("dv", [P, TT, HEAD_DIM])
        wi = sb("wi", [P, TT, IDX_HEADS])
        gain_rows = sb("gain_rows", [P, P])
        gain = sb("gain", [P, 33])
        w_up = sb("w_up", [GLA_RANK, P])
        norm_g = sb("norm_g", [P, HEAD_DIM])
        tmp = sb("tmp", [P, 2 * SEQ])
        scr = sb("scr", [P, 6656])
        st = sb("st", [P, 64])
        junk = sb("junk", [P, 64])
        m8 = sb("m8", [P, TT, 8])
        bank = [ctx.enter_context(nc.psum_tensor(f"bank{i}", [P, 512], F32)) for i in range(8)]

        sig = [[scr[:, (3 * j + b) * 512:(3 * j + b + 1) * 512] for b in range(3)] for j in range(4)]
        score = [scr[:, 3072:3200], scr[:, 3200:3456]]
        bias = [scr[:, 3456:3584], scr[:, 3584:3840]]
        F0 = 3840
        relu = {1: [scr[:, F0:F0 + 512], scr[:, F0 + 512:F0 + 1024]],
                0: [scr[:, F0 + 1024:F0 + 1280], scr[:, F0 + 1280:F0 + 1536]]}
        dprob = {1: scr[:, F0:F0 + 1024], 0: scr[:, F0 + 1024:F0 + 1536]}
        dpt = [scr[:, F0 + 1536:F0 + 2048], scr[:, F0 + 2048:F0 + 2560], tmp[:, :]]
        sbuf3 = [[scr[:, 1152 * p + 384 * i:1152 * p + 384 * (i + 1)] for i in range(3)] for p in range(2)]
        dec = [scr[:, F0:F0 + 256], scr[:, F0 + 256:F0 + 512]]
        ke = [scr[:, F0 + 512:F0 + 768], scr[:, F0 + 768:F0 + 1024]]
        att = [scr[:, F0 + 1024:F0 + 1536], scr[:, F0 + 1536:F0 + 2048]]
        attx = scr[:, F0 + 2048:F0 + 2560]
        cum = scr[:, F0 + 2560:F0 + 2816]
        lx, la = tmp[:, 0:SEQ], tmp[:, SEQ:2 * SEQ]
        qe = [xn[:, i, :].rearrange("p (h t) -> p h t", h=HEADS) for i in range(2)]
        gl_raw = xn[:, 0, 0:2 * SEQ]
        xq = xn[:, :, :].rearrange("p a b -> p (a b)").rearrange("p (k t) -> p k t", k=KT)
        xprob = [scr[:, 512 * i:512 * (i + 1)] for i in range(4)]
        xpt = [scr[:, 2048 + 512 * i:2560 + 512 * i] for i in range(4)]
        acc, part = scr[:, 6144:6656], tmp[:, :]
        silu = [scr[:, 0:512], scr[:, 512:1024]]
        actf = [scr[:, 1024:1536], scr[:, 1536:2048]]
        memx = xk[:, :, :].rearrange("p a b -> p (a b)").rearrange("p (t d) -> p t d", t=TT)

        def pair(ap, n=2):
            return ap.rearrange("p (a b) -> p a b", a=n)

        def over(ap, n):
            return ap.unsqueeze(1).to_broadcast([P, n, ap.shape[1]])

        def spread(ap, n):
            return ap.unsqueeze(2).to_broadcast([P, ap.shape[1], n])

        def right(ap, i):
            s = 1 << (i - 1)
            return ap.rearrange("p h (n w) -> p h n w", w=2 * s)[:, :, :, s:2 * s]

        def compact(ap, i):
            return ap[:, 0:4 * P // 2].rearrange("p (h n w) -> p h n w", h=4, w=1 << (i - 1))

        def slot_of(n):
            return n % RING

        def ffn_index(kind, j):
            if kind == "out":
                return 3 * j + 4 if j < N_PAIRS - 1 else 3 * N_PAIRS - 1
            first = 3 * j - 1 if j else 0
            return first + (kind == "up")

        PAIRS_LOOPED = N_PAIRS - 3
        assert PAIRS_LOOPED % 2 == 0

        def ffn_walk(eng, step):
            step("gate", 0, 0)
            step("up", 0, 0)
            for kind, j in (("gate", 1), ("up", 1), ("out", 0)):
                step(kind, j, 0)
            with eng.Fori(0, PAIRS_LOOPED // 2) as i:
                for d in (1, 2):
                    for kind, j in (("gate", d + 1), ("up", d + 1), ("out", d)):
                        step(kind, j, i)
            for kind, j in (("gate", N_PAIRS - 1), ("up", N_PAIRS - 1), ("out", N_PAIRS - 2), ("out", N_PAIRS - 1)):
                step(kind, j, 0)

        block = ctx.enter_context(nc.Block())

        @block.sync
        def _(sp):
            sp.dma_start(x[:, :, :], a["x"].rearrange("b (t p) d -> p (b t) d", p=P)).then_inc(once["x_in"], 16)
            sp.dma_start(const[:, :], a["shape_constants"]).then_inc(once["consts"], 16)
            sp.wait_ge(once["ones"], 2)
            with sp.Fori(0, DEPTH) as L:
                def at(name, n):
                    return L * PER[name] + n + PRIMED.get(name, 0)

                def load_slab(n, pieces, i=0):
                    if n != RING:
                        sp.wait_ge(S["slab_lo"], at("slab_lo", max(n - RING + 1, 0) + 6 * i))
                    for dst, src in pieces:
                        sp.dma_start(dst, src).then_inc(landed[slot_of(n)], 16)

                def gains():
                    sp.wait_ge(S["gain_t"], at("gain_t", 0))
                    for r, name in enumerate(("mix_norm_g", "xattn_norm_g", "ffn_norm_g", "mem_norm_g")):
                        sp.dma_start(gain_rows[8 * r:8 * r + 8, :],
                                     a[name][L].rearrange("(k p) -> k p", p=P)).then_inc(S["gain_rows"], 16)
                    sp.dma_start(gain_rows[32:33, :], a["gla_b"][L].rearrange("(a n) -> a n", a=1)).then_inc(S["gain_rows"], 16)

                def col_slab(w, c0, cols=CW):
                    return w[L].rearrange("(k p) n -> p k n", p=P)[:, :, c0:c0 + cols]

                def head_slab(n):
                    kind, idx = SLABS[n]
                    dst = raw[:, slot_of(n), :].rearrange("p (k n) -> p k n", k=KT)
                    pieces = slab_pieces(kind, idx)
                    if pieces is not None:
                        load_slab(n, [(dst[:, :, d:d + c], col_slab(a["w_in"], s, c)) for s, d, c in pieces])
                    elif kind == "gate":
                        j, b = idx
                        load_slab(n, [(dst, col_slab(a["w_in"], C_GATE + b * D_MODEL + j * CW))])
                    elif kind == "y":
                        load_slab(n, [(dst[:, 2 * b:2 * b + 2, :], col_slab(a[w], idx * CW))
                                      for b, w in enumerate(("w_br_a", "w_br_b", "w_br_c"))])
                    elif kind in ("xk", "xv"):
                        load_slab(n, [(dst, col_slab(a["w_xkv"], (kind == "xv") * D_MODEL + idx * CW))])
                    elif kind == "xq":
                        load_slab(n, [(dst, col_slab(a["w_xq"], idx * CW))])
                    else:
                        w = a["w_mix_out" if kind == "mix" else "w_xo"]
                        load_slab(n, [(raw[:, slot_of(n), :].rearrange("p (k n) -> p k n", k=2),
                                       w[L, idx * 256:idx * 256 + 256, :].rearrange("(k p) n -> p k n", p=P))])

                gains()
                head_slab(0)
                head_slab(1)
                sp.wait_ge(S["xs"], at("xs", 0))
                sp.dma_start(memx, a["mem"].rearrange("b (t p) d -> p (b t) d", p=P)).then_inc(S["mem_in"], 16)
                head_slab(2)
                sp.wait_ge(S["gl_gate"], at("gl_gate", 0))
                sp.dma_start(w_up[:, :], a["gla_w_up"][L]).then_inc(S["gate_w"], 16)
                sp.wait_ge(S["slab_lo"], at("slab_lo", 1))
                sp.wait_ge(S["gl_silu"], at("gl_silu", 0))
                sp.dma_start(norm_g[:, :], a["gla_norm_g"][L].rearrange("(a n) -> a n", a=1)
                             .to_broadcast([P, HEAD_DIM])).then_inc(S["gate_w"], 16)
                for n in range(3, N_HEAD_SLABS):
                    head_slab(n)

                def ffn_slab(kind, j, i):
                    n = N_HEAD_SLABS + ffn_index(kind, j)
                    if kind == "out":
                        src = a["w_ffn_out"][L, bass.ds(i * 2 * CW + j * CW, CW), :].rearrange("(k p) n -> p k n", p=P)
                        dst = raw[:, slot_of(n), :].rearrange("p (k n) -> p k n", k=2)
                    else:
                        c0 = (kind == "up") * D_FF + j * CW
                        src = a["w_ffn_in"][L].rearrange("(k p) n -> p k n", p=P)[:, :, bass.ds(i * 2 * CW + c0, CW)]
                        dst = raw[:, slot_of(n), :].rearrange("p (k n) -> p k n", k=KT)
                    load_slab(n, [(dst, src)], i)

                ffn_walk(sp, ffn_slab)
            sp.wait_ge(S["xs"], DEPTH * PER["xs"] + PRIMED["xs"])
            sp.dma_start(xk[:, 0:4, :].rearrange("p a b -> p (a b)"),
                         a["final_norm_g"].rearrange("(a n) -> a n", a=1).to_broadcast([P, D_MODEL])).then_inc(once["f_g"], 16)
            for t in range(TT):
                sp.wait_ge(once["f_out"], t + 1)
                sp.dma_start(out[0, t * P:(t + 1) * P, :], xn[:, t, :]).then_inc(once["stored"], 16)
            sp.wait_ge(once["stored"], 32)

        @block.gpsimd
        def _(pool):
            pool.memset(ones[:, :], 1.0).then_inc(once["ones"], 1)
            pool.memset(gain_rows[:, :], 0.0).then_inc(once["ones"], 1)
            pool.wait_ge(once["ones"], 2)
            with pool.Fori(0, DEPTH) as L:
                pool.wait_ge(S["mem_sq"], L * PER["mem_sq"] + 2)
                pool.tensor_tensor(junk[:, 0:1], ones[:, 0:1], ones[:, 0:1], ALU.add).then_inc(once["pool_junk"], 1)
                pool.memset(xn[:, :, :], 0.0).then_inc(S["zeroed"], 1)

        @block.tensor
        def _(pe):
            for name, count in PRIMED_BY_PE.items():
                pe.sem_inc(S[name], count)
            pe.wait_ge(once["consts"], 16)
            with pe.Fori(0, DEPTH) as L:
                def at(name, n):
                    return L * PER[name] + n + PRIMED.get(name, 0)

                reader = {b: ("ffn_mul", 0) for b in range(4)}
                reader.update({b: ("res", 0) for b in range(4, 8)})

                def take(b, name, n):
                    pe.wait_ge(S[reader[b][0]], at(*reader[b]))
                    reader[b] = (name, n)

                def three(dst, st_hi, st_lo, mv_hi, mv_lo, first, last):
                    pe.matmul(dst, st_hi, mv_hi, start=first, stop=False, skip_group_check=True)
                    pe.matmul(dst, st_hi, mv_lo, start=False, stop=False, skip_group_check=True)
                    return pe.matmul(dst, st_lo, mv_hi, start=False, stop=last, skip_group_check=True)

                def feature_major(dst, n, width, c0, cols, act_hi, act_lo, norm=None):
                    for k, (ah, al) in enumerate(zip(act_hi, act_lo)):
                        if norm is not None and k % 2 == 0:
                            pe.wait_ge(S["norm_lo"], at("norm_lo", 4 * norm + k // 2 + 1))
                        o = k * width + c0
                        wh, wl = w_hi[:, slot_of(n), o:o + cols], w_lo[:, slot_of(n), o:o + cols]
                        mm = three(dst, wh, wl, ah, al, k == 0, k == len(act_hi) - 1)
                    return mm

                def token_major(dst, n, c0, cols, t, a_hi, a_lo):
                    for k in range(KT):
                        o = k * CW + c0
                        mm = three(dst, a_hi[:, k, t * P:(t + 1) * P], a_lo[:, k, t * P:(t + 1) * P],
                                   w_hi[:, slot_of(n), o:o + cols], w_lo[:, slot_of(n), o:o + cols], k == 0, k == KT - 1)
                    return mm

                def row_slab(n, banks, k_hi, k_lo, first, last):
                    wh = w_hi[:, slot_of(n), :].rearrange("p (k n) -> p k n", k=2)
                    wl = w_lo[:, slot_of(n), :].rearrange("p (k n) -> p k n", k=2)
                    order = [(0, 0), (0, 1), (1, 0), (1, 1)] if last else [(0, 0), (1, 0), (0, 1), (1, 1)]
                    for t, k in order:
                        if last and (t, k) == (1, 0):
                            mm.then_inc(S["tile0_out"], 1)
                        ah, al = k_hi[:, k, t * P:(t + 1) * P], k_lo[:, k, t * P:(t + 1) * P]
                        for st_, w, begin, end in ((ah, wh, first and k == 0, False), (ah, wl, False, False),
                                                   (al, wh, False, last and k == 1)):
                            for m in range(2):
                                mm = pe.matmul(bank[banks[2 * t + m]][:, :], st_, w[:, k, m * 512:(m + 1) * 512],
                                               start=begin, stop=end, skip_group_check=True)
                    return mm

                def to_features(src, t, i):
                    for kk in range(2):
                        mm = pe.transpose(bank[4 + i][:, kk * SEQ + t * P:kk * SEQ + (t + 1) * P],
                                          src[:, t, (2 * i + kk) * P:(2 * i + kk + 1) * P], K["ident"])
                    return mm

                def norm(n):
                    pe.wait_ge(S["norm_xn"], at("norm_xn", 2 * n + 1))
                    for i in range(4):
                        take(4 + i, "norm_lo", 4 * n + i + 1)
                        to_features(xn, 0, i)
                    pe.wait_ge(S["norm_xn"], at("norm_xn", 2 * n + 2))
                    for i in range(4):
                        to_features(xn, 1, i).then_inc(S["norm_tr"], 1)

                def mem_tr():
                    pe.wait_ge(S["mem_x"], at("mem_x", 1))
                    for i in range(4):
                        take(4 + i, "mem_lo", i + 1)
                        to_features(memx, 0, i)
                    pe.wait_ge(S["mem_x"], at("mem_x", 2))
                    for i in range(4):
                        to_features(memx, 1, i).then_inc(S["mem_tr"], 1)

                def rot(i):
                    src = proj[("ixq", "kk", "dsq")[i]]
                    pe.wait_ge(S["evac"], at("evac", (1, 2, EVAC["dsq"])[i]))
                    b = (4, 7, 7)[i]
                    take(b, "rope", i + 1)
                    w = SEQ if i == 1 else 2 * SEQ
                    pe.matmul(bank[b][:, 0:w], K["rot"], src[:, 0:w], start=True, stop=True).then_inc(S["rot"], 1)

                def swap():
                    pe.wait_ge(S["rope"], at("rope", 2))
                    take(5, "swapped", 1)
                    for half in range(2):
                        mm = pe.matmul(bank[5][64 * half:64 * half + 64, 0:SEQ], K["ident"][:, 64 - 64 * half:P - 64 * half],
                                       proj["kk"][:, 0:SEQ], start=True, stop=True)
                    mm.then_inc(S["swap"], 1)

                def head_scores(q, kt, signal, freed):
                    for n, (t, half) in enumerate(((1, 0), (1, 1), (0, 0), (0, 1))):
                        b, nk = (4 + 2 * t + half), (t + 1) * P
                        take(b, freed, n + 1)
                        r = slice(64 * half, 64 * half + 64)
                        for hh in range(2):
                            mm = pe.matmul(bank[b][:, hh * nk:(hh + 1) * nk],
                                           q[r, hh * SEQ + t * P:hh * SEQ + (t + 1) * P],
                                           proj["kk"][r, (kt ^ half) * SEQ:(kt ^ half) * SEQ + nk], start=True, stop=True)
                        mm.then_inc(S[signal], 1)

                def index():
                    pe.wait_ge(S["swapped"], at("swapped", 1))
                    head_scores(proj["ixq"], 0, "idx", "idx_relu")

                def ds_s():
                    pe.wait_ge(S["rope"], at("rope", 3))
                    head_scores(proj["dsq"], 1, "ds_s", "ds_p")

                def sb_z(h):
                    pe.wait_ge(S["evac"], at("evac", EVAC["sbq"]))
                    b, r, o = 4 + h % 2, slice(64 * (h % 2), 64 * (h % 2) + 64), (h // 2) * SEQ
                    take(b, "sb_keep", h + 1)
                    pe.matmul(bank[b][:, 0:SEQ], proj["sbk"][r, o:o + P], proj["sbq"][r, o:o + SEQ], start=True, stop=True)
                    pe.matmul(bank[b][:, SEQ:SEQ + P], proj["sbk"][r, o + P:o + SEQ], proj["sbq"][r, o + P:o + SEQ],
                              start=True, stop=True).then_inc(S["sb_z"], 1)

                def sb_btw(h):
                    keep = sbuf3[h % 2][1]
                    pe.wait_ge(S["sb_keep"], at("sb_keep", h + 1))
                    b = bank[4 + h % 2]
                    take(4 + h % 2, "sb_arg", h + 1)
                    pe.matmul(b[:, 0:384], K["later"], keep, start=True, stop=False, skip_group_check=True)
                    pe.matmul(b[:, P:2 * P], ones[:, 0:P], keep[:, 256:384], start=False, stop=True,
                              skip_group_check=True).then_inc(S["sb_btw"], 1)

                def sb_pv(h):
                    w = sbuf3[h % 2][0]
                    pe.wait_ge(S["sb_w"], at("sb_w", h + 1))
                    if h == 0:
                        pe.wait_ge(S["evac"], at("evac", EVAC["sbv"]))
                        take(7, "y_lo", 1)
                    o = bank[7][64 * (h % 2):64 * (h % 2) + 64, (h // 2) * SEQ:(h // 2 + 1) * SEQ]
                    v = pair(proj["sbv"][:, :])
                    pe.matmul(o, v[:, 0, h * 64:h * 64 + 64], w[:, 0:SEQ], start=True, stop=False, skip_group_check=True)
                    pe.matmul(o[:, P:SEQ], v[:, 1, h * 64:h * 64 + 64], w[:, SEQ:384], start=False, stop=True,
                              skip_group_check=True).then_inc(S["sb_pv"], 1)

                def gl_gate():
                    pe.wait_ge(S["evac"], at("evac", EVAC["misc"]))
                    pe.wait_ge(S["gate_w"], at("gate_w", 32))
                    take(6, "gl_x", 1)
                    pe.matmul(bank[6][:, 0:SEQ], w_up[:, :], gg[:, :], start=True, stop=True).then_inc(S["gl_gate"], 1)

                def level(i):
                    pe.wait_ge(S["gl_qk"], at("gl_qk", i + 1))
                    k = ke[i % 2] if i else proj["glqk"][:, SEQ:2 * SEQ]
                    for t in ((1,) if i == 8 else (0, 1)):
                        b = LEVEL_BANKS[i][t]
                        n = LEVEL_COUNT[i] + t + 1 if i != 8 else LEVEL_COUNT[i] + 1
                        take(b, "gl_app", n)
                        kt = 0 if i == 8 else t
                        queries, dst = qe[i % 2][:, :, t * P:(t + 1) * P], pair(bank[b][:, :], 4)
                        if 0 < i < 8:
                            queries, dst = right(queries, i), compact(bank[b], i)
                        pe.matmul(dst, k[:, kt * P:(kt + 1) * P], queries, start=True, stop=True).then_inc(S["gl_lev"], 1)

                def gl_pv():
                    pe.wait_ge(S["gl_app"], at("gl_app", LEVEL_COUNT[9]))
                    pe.wait_ge(S["evac"], at("evac", EVAC["glv"]))
                    take(6, "gl_sq", 1)
                    v = pair(proj["glv"][:, :])
                    for t in range(TT):
                        for h in range(HEADS):
                            o = bank[6][:, t * 256 + h * 64:t * 256 + (h + 1) * 64]
                            c = slice(h * 64, (h + 1) * 64)
                            mm = pe.matmul(o, att[t][:, h * P:(h + 1) * P], v[:, t, c], start=True, stop=(t == 0),
                                           skip_group_check=True)
                            if t == 1:
                                mm = pe.matmul(o, attx[:, h * P:(h + 1) * P], v[:, 0, c], start=False, stop=True,
                                               skip_group_check=True)
                    mm.then_inc(S["gl_pv"], 1)

                def gl_otr():
                    pe.wait_ge(S["gl_o"], at("gl_o", 1))
                    take(7, "y_lo", Y_ORDER["c"])
                    for k in range(2):
                        for t in range(TT):
                            mm = pe.transpose(bank[7][:, k * SEQ + t * P:k * SEQ + (t + 1) * P],
                                              tmp[:, t * SEQ + k * P:t * SEQ + (k + 1) * P], K["ident"])
                    mm.then_inc(S["gl_otr"], 1)

                def ds_tr():
                    p1, p0 = pair(dprob[1], 4), pair(dprob[0], 4)
                    pe.wait_ge(S["ds_norm"], at("ds_norm", 2))
                    for g in range(2):
                        take(4 + g, "ds_pt", g + 1)
                        for s in range(2):
                            pe.transpose(bank[4 + g][:, s * SEQ:s * SEQ + P], p0[:, 2 * g + s, :], K["ident"])
                            mm = pe.transpose(bank[4 + g][:, s * SEQ + P:(s + 1) * SEQ], p1[:, 2 * g + s, 0:P], K["ident"])
                        mm.then_inc(S["ds_tr"], 1)
                    take(6, "ds_pt", 3)
                    for s in range(4):
                        mm = pe.transpose(bank[6][:, s * P:(s + 1) * P], p1[:, s, P:SEQ], K["ident"])
                    mm.then_inc(S["ds_tr"], 1)

                def ds_pv():
                    pe.wait_ge(S["ds_pt"], at("ds_pt", 3))
                    take(7, "y_lo", Y_ORDER["b"])
                    for s in range(4):
                        h = 2 * (s % 2) + s // 2
                        o = bank[7][64 * (h % 2):64 * (h % 2) + 64, (h // 2) * SEQ:(h // 2 + 1) * SEQ]
                        pe.matmul(o, dv[:, 0, :], dpt[s // 2][:, (s % 2) * SEQ:(s % 2 + 1) * SEQ], start=True, stop=False,
                                  skip_group_check=True)
                        mm = pe.matmul(o[:, P:SEQ], dv[:, 1, :], dpt[2][:, s * P:(s + 1) * P], start=False, stop=True,
                                       skip_group_check=True)
                    mm.then_inc(S["ds_pv"], 1)

                def cross():
                    pe.wait_ge(S["evac"], at("evac", EVAC[("xq", 3)]))
                    for i in range(4):
                        t = i % 2
                        take(4 + i, "x_exp", i + 1)
                        for s in range(2):
                            h = 2 * (i // 2) + s
                            for k in range(2):
                                mm = pe.matmul(bank[4 + i][:, s * SEQ:(s + 1) * SEQ], xq[:, 2 * h + k, t * P:(t + 1) * P],
                                               xk[:, 2 * h + k, :], start=(k == 0), stop=(k == 1), skip_group_check=True)
                        mm.then_inc(S["xs"], 1)

                    def turn(i):
                        m = i % 2
                        pe.wait_ge(S["x_norm"], at("x_norm", 2 * (i // 2) + 2))
                        take(4 + i, "x_pt", i + 1)
                        for s in range(2):
                            for t in range(TT):
                                src = pair(xprob[2 * (i // 2) + t])[:, s, m * P:(m + 1) * P]
                                mm = pe.transpose(bank[4 + i][:, s * SEQ + t * P:s * SEQ + (t + 1) * P], src, K["ident"])
                        mm.then_inc(S["x_tr"], 1)

                    def values(h):
                        pe.wait_ge(S["x_pt"], at("x_pt", 2 * (h // 2) + 2))
                        take(4 + h, "o_lo", h + 1)
                        for d in range(2):
                            for m in range(2):
                                mm = pe.matmul(bank[4 + h][:, d * SEQ:(d + 1) * SEQ],
                                               xv[:, m, h * X_DIM + d * P:h * X_DIM + (d + 1) * P],
                                               pair(xpt[2 * (h // 2) + m])[:, h % 2, :], start=(m == 0), stop=(m == 1),
                                               skip_group_check=True)
                        mm.then_inc(S["x_pv"], 1)

                    turn(0)
                    turn(1)
                    values(0)
                    turn(2)
                    turn(3)
                    for h in range(1, HEADS):
                        values(h)

                steps = {"index": index, "mem_tr": mem_tr, "swap": swap, "ds_s": ds_s, "gl_gate": gl_gate, "gl_pv": gl_pv, "gl_otr": gl_otr,
                         "ds_tr": ds_tr, "ds_pv": ds_pv}
                for i in range(3):
                    steps[f"rot{i}"] = lambda i=i: rot(i)
                for h in range(HEADS):
                    steps[f"sb_z{h}"] = lambda h=h: sb_z(h)
                    steps[f"sb_btw{h}"] = lambda h=h: sb_btw(h)
                    steps[f"sb_pv{h}"] = lambda h=h: sb_pv(h)
                for i in range(9):
                    steps[f"lev{i}"] = lambda i=i: level(i)

                def product(n):
                    kind, idx = SLABS[n]
                    b = [bank[i] for i in BANKS[n]]
                    pe.wait_ge(S["slab_lo"], at("slab_lo", n + 1))
                    if kind in ("mix", "xo"):
                        if kind == "mix":
                            pe.wait_ge(S["merged_lo"], at("merged_lo", idx + 1))
                        else:
                            pe.wait_ge(S["o_lo"], at("o_lo", idx + 1))
                        if idx == 0:
                            for i in BANKS[n]:
                                if kind == "mix":
                                    reader[i] = ("res", 4)
                                else:
                                    take(i, "res", 8)
                        ah, al = (h_hi, h_lo) if kind == "mix" else (s_hi, s_lo)
                        mm = row_slab(n, BANKS[n], ah[:, 2 * idx:2 * idx + 2, :], al[:, 2 * idx:2 * idx + 2, :],
                                      idx == 0, idx == 3)
                    elif kind == "y":
                        pe.wait_ge(S["y_lo"], at("y_lo", 3))
                        for i, br in zip(BANKS[n], range(3)):
                            take(i, "merged_mul", 3 * idx + br + 1)
                            for f in range(2):
                                mm = feature_major(bank[i][:, f * SEQ:(f + 1) * SEQ], n, CW, 2 * br * CW + f * P, P,
                                                   [y_hi[:, br, k, :] for k in range(2)], [y_lo[:, br, k, :] for k in range(2)])
                    else:
                        for i, part in zip(BANKS[n], ("kk", "misc") if kind == "keys" else (kind,)):
                            take(i, "evac", EVAC[(part, idx)])
                        if kind in ("sbv", "glv", "glo"):
                            for t in range(TT):
                                mm = token_major(b[0][:, t * CW:(t + 1) * CW], n, 0, CW, t, h_hi, h_lo)
                        elif kind == "xv":
                            for t in range(2):
                                if t == 1 and idx == 3:
                                    norm(1)
                                mm = token_major(b[0][:, t * CW:(t + 1) * CW], n, 0, CW, t, s_hi, s_lo)
                        elif kind == "keys":
                            hs = [h_hi[:, k, :] for k in range(KT)], [h_lo[:, k, :] for k in range(KT)]
                            feature_major(b[0][:, 0:SEQ], n, CW, K_IX, P, *hs)
                            for t in range(TT):
                                token_major(b[1][:, SEQ + t * 68:SEQ + (t + 1) * 68], n, K_V, 68, t, h_hi, h_lo)
                            mm = feature_major(b[1][0:GLA_RANK, 0:SEQ], n, CW, K_G, GLA_RANK, *hs)
                        else:
                            if kind == "xk":
                                pe.wait_ge(S["mem_lo"], at("mem_lo", 4))
                            ah, al = (s_hi, s_lo) if kind == "xk" else (h_hi, h_lo)
                            for f in range(2):
                                mm = feature_major(b[0][:, f * SEQ:(f + 1) * SEQ], n, CW, f * P, P,
                                                   [ah[:, k, :] for k in range(KT)], [al[:, k, :] for k in range(KT)],
                                                   {0: 0, AT[("xq", 0)]: 1}.get(n) if f == 0 else None)
                    mm.then_inc(S["slab_used"], 1)

                pe.wait_ge(once["ones"], 2)
                pe.wait_ge(S["gain_rows"], at("gain_rows", 80))
                take(0, "gain", 1)
                pe.transpose(bank[0][:, 0:P], gain_rows[:, :], K["ident"]).then_inc(S["gain_t"], 1)
                norm(0)
                for n in range(N_HEAD_SLABS):
                    if SLABS[n] == ("xo", 0):
                        cross()
                    product(n)
                    for s in PLAN.get(n, ()):
                        if s in steps:
                            steps[s]()
                norm(2)

                def ffn(kind, j, i):
                    n = N_HEAD_SLABS + ffn_index(kind, j)
                    pe.wait_ge(S["slab_lo"], at("slab_lo", n + 1 + 6 * i))
                    if kind == "out":
                        pe.wait_ge(S["ffn_lo"], at("ffn_lo", j + 1 + 2 * i))
                        o = 2 * (j % 2)
                        mm = row_slab(n, (4, 5, 6, 7), s_hi[:, o:o + 2, :], s_lo[:, o:o + 2, :], j == 0, j == N_PAIRS - 1)
                    else:
                        b = 2 * (j % 2) + (kind == "up")
                        if j < 2:
                            pe.wait_ge(S[reader[b][0]], at(*reader[b]))
                        else:
                            pe.wait_ge(S["ffn_mul"], at("ffn_mul", j - 1 + 2 * i))
                        for f in range(2):
                            mm = feature_major(bank[b][:, f * SEQ:(f + 1) * SEQ], n, CW, f * P, P,
                                               [h_hi[:, k, :] for k in range(KT)], [h_lo[:, k, :] for k in range(KT)],
                                               2 if (kind, j, f) == ("gate", 0, 0) else None)
                    mm.then_inc(S["slab_used"], 1)

                ffn_walk(pe, ffn)

        @block.scalar
        def _(act):
            act.wait_ge(once["ones"], 2)
            act.wait_ge(once["x_in"], 16)

            with act.Fori(0, DEPTH) as L:
                links = [0]

                def at(name, n):
                    return L * PER[name] + n + PRIMED.get(name, 0)

                def link(ins):
                    links[0] += 1
                    ins.then_inc(S["act_chain"], 1)
                    act.wait_ge(S["act_chain"], at("act_chain", links[0]))

                def upper(n, i=0):
                    act.wait_ge(landed[slot_of(n)], L * (16 * LANDED_TOTAL[slot_of(n)]) + 16 * LANDED[n] + 32 * i)
                    act.wait_ge(S["slab_used"], at("slab_used", max(n - RING + 1, 0) + 6 * i))
                    dst, src = (r[:, slot_of(n), :] for r in (w_hi, raw))
                    kind = SLABS[n][0] if n < N_HEAD_SLABS else ""
                    if kind == "keys":
                        dst, src = (r.rearrange("p (k n) -> p k n", k=KT)[:, :, 0:K_END] for r in (dst, src))
                    elif kind == "y":
                        dst, src = dst[:, 0:6 * CW], src[:, 0:6 * CW]
                    act.activation(dst, src, ACT.Copy).then_inc(S["slab_hi"], 1)

                def norm_rows(n):
                    act.activation(junk[:, 62:63], ones[:, 0:1], ACT.Sqrt)
                    if n == 1:
                        act.wait_ge(S["gl_lev"], at("gl_lev", PER["gl_lev"]))
                    for t in range(TT):
                        act.wait_ge(S["res"], at("res", 4 * n - 2 + 2 * t))
                        act.activation(xn[:, t, :], x[:, t, :], ACT.Square, accum_out=st[:, t:t + 1]).then_inc(S["norm_sq"], 1)
                    act.wait_ge(S["norm_v"], at("norm_v", n + 1))
                    act.activation(st[:, 4:6], st[:, 2:4], ACT.Sqrt).then_inc(S["norm_y"], 1)

                def norm_features(n):
                    for i in range(4):
                        act.wait_ge(S["norm_tr"], at("norm_tr", 4 * n + i + 1))
                        for k in range(2):
                            f = 2 * i + k
                            ins = act.activation(h_hi[:, f, :], bank[4 + i][:, k * SEQ:(k + 1) * SEQ], ACT.Copy,
                                                 scale=gain[:, 8 * n + f:8 * n + f + 1])
                        ins.then_inc(S["norm_hi"], 1)

                def evacuate(n):
                    kind, idx = SLABS[n]
                    if kind in ("y", "mix", "xo"):
                        return
                    act.wait_ge(S["slab_used"], at("slab_used", n + 1))
                    b = bank[BANKS[n][0]]
                    if kind == "keys":
                        act.activation(proj["kk"][:, 0:SEQ], b[:, 0:SEQ], ACT.Copy).then_inc(S["evac"], 1)
                        b = bank[BANKS[n][1]]
                        act.activation(gg[:, :], b[0:GLA_RANK, 0:SEQ], ACT.Copy)
                        rest = b[:, SEQ:SEQ + 2 * 68].rearrange("p (t c) -> p t c", t=TT)
                        act.activation(dv[:, :, :], rest[:, :, 0:HEAD_DIM], ACT.Copy)
                        ins = act.activation(wi[:, :, :], rest[:, :, HEAD_DIM:68], ACT.Copy, scale=IDX_HEADS ** -0.5)
                    elif kind == "glqk":
                        act.activation(proj[kind][:, 0:SEQ], b[:, 0:SEQ], ACT.Copy, scale=GLA_DK ** -0.5)
                        ins = act.activation(proj[kind][:, SEQ:], b[:, SEQ:], ACT.Copy)
                    elif kind == "glo":
                        act.wait_ge(S["gl_cum"], at("gl_cum", 1))
                        act.activation(proj[kind][:, :], b[:, :], ACT.Copy)
                        ins = act.activation(tmp[:, :], b[:, :], ACT.Exp, scale=-1.0)
                    elif kind == "xk":
                        if idx == 0:
                            act.wait_ge(S["mem_tr"], at("mem_tr", 4))
                        ins = act.activation(xk[:, 2 * idx:2 * idx + 2, :], pair(b[:, :]), ACT.Copy)
                    elif kind == "xv":
                        ins = act.activation(xv[:, :, idx * CW:(idx + 1) * CW], pair(b[:, :]), ACT.Copy)
                    elif kind == "xq":
                        ins = act.activation(xq[:, 2 * idx:2 * idx + 2, :], pair(b[:, :]), ACT.Copy)
                    elif kind == "gate":
                        j, br = idx
                        if j < 2:
                            act.wait_ge(S["sb_pv"], at("sb_pv", 4))
                        else:
                            act.wait_ge(S["ds_pv"], at("ds_pv", 1))
                        ins = act.activation(sig[j][br], b[:, :], ACT.Sigmoid)
                    else:
                        ins = act.activation(proj[kind][:, :], b[:, :], ACT.Copy, scale=HEAD_DIM ** -0.5 if kind == "sbq" else 1.0)
                    ins.then_inc(S["evac"], 1)

                def index():
                    for n, (t, half) in enumerate(((1, 0), (1, 1), (0, 0), (0, 1))):
                        act.wait_ge(S["idx"], at("idx", n + 1))
                        nk = (t + 1) * P
                        act.activation(relu[t][half], bank[4 + 2 * t + half][:, 0:2 * nk], ACT.Relu,
                                       scale=HEAD_DIM ** -0.5).then_inc(S["idx_relu"], 1)

                def swapped():
                    act.wait_ge(S["swap"], at("swap", 1))
                    act.activation(proj["kk"][:, SEQ:], bank[5][:, 0:SEQ], ACT.Copy).then_inc(S["swapped"], 1)

                def mem_sq():
                    act.wait_ge(S["mem_in"], at("mem_in", 16))
                    act.wait_ge(S["norm_tr"], at("norm_tr", 4))
                    for t in range(TT):
                        act.activation(xn[:, t, :], memx[:, t, :], ACT.Square, accum_out=st[:, 58 + t:59 + t]).then_inc(S["mem_sq"], 1)

                def mem_root():
                    act.wait_ge(S["mem_v"], at("mem_v", 1))
                    act.activation(st[:, 62:64], st[:, 60:62], ACT.Sqrt).then_inc(S["mem_y"], 1)

                def mem_split():
                    act.wait_ge(S["slab_used"], at("slab_used", 0))
                    for i in range(4):
                        act.wait_ge(S["mem_tr"], at("mem_tr", i + 1))
                        for k in range(2):
                            f = 2 * i + k
                            ins = act.activation(s_hi[:, f, :], bank[4 + i][:, k * SEQ:(k + 1) * SEQ], ACT.Copy,
                                                 scale=gain[:, 24 + f:25 + f])
                        ins.then_inc(S["mem_hi"], 1)

                def sb_ln(p):
                    if p == 0:
                        act.wait_ge(S["ffn_lo"], at("ffn_lo", 0))
                    for h in (2 * p, 2 * p + 1):
                        act.wait_ge(S["sb_z"], at("sb_z", h + 1))
                        if h >= 2:
                            act.wait_ge(S["sb_pv"], at("sb_pv", h - 1))
                        link(act.activation(sbuf3[h % 2][0], bank[4 + h % 2][:, 0:384], ACT.Abs))
                        link(act.activation(sbuf3[h % 2][0], sbuf3[h % 2][0], ACT.Exp, scale=-1.0))
                    for b in (sbuf3[0][0], sbuf3[1][0]):
                        act.activation(b, b, ACT.Ln, bias=1.0).then_inc(S["sb_ln"], 1)

                def sb_exp(h):
                    act.wait_ge(S["sb_arg"], at("sb_arg", h + 1))
                    act.activation(sbuf3[h % 2][0], sbuf3[h % 2][2], ACT.Exp).then_inc(S["sb_exp"], 1)

                def branch_hi(br, done, order):
                    act.wait_ge(S[done], at(done, PER[done]))
                    act.activation(y_hi[:, br, :, :], pair(bank[7][:, :]), ACT.Copy).then_inc(S["y_hi"], 1)

                def gl_ln():
                    act.wait_ge(S["gl_x"], at("gl_x", 1))
                    link(act.activation(la, lx, ACT.Abs))
                    link(act.activation(la, la, ACT.Exp, scale=-1.0))
                    act.activation(la, la, ACT.Ln, bias=1.0).then_inc(S["gl_ln"], 1)

                def decay(i):
                    act.wait_ge(S["gl_dif"], at("gl_dif", i))
                    link(act.activation(dec[i % 2], dec[i % 2], ACT.Abs))
                    act.activation(dec[i % 2], dec[i % 2], ACT.Exp, scale=-1.0 / GLA_TAU).then_inc(S["gl_dec"], 1)

                def gl_var():
                    act.wait_ge(S["gl_pv"], at("gl_pv", 1))
                    act.wait_ge(S["gl_silu"], at("gl_silu", 1))
                    link(act.activation(gl_raw, bank[6][:, :], ACT.Copy))
                    act.activation(tmp[:, :], gl_raw, ACT.Square).then_inc(S["gl_sq"], 1)

                def gl_root():
                    act.wait_ge(S["gl_v"], at("gl_v", 1))
                    act.activation(st[:, 26:34], st[:, 18:26], ACT.Sqrt).then_inc(S["gl_y"], 1)

                def ds_exp():
                    for n, t in enumerate((1, 0)):
                        act.wait_ge(S["ds_max"], at("ds_max", n + 1))
                        p = pair(dprob[t], 4)
                        for s in range(4):
                            c = 4 * n + s
                            ins = act.activation(p[:, s, :], p[:, s, :], ACT.Exp, bias=st[:, 42 + c:43 + c],
                                                 accum_out=st[:, 50 + c:51 + c])
                        ins.then_inc(S["ds_exp"], 1)

                def ds_tr():
                    for g in range(3):
                        act.wait_ge(S["ds_tr"], at("ds_tr", g + 1))
                        act.activation(dpt[g], bank[4 + g][:, :], ACT.Copy).then_inc(S["ds_pt"], 1)

                def merge(j):
                    act.wait_ge(S["merged"], at("merged", j + 1))
                    act.activation(h_hi[:, 2 * j:2 * j + 2, :], pair(acc), ACT.Copy).then_inc(S["merged_hi"], 1)

                def cross():
                    def exponent(i):
                        act.wait_ge(S["x_max"], at("x_max", i + 1))
                        for s in range(2):
                            c = 2 * i + s
                            ins = act.activation(pair(xprob[i])[:, s, :], bank[4 + i][:, s * SEQ:(s + 1) * SEQ], ACT.Exp,
                                                 bias=st[:, 42 + c:43 + c], scale=X_DIM ** -0.5, accum_out=st[:, 50 + c:51 + c])
                        ins.then_inc(S["x_exp"], 1)

                    def turned(i):
                        act.wait_ge(S["x_tr"], at("x_tr", i + 1))
                        act.activation(xpt[i], bank[4 + i][:, :], ACT.Copy).then_inc(S["x_pt"], 1)

                    def values_hi(h):
                        act.wait_ge(S["x_pv"], at("x_pv", h + 1))
                        act.activation(s_hi[:, 2 * h:2 * h + 2, :], pair(bank[4 + h][:, :]), ACT.Copy).then_inc(S["o_hi"], 1)

                    for i in range(3):
                        exponent(i)
                    turned(0)
                    turned(1)
                    exponent(3)
                    values_hi(0)
                    turned(2)
                    turned(3)
                    for h in range(1, HEADS):
                        values_hi(h)

                steps = {"index": index, "swapped": swapped, "mem_sq": mem_sq, "mem_root": mem_root,
                         "mem_split": mem_split, "gl_ln": gl_ln, "gl_var": gl_var, "gl_root": gl_root,
                         "ds_exp": ds_exp, "ds_tr": ds_tr,
                         "sb_out": lambda: branch_hi(0, "sb_pv", 1), "gl_out": lambda: branch_hi(2, "gl_otr", 2),
                         "ds_out": lambda: branch_hi(1, "ds_pv", 3)}
                for p in range(2):
                    steps[f"sb_ln{p}"] = lambda p=p: sb_ln(p)
                for h in range(HEADS):
                    steps[f"sb_exp{h}"] = lambda h=h: sb_exp(h)
                for i in range(1, 9):
                    steps[f"dec{i}"] = lambda i=i: decay(i)

                norm_rows(0)
                act.wait_ge(S["gain_t"], at("gain_t", 1))
                act.wait_ge(S["norm_lo"], at("norm_lo", 0))
                act.activation(gain[:, :], bank[0][:, 0:33], ACT.Copy).then_inc(S["gain"], 1)
                upper(0)
                act.wait_ge(S["gain"], at("gain", 1))
                norm_features(0)
                upper(1)
                for n in range(N_HEAD_SLABS):
                    if SLABS[n] != ("xo", 0):
                        upper(n + 2)
                    steps_first = SLABS[n - 1][0] == "gate" and SLABS[n - 1][1][0] == 2
                    if n and not steps_first:
                        evacuate(n - 1)
                    if SLABS[n - 1][0] == "y":
                        merge(SLABS[n - 1][1])
                    if SLABS[n - 1] == ("mix", 3):
                        norm_rows(1)
                    if SLABS[n] == ("xv", 3):
                        norm_features(1)
                    if SLABS[n] == ("xo", 0):
                        cross()
                        upper(n + 2)
                    for s in PLAN.get(n, ()):
                        if s in steps:
                            steps[s]()
                    if steps_first:
                        evacuate(n - 1)
                norm_rows(2)
                norm_features(2)

                def silu_of(p, i):
                    act.wait_ge(S["slab_used"], at("slab_used", N_HEAD_SLABS + ffn_index("up", p) + 1 + 6 * i))
                    act.wait_ge(S["ffn_mul"], at("ffn_mul", max(p - 1, 0) + 2 * i))
                    act.activation(silu[p % 2], bank[2 * (p % 2)][:, :], ACT.Silu).then_inc(S["ffn_silu"], 1)

                def act_hi(p, i):
                    act.wait_ge(S["ffn_mul"], at("ffn_mul", p + 1 + 2 * i))
                    act.wait_ge(S["slab_used"], at("slab_used", N_HEAD_SLABS + max(3 * p - 1, 0) + 6 * i))
                    o = 2 * (p % 2)
                    act.activation(s_hi[:, o:o + 2, :], pair(actf[p % 2]), ACT.Copy).then_inc(S["ffn_hi"], 1)

                def ffn(kind, j, i):
                    n = N_HEAD_SLABS + ffn_index(kind, j)
                    if kind == "gate" and j:
                        silu_of(j - 1, i)
                    if kind == "up" and j:
                        act_hi(j - 1, i)
                    if n + 2 < N_SLABS:
                        upper(n + 2, i)
                    if kind == "out" and j == N_PAIRS - 2:
                        silu_of(N_PAIRS - 1, 0)
                        act_hi(N_PAIRS - 1, 0)

                ffn_walk(act, ffn)
                assert links[0] == PER["act_chain"], links[0]

            act.activation(junk[:, 62:63], ones[:, 0:1], ACT.Sqrt)
            for t in range(TT):
                act.wait_ge(S["res"], DEPTH * PER["res"] + PRIMED["res"] - 2 + 2 * t)
                act.activation(xn[:, t, :], x[:, t, :], ACT.Square, accum_out=st[:, t:t + 1]).then_inc(once["f_sq"], 1)
            act.wait_ge(once["f_v"], 1)
            act.activation(st[:, 4:6], st[:, 2:4], ACT.Sqrt).then_inc(once["f_y"], 1)

        @block.vector
        def _(dve):
            def mean_and_eps(v, sq, count):
                return dve.tensor_scalar(v, sq, 1.0 / count, EPS, ALU.mult, ALU.add)

            def inverse_root(link, y, root, v, t):
                link(dve.reciprocal(y, root))
                link(dve.tensor_tensor(t, y, y, ALU.mult))
                link(dve.scalar_tensor_tensor(t, t, -0.5, v, ALU.mult, ALU.mult))
                link(dve.scalar_tensor_tensor(y, t, 1.5, y, ALU.add, ALU.mult))

            for name, count in PRIMED_BY_DVE.items():
                dve.sem_inc(S[name], count)
            outside = [0]

            def link_once(ins):
                outside[0] += 1
                ins.then_inc(once["f_chain"], 1)
                dve.wait_ge(once["f_chain"], outside[0])

            dve.wait_ge(once["consts"], 16)
            dve.wait_ge(once["x_in"], 16)

            with dve.Fori(0, DEPTH) as L:
                links, aparts = [0], [0]

                def at(name, n):
                    return L * PER[name] + n + PRIMED.get(name, 0)

                def link(ins):
                    links[0] += 1
                    ins.then_inc(S["dve_chain"], 1)
                    dve.wait_ge(S["dve_chain"], at("dve_chain", links[0]))

                def apart():
                    aparts[0] += 1
                    dve.memset(junk[:, aparts[0]:aparts[0] + 1], 0.0)

                def lower(n, i=0):
                    dve.wait_ge(S["slab_hi"], at("slab_hi", n + 1 + 6 * i))
                    dst, src, hi = w_lo[:, slot_of(n), :], raw[:, slot_of(n), :], w_hi[:, slot_of(n), :].bitcast(F32)
                    kind = SLABS[n][0] if n < N_HEAD_SLABS else ""
                    if kind == "keys":
                        dst, src, hi = (r.rearrange("p (k n) -> p k n", k=KT)[:, :, 0:K_END] for r in (dst, src, hi))
                    elif kind == "y":
                        dst, src, hi = dst[:, 0:6 * CW], src[:, 0:6 * CW], hi[:, 0:6 * CW]
                    dve.tensor_tensor(dst, src, hi, ALU.subtract).then_inc(S["slab_lo"], 1)

                def features_lo(lo, hi, g, done, first, signal):
                    for i in range(4):
                        dve.wait_ge(S[done], at(done, first + i + 1))
                        for k in range(2):
                            f = 2 * i + k
                            ins = dve.scalar_tensor_tensor(lo[:, f, :], bank[4 + i][:, k * SEQ:(k + 1) * SEQ],
                                                           gain[:, g + f:g + f + 1], hi[:, f, :].bitcast(F32),
                                                           ALU.mult, ALU.subtract)
                        ins.then_inc(S[signal], 1)

                def norm_rows(n):
                    dve.wait_ge(S["norm_sq"], at("norm_sq", 2 * n + 2))
                    dve.wait_ge(S["norm_xn"], at("norm_xn", 2 * n))
                    mean_and_eps(st[:, 2:4], st[:, 0:2], D_MODEL).then_inc(S["norm_v"], 1)
                    dve.wait_ge(S["norm_y"], at("norm_y", n + 1))
                    inverse_root(link, st[:, 6:8], st[:, 4:6], st[:, 2:4], st[:, 8:10])
                    for t in range(TT):
                        dve.tensor_scalar(xn[:, t, :], x[:, t, :], st[:, 6 + t:7 + t], None, ALU.mult).then_inc(S["norm_xn"], 1)

                def norm_features(n):
                    features_lo(h_lo, h_hi, 8 * n, "norm_hi", 4 * n, "norm_lo")

                def residual(n, banks, first):
                    for t in range(TT):
                        if t == 0:
                            dve.wait_ge(S["tile0_out"], at("tile0_out", first // 4 + 1))
                        else:
                            dve.wait_ge(S["slab_used"], at("slab_used", n))
                        for m in range(2):
                            r = x[:, t, m * 512:(m + 1) * 512]
                            dve.tensor_tensor(r, r, bank[banks[2 * t + m]][:, :], ALU.add).then_inc(S["res"], 1)
                    dve.wait_ge(S["res"], at("res", first + 4))

                def rope(i):
                    n = 1 if i == 1 else 2
                    src, t = (pair(ap[:, 0:n * SEQ], n) for ap in (proj[("ixq", "kk", "dsq")[i]], tmp))
                    dve.wait_ge(S["rot"], at("rot", i + 1))
                    dve.wait_ge(S["rope"], at("rope", i))
                    link(dve.tensor_tensor(t, pair(bank[(4, 7, 7)[i]][:, 0:n * SEQ], n), over(K["sin"], n), ALU.mult))
                    link(dve.tensor_tensor(src, src, over(K["cos"], n), ALU.mult))
                    dve.tensor_tensor(src, src, t, ALU.add).then_inc(S["rope"], 1)

                def index():
                    dve.wait_ge(S["evac"], at("evac", EVAC["misc"]))
                    for n, (t, half) in enumerate(((1, 0), (1, 1), (0, 0), (0, 1))):
                        dve.wait_ge(S["idx_relu"], at("idx_relu", n + 1))
                        nk = (t + 1) * P
                        for hh in range(2):
                            h = 2 * hh + half
                            before = K[f"adm{t}"] if half == 0 and hh == 0 else score[t]
                            ins = dve.scalar_tensor_tensor(score[t], relu[t][half][:, hh * nk:(hh + 1) * nk],
                                                           wi[:, t, h:h + 1], before, ALU.mult, ALU.add)
                            if (n, hh) != (3, 1):
                                link(ins)
                    ins.then_inc(S["scored"], 1)
                    dve.wait_ge(S["scored"], at("scored", 1))

                def topk(t, part):
                    for _ in range(TOPK // 16):
                        apart()
                        link(dve.max(m8[:, t, :], score[t]))
                        apart()
                        link(dve.match_replace(score[t], m8[:, t, :], score[t], TAKEN))
                    if part == 1:
                        link(dve.tensor_scalar(bias[t], score[t], TAKEN, NEG, ALU.not_equal, ALU.mult))

                def mem_sq():
                    dve.wait_ge(S["mem_sq"], at("mem_sq", 2))
                    mean_and_eps(st[:, 60:62], st[:, 58:60], D_MODEL).then_inc(S["mem_v"], 1)

                def mem_root():
                    dve.wait_ge(S["mem_y"], at("mem_y", 1))
                    inverse_root(link, st[:, 62:64], st[:, 62:64], st[:, 60:62], st[:, 58:60])
                    for t in range(TT):
                        dve.tensor_scalar(memx[:, t, :], memx[:, t, :], st[:, 62 + t:63 + t], None, ALU.mult).then_inc(S["mem_x"], 1)

                def mem_split():
                    features_lo(s_lo, s_hi, 24, "mem_hi", 0, "mem_lo")

                def diagonal(ap):
                    return ap.rearrange("p (a b) -> p a b", b=P)[:, 0:3:2, :]

                def sb_keep(h):
                    soft, keep, beta = sbuf3[h % 2]
                    z = bank[4 + h % 2][:, 0:384]
                    dve.wait_ge(S["sb_ln"], at("sb_ln", h + 1))
                    link(dve.scalar_tensor_tensor(beta, z, 0.0, soft, ALU.min, ALU.subtract))
                    link(dve.tensor_tensor(keep, beta, z, ALU.subtract))
                    dve.tensor_tensor(diagonal(keep), diagonal(keep), over(K["valid"], 2), ALU.mult).then_inc(S["sb_keep"], 1)

                def sb_arg(h):
                    beta = sbuf3[h % 2][2]
                    dve.wait_ge(S["sb_btw"], at("sb_btw", h + 1))
                    dve.tensor_tensor(beta, beta, bank[4 + h % 2][:, 0:384], ALU.add).then_inc(S["sb_arg"], 1)

                def sb_w(h):
                    w = diagonal(sbuf3[h % 2][0])
                    dve.wait_ge(S["sb_exp"], at("sb_exp", h + 1))
                    dve.tensor_tensor(w, w, over(K["valid"], 2), ALU.mult).then_inc(S["sb_w"], 1)

                def branch_lo(br, order):
                    dve.wait_ge(S["y_hi"], at("y_hi", order))
                    dve.tensor_tensor(y_lo[:, br, :, :], pair(bank[7][:, :]), y_hi[:, br, :, :].bitcast(F32),
                                      ALU.subtract).then_inc(S["y_lo"], 1)

                def gl_gate():
                    dve.wait_ge(S["rope"], at("rope", 3))
                    dve.wait_ge(S["gl_gate"], at("gl_gate", 1))
                    dve.tensor_scalar(lx, bank[6][:, 0:SEQ], gain[:, 32:33], None, ALU.add).then_inc(S["gl_x"], 1)

                def gl_cum():
                    dve.wait_ge(S["gl_ln"], at("gl_ln", 1))
                    link(dve.scalar_tensor_tensor(la, lx, 0.0, la, ALU.min, ALU.subtract))
                    dve.wait_ge(once["ones"], 2)
                    dve.tensor_tensor_scan(cum, ones[:, :], la, 0.0, ALU.mult, ALU.add).then_inc(S["gl_cum"], 1)

                def difference(i):
                    s = 1 << (i - 1)
                    if i >= 3:
                        dve.wait_ge(S["gl_qk"], at("gl_qk", i - 1))
                    if i == 1:
                        dve.wait_ge(S["scored"], at("scored", 1))
                    dve.wait_ge(S["gl_cum"], at("gl_cum", 1))
                    b = cum.rearrange("p (n w) -> p n w", w=2 * s)
                    dve.tensor_tensor(dec[i % 2].rearrange("p (n w) -> p n w", w=2 * s), b,
                                      b[:, :, s - 1:s].to_broadcast([P, SEQ // (2 * s), 2 * s]),
                                      ALU.subtract).then_inc(S["gl_dif"], 1)

                def level(i):
                    q, k = proj["glqk"][:, 0:SEQ], proj["glqk"][:, SEQ:2 * SEQ]
                    dve.wait_ge(S["zeroed"], at("zeroed", 1))
                    if i == 0:
                        dve.wait_ge(S["evac"], at("evac", EVAC["glqk"]))
                    if i >= 2:
                        dve.wait_ge(S["gl_lev"], at("gl_lev", LEVEL_COUNT[i - 1]))
                    if i:
                        dve.wait_ge(S["gl_dec"], at("gl_dec", i))
                        dve.tensor_tensor(ke[i % 2], k, dec[i % 2], ALU.mult)
                    for h in range(HEADS):
                        r = slice(32 * h, 32 * h + 32)
                        if i:
                            dst, src, decay = (right(ap.unsqueeze(1), i) for ap in (qe[i % 2][r, h, :], q[r, :], dec[i % 2][r, :]))
                            ins = dve.tensor_tensor(dst, src, decay, ALU.mult)
                        else:
                            ins = dve.tensor_copy(qe[0][r, h, :], q[r, :])
                    ins.then_inc(S["gl_qk"], 1)

                def apply(i):
                    for t in ((1,) if i == 8 else (0, 1)):
                        b = bank[LEVEL_BANKS[i][t]]
                        dve.wait_ge(S["gl_lev"], at("gl_lev", LEVEL_COUNT[i] + (t + 1 if i != 8 else 1)))
                        if i:
                            dve.wait_ge(S["gl_app"], at("gl_app", LEVEL_COUNT[i]))
                        if i == 8:
                            ins = dve.tensor_copy(attx, b[:, :])
                        elif i == 0:
                            ins = dve.tensor_tensor(pair(att[t], 4), pair(b[:, :], 4), over(K["ident"], 4), ALU.mult)
                        else:
                            apart()
                            mask = right(over(K[f"lev{i - 1}"].bitcast(I32), 4), i)
                            ins = dve.copy_predicated(right(pair(att[t], 4), i), mask, compact(b, i))
                        ins.then_inc(S["gl_app"], 1)

                def gl_silu():
                    g = proj["glo"]
                    dve.wait_ge(S["evac"], at("evac", EVAC["glo"]))
                    dve.wait_ge(S["gate_w"], at("gate_w", 32))
                    link(dve.tensor_scalar(tmp[:, :], tmp[:, :], 1.0, None, ALU.add))
                    link(dve.reciprocal(tmp[:, :], tmp[:, :]))
                    link(dve.tensor_tensor(g[:, :], g[:, :], tmp[:, :], ALU.mult))
                    dve.tensor_tensor(pair(g[:, :], 8), pair(g[:, :], 8), over(norm_g[:, :], 8), ALU.mult).then_inc(S["gl_silu"], 1)

                def gl_var():
                    dve.wait_ge(S["gl_sq"], at("gl_sq", 1))
                    link(dve.tensor_reduce(st[:, 10:18], pair(tmp[:, :], 8), AX_X, ALU.add))
                    mean_and_eps(st[:, 18:26], st[:, 10:18], HEAD_DIM).then_inc(S["gl_v"], 1)

                def gl_o():
                    dve.wait_ge(S["gl_y"], at("gl_y", 1))
                    dve.wait_ge(S["gl_silu"], at("gl_silu", 1))
                    inverse_root(link, st[:, 26:34], st[:, 26:34], st[:, 18:26], st[:, 34:42])
                    link(dve.tensor_tensor(pair(tmp[:, :], 8), pair(gl_raw, 8), spread(st[:, 26:34], HEAD_DIM), ALU.mult))
                    dve.tensor_tensor(tmp[:, :], tmp[:, :], proj["glo"][:, :], ALU.mult).then_inc(S["gl_o"], 1)

                def ds_max():
                    for n, (t, half) in enumerate(((1, 0), (1, 1), (0, 0), (0, 1))):
                        dve.wait_ge(S["ds_s"], at("ds_s", n + 1))
                        nk = (t + 1) * P
                        if n == 0:
                            dve.wait_ge(S["gl_pv"], at("gl_pv", 1))
                        dve.scalar_tensor_tensor(pair(dprob[t][:, half * 2 * nk:(half + 1) * 2 * nk]),
                                                 pair(bank[4 + 2 * t + half][:, 0:2 * nk]), HEAD_DIM ** -0.5,
                                                 over(bias[t], 2), ALU.mult, ALU.add).then_inc(S["ds_p"], 1)
                    for n, t in enumerate((1, 0)):
                        dve.wait_ge(S["ds_p"], at("ds_p", 2 * n + 2))
                        dve.tensor_reduce(st[:, 42 + 4 * n:46 + 4 * n], pair(dprob[t], 4), AX_X, ALU.max,
                                          negate=True).then_inc(S["ds_max"], 1)

                def ds_norm():
                    for n, t in enumerate((1, 0)):
                        sums = st[:, 50 + 4 * n:54 + 4 * n]
                        dve.wait_ge(S["ds_exp"], at("ds_exp", n + 1))
                        link(dve.reciprocal(sums, sums))
                        dve.tensor_tensor(pair(dprob[t], 4), pair(dprob[t], 4), spread(sums, (t + 1) * P), ALU.mult).then_inc(S["ds_norm"], 1)

                def merge(n):
                    j = SLABS[n][1]
                    dve.wait_ge(S["slab_used"], at("slab_used", n + 1))
                    dve.wait_ge(S["evac"], at("evac", EVAC[("gate", (j, 2))]))
                    if j:
                        dve.wait_ge(S["merged_lo"], at("merged_lo", j))
                    for br in range(3):
                        dst = part if br else acc
                        dve.tensor_tensor(dst, sig[j][br], bank[BANKS[n][br]][:, :], ALU.mult).then_inc(S["merged_mul"], 1)
                        dve.wait_ge(S["merged_mul"], at("merged_mul", 3 * j + br + 1))
                        if br == 1:
                            link(dve.tensor_tensor(acc, acc, part, ALU.add))
                        if br == 2:
                            dve.tensor_tensor(acc, acc, part, ALU.add).then_inc(S["merged"], 1)

                def merge_lo(n):
                    j = SLABS[n][1]
                    dve.wait_ge(S["merged_hi"], at("merged_hi", j + 1))
                    dve.tensor_tensor(h_lo[:, 2 * j:2 * j + 2, :], pair(acc), h_hi[:, 2 * j:2 * j + 2, :].bitcast(F32),
                                      ALU.subtract).then_inc(S["merged_lo"], 1)

                def cross():
                    def maximum(i):
                        m = st[:, 42 + 2 * i:44 + 2 * i]
                        dve.wait_ge(S["xs"], at("xs", i + 1))
                        link(dve.tensor_reduce(m, pair(bank[4 + i][:, :]), AX_X, ALU.max, negate=True))
                        dve.tensor_scalar(m, m, X_DIM ** -0.5, None, ALU.mult).then_inc(S["x_max"], 1)

                    def normalise(i):
                        sums = st[:, 50 + 2 * i:52 + 2 * i]
                        dve.wait_ge(S["x_exp"], at("x_exp", i + 1))
                        link(dve.reciprocal(sums, sums))
                        dve.tensor_tensor(pair(xprob[i]), pair(xprob[i]), spread(sums, SEQ), ALU.mult).then_inc(S["x_norm"], 1)

                    maximum(0)
                    for i in range(1, 4):
                        maximum(i)
                        normalise(i - 1)
                    normalise(3)
                    for h in range(HEADS):
                        dve.wait_ge(S["o_hi"], at("o_hi", h + 1))
                        dve.tensor_tensor(s_lo[:, 2 * h:2 * h + 2, :], pair(bank[4 + h][:, :]),
                                          s_hi[:, 2 * h:2 * h + 2, :].bitcast(F32), ALU.subtract).then_inc(S["o_lo"], 1)

                steps = {"index": index, "mem_sq": mem_sq,
                         "mem_root": mem_root, "mem_split": mem_split,
                         "gl_x": gl_gate, "gl_cum": gl_cum, "gl_silu": gl_silu, "gl_var": gl_var, "gl_o": gl_o,
                         "ds_max": ds_max, "ds_norm": ds_norm,
                         "sb_out": lambda: branch_lo(0, 1), "gl_out": lambda: branch_lo(2, 2), "ds_out": lambda: branch_lo(1, 3)}
                for t in range(TT):
                    steps[f"topk{t}a"] = lambda t=t: topk(t, 0)
                    steps[f"topk{t}b"] = lambda t=t: topk(t, 1)
                for i in range(3):
                    steps[f"rope{i}"] = lambda i=i: rope(i)
                for h in range(HEADS):
                    for name, f in (("sb_keep", sb_keep), ("sb_arg", sb_arg), ("sb_w", sb_w)):
                        steps[f"{name}{h}"] = lambda h=h, f=f: f(h)
                for i in range(9):
                    steps[f"dif{i}"] = lambda i=i: difference(i)
                    steps[f"form{i}"] = lambda i=i: level(i)
                    steps[f"app{i}"] = lambda i=i: apply(i)

                norm_rows(0)
                lower(0)
                norm_features(0)
                lower(1)
                for n in range(N_HEAD_SLABS):
                    if SLABS[n - 1][0] == "y":
                        merge(n - 1)
                    if SLABS[n - 1] == ("mix", 3):
                        residual(n, BANKS[n - 1], 0)
                        norm_rows(1)
                    if SLABS[n] == ("xv", 3):
                        norm_features(1)
                    if SLABS[n] == ("xo", 0):
                        cross()
                    if SLABS[n - 1][0] == "y":
                        merge_lo(n - 1)
                    steps["lower"] = lambda n=n: lower(n + 2)
                    if "lower" not in PLAN.get(n, ()):
                        lower(n + 2)
                    for s in PLAN.get(n, ()):
                        if s in steps:
                            steps[s]()
                residual(N_HEAD_SLABS, BANKS[N_HEAD_SLABS - 1], 4)
                norm_rows(2)
                norm_features(2)

                def multiply(p, i):
                    dve.wait_ge(S["ffn_silu"], at("ffn_silu", p + 1 + 2 * i))
                    dve.tensor_tensor(actf[p % 2], silu[p % 2], bank[1 + 2 * (p % 2)][:, :], ALU.mult).then_inc(S["ffn_mul"], 1)

                def act_lo(p, i):
                    dve.wait_ge(S["ffn_hi"], at("ffn_hi", p + 1 + 2 * i))
                    o = 2 * (p % 2)
                    dve.tensor_tensor(s_lo[:, o:o + 2, :], pair(actf[p % 2]), s_hi[:, o:o + 2, :].bitcast(F32),
                                      ALU.subtract).then_inc(S["ffn_lo"], 1)

                def ffn(kind, j, i):
                    n = N_HEAD_SLABS + ffn_index(kind, j)
                    if kind == "gate" and j:
                        multiply(j - 1, i)
                    if kind == "up" and j:
                        act_lo(j - 1, i)
                    if n + 2 < N_SLABS:
                        lower(n + 2, i)
                    if kind == "out" and j == N_PAIRS - 2:
                        multiply(N_PAIRS - 1, 0)
                        act_lo(N_PAIRS - 1, 0)

                ffn_walk(dve, ffn)
                residual(N_SLABS, (4, 5, 6, 7), 8)
                assert links[0] == PER["dve_chain"], links[0]

            dve.wait_ge(once["f_sq"], 2)
            mean_and_eps(st[:, 2:4], st[:, 0:2], D_MODEL).then_inc(once["f_v"], 1)
            dve.wait_ge(once["f_y"], 1)
            inverse_root(link_once, st[:, 6:8], st[:, 4:6], st[:, 2:4], st[:, 8:10])
            dve.wait_ge(once["f_g"], 16)
            for t in range(TT):
                dve.scalar_tensor_tensor(xn[:, t, :], x[:, t, :], st[:, 6 + t:7 + t],
                                         xk[:, 0:4, :].rearrange("p a b -> p (a b)"), ALU.mult, ALU.mult).then_inc(once["f_out"], 1)


_INS = ("x", "mem", "mix_norm_g", "w_in", "gla_w_up", "gla_b", "gla_norm_g", "w_br_a", "w_br_b", "w_br_c",
        "w_mix_out", "xattn_norm_g", "mem_norm_g", "w_xq", "w_xkv", "w_xo", "ffn_norm_g", "w_ffn_in",
        "w_ffn_out", "final_norm_g")


def kernel(**inputs):
    import concourse.bacc as bacc
    from concourse.bass_utils import run_bass_kernel_spmd

    nc = bacc.Bacc("TRN2", target_bir_lowering=False, num_devices=1)
    arrays, args = {}, {}
    for name in _INS:
        v = np.ascontiguousarray(inputs[name])
        arrays[f"in_{name}"] = v
        args[name] = nc.dram_tensor(f"in_{name}", v.shape, mybir.dt.from_np(v.dtype), kind="ExternalInput").ap()
    arrays["shape_constants"] = CONST_ARRAY
    args["shape_constants"] = nc.dram_tensor("shape_constants", CONST_ARRAY.shape, F32, kind="ExternalInput").ap()
    out = nc.dram_tensor("out", (1, SEQ, D_MODEL), F32, kind="ExternalOutput").ap()
    program(nc, args, out)
    return run_bass_kernel_spmd(nc, [arrays], core_ids=[0]).results[0]["out"]
```
